# Optimizing a Trainium2 kernel written in Bass

```python
import jax, jax.numpy as jnp
from jax import lax
import numpy as np

D_MODEL = 1024
BATCH = 1
SEQ = 512
DEPTH = 2

D_MIX = D_MODEL
D_SGU = D_MIX // 2
SGU_GROUPS = 4
SGU_GROUP_DIM = D_SGU // SGU_GROUPS
CHUNK = 128
D_ATTN = D_MIX - D_SGU
N_HEADS = 4
HEAD_DIM = D_ATTN // N_HEADS // 2
V_HEAD_DIM = 2 * HEAD_DIM
ROT_DIM = HEAD_DIM // 4
ROPE_THETA = 500000.0
Q_BLOCK = 128
D_FF = 2816
CONV_WIDTH = 3
EPS = 1e-6
D_IN = 2 * D_SGU + 3 * D_ATTN


def rmsnorm(x, g):
    xf = x.astype(jnp.float32)
    y = xf * lax.rsqrt(jnp.mean(xf * xf, axis=-1, keepdims=True) + EPS)
    return (y * g.astype(jnp.float32)).astype(x.dtype)

def apply_partial_rope(t, cos, sin):
    half = ROT_DIM // 2
    t1 = t[..., :half]
    t2 = t[..., half:ROT_DIM]
    rot = jnp.concatenate([t1 * cos - t2 * sin, t2 * cos + t1 * sin], axis=-1)
    return jnp.concatenate([rot.astype(t.dtype), t[..., ROT_DIM:]], axis=-1)

def sgu_mixer(u, v, v_gain, w_s, b_s):
    B, S, _ = u.shape
    n_chunks = S // CHUNK
    vg = rmsnorm(v.reshape(B, S, SGU_GROUPS, SGU_GROUP_DIM), v_gain.reshape(SGU_GROUPS, SGU_GROUP_DIM))
    vg = vg.reshape(B, n_chunks, CHUNK, SGU_GROUPS, SGU_GROUP_DIM)
    causal = jnp.tril(jnp.ones((CHUNK, CHUNK), dtype=bool))
    w = jnp.where(causal[None], w_s, jnp.zeros_like(w_s))
    mixed = jnp.einsum('gpq,bcqgd->bcpgd', w, vg) + b_s.T[None, None, :, :, None]
    return u * mixed.reshape(B, S, D_SGU)

def diff_attention(q, k, v, positions, lq1, lk1, lq2, lk2, subln_g, layer_idx):
    B, S, _ = q.shape
    q = q.reshape(B, S, N_HEADS, 2, HEAD_DIM)
    k = k.reshape(B, S, N_HEADS, 2, HEAD_DIM)
    v = v.reshape(B, S, N_HEADS, V_HEAD_DIM)
    inv_freq = ROPE_THETA ** (-jnp.arange(0, ROT_DIM, 2, dtype=jnp.float32) / ROT_DIM)
    ang = positions.astype(jnp.float32)[..., None] * inv_freq
    cos = jnp.cos(ang)[:, :, None, None, :]
    sin = jnp.sin(ang)[:, :, None, None, :]
    q = apply_partial_rope(q, cos, sin)
    k = apply_partial_rope(k, cos, sin)

    lambda_init = 0.8 - 0.6 * float(np.exp(-0.3 * layer_idx))
    lam = (jnp.exp(jnp.sum(lq1.astype(jnp.float32) * lk1.astype(jnp.float32)))
           - jnp.exp(jnp.sum(lq2.astype(jnp.float32) * lk2.astype(jnp.float32)))
           + lambda_init)
    scale = HEAD_DIM ** -0.5

    outs = []
    for start in range(0, S, Q_BLOCK):
        end = start + Q_BLOCK
        qb = q[:, start:end]
        kb = k[:, :end]
        scores = jnp.einsum('bqhmd,bkhmd->bhmqk', qb, kb).astype(jnp.float32) * scale
        q_idx = start + jnp.arange(Q_BLOCK)
        k_idx = jnp.arange(end)
        mask = k_idx[None, :] <= q_idx[:, None]
        scores = jnp.where(mask, scores, -jnp.inf)
        p = jax.nn.softmax(scores, axis=-1)
        attn = p[:, :, 0] - lam * p[:, :, 1]
        outs.append(jnp.einsum('bhqk,bkhd->bqhd', attn.astype(v.dtype), v[:, :end]))
    o = jnp.concatenate(outs, axis=1)
    o = rmsnorm(o, subln_g) * (1.0 - lambda_init)
    return o.reshape(B, S, D_ATTN)

def conv_ffn(h, w_up, conv_w, conv_b, w_down):
    S = h.shape[1]
    up = h @ w_up
    up_p = jnp.pad(up, ((0, 0), (CONV_WIDTH - 1, 0), (0, 0)))
    conv = conv_b
    for j in range(CONV_WIDTH):
        conv = conv + up_p[:, j:j + S] * conv_w[j]
    gate, val = jnp.split(conv, 2, axis=-1)
    return (jax.nn.silu(gate) * val) @ w_down

def first_inputs(seed: int = 0) -> dict:
    key = jax.random.key(seed)
    ks = jax.random.split(key, 20)
    f32 = jnp.float32
    x = jax.random.normal(ks[0], (BATCH, SEQ, D_MODEL), f32)
    positions = jnp.tile(jnp.arange(SEQ, dtype=jnp.int32)[None, :], (BATCH, 1))
    attn_norm = 1.0 + 0.02 * jax.random.normal(ks[1], (DEPTH, D_MODEL), f32)
    w_in = jax.random.normal(ks[2], (DEPTH, D_MODEL, D_IN), f32) * D_MODEL ** -0.5
    sgu_v_norm = 1.0 + 0.02 * jax.random.normal(ks[3], (DEPTH, D_SGU), f32)
    sgu_w_spatial = jax.random.normal(ks[4], (DEPTH, SGU_GROUPS, CHUNK, CHUNK), f32) * CHUNK ** -0.5
    sgu_b_spatial = 1.0 + 0.02 * jax.random.normal(ks[5], (DEPTH, SGU_GROUPS, CHUNK), f32)
    lambda_q1 = 0.1 * jax.random.normal(ks[6], (DEPTH, HEAD_DIM), f32)
    lambda_k1 = 0.1 * jax.random.normal(ks[7], (DEPTH, HEAD_DIM), f32)
    lambda_q2 = 0.1 * jax.random.normal(ks[8], (DEPTH, HEAD_DIM), f32)
    lambda_k2 = 0.1 * jax.random.normal(ks[9], (DEPTH, HEAD_DIM), f32)
    subln_gain = 1.0 + 0.02 * jax.random.normal(ks[10], (DEPTH, V_HEAD_DIM), f32)
    w_out = jax.random.normal(ks[11], (DEPTH, D_MIX, D_MODEL), f32) * D_MIX ** -0.5
    ffn_norm = 1.0 + 0.02 * jax.random.normal(ks[12], (DEPTH, D_MODEL), f32)
    w_up = jax.random.normal(ks[13], (DEPTH, D_MODEL, 2 * D_FF), f32) * D_MODEL ** -0.5
    conv_w = jax.random.normal(ks[14], (DEPTH, CONV_WIDTH, 2 * D_FF), f32) * CONV_WIDTH ** -0.5
    conv_b = 0.02 * jax.random.normal(ks[15], (DEPTH, 2 * D_FF), f32)
    w_down = jax.random.normal(ks[16], (DEPTH, D_FF, D_MODEL), f32) * D_FF ** -0.5
    final_norm = 1.0 + 0.02 * jax.random.normal(ks[17], (D_MODEL,), f32)
    return {"x": x, "positions": positions, "attn_norm": attn_norm, "w_in": w_in,
            "sgu_v_norm": sgu_v_norm, "sgu_w_spatial": sgu_w_spatial, "sgu_b_spatial": sgu_b_spatial,
            "lambda_q1": lambda_q1, "lambda_k1": lambda_k1, "lambda_q2": lambda_q2, "lambda_k2": lambda_k2,
            "subln_gain": subln_gain, "w_out": w_out, "ffn_norm": ffn_norm, "w_up": w_up,
            "conv_w": conv_w, "conv_b": conv_b, "w_down": w_down, "final_norm": final_norm}

def first_block(x, positions, attn_norm, w_in, sgu_v_norm, sgu_w_spatial, sgu_b_spatial,
              lambda_q1, lambda_k1, lambda_q2, lambda_k2, subln_gain, w_out, ffn_norm,
              w_up, conv_w, conv_b, w_down, final_norm):
    h = x
    for l in range(DEPTH):
        n = rmsnorm(h, attn_norm[l])
        proj = n @ w_in[l]
        u, v_sgu, q, k, v_att = jnp.split(
            proj, [D_SGU, 2 * D_SGU, 2 * D_SGU + D_ATTN, 2 * D_SGU + 2 * D_ATTN], axis=-1)
        u = jax.nn.gelu(u)
        v_sgu = jax.nn.gelu(v_sgu)
        y_sgu = sgu_mixer(u, v_sgu, sgu_v_norm[l], sgu_w_spatial[l], sgu_b_spatial[l])
        y_att = diff_attention(q, k, v_att, positions, lambda_q1[l], lambda_k1[l],
                               lambda_q2[l], lambda_k2[l], subln_gain[l], l)
        mixed = jnp.concatenate([y_sgu, y_att], axis=-1)
        h = h + mixed @ w_out[l]
        h = h + conv_ffn(rmsnorm(h, ffn_norm[l]), w_up[l], conv_w[l], conv_b[l], w_down[l])
    return rmsnorm(h, final_norm)


_first_inputs = first_inputs


def first_inputs(seed=0):
    import zlib

    import numpy as np

    out = dict(_first_inputs(seed))
    spreads = {}
    factors = {'sgu_v_norm': 8.0,
     'sgu_b_spatial': 5.202,
     'lambda_q2': 4.067,
     'subln_gain': 4.3,
     'ffn_norm': 3.44,
     'conv_b': 3.186,
     'final_norm': 2.863}
    for name, (base, spread) in spreads.items():
        noise = np.random.default_rng([zlib.crc32(name.encode()), seed]).standard_normal(out[name].shape)
        drawn = base * np.exp(spread * noise) if base else spread * noise
        out[name] = __import__('jax').numpy.asarray(drawn.astype(out[name].dtype))
    for name, factor in factors.items():
        out[name] = (out[name] * factor).astype(out[name].dtype)
    return out


_narrow_inputs = first_inputs


def first_inputs(seed=0):

    out = dict(_narrow_inputs(seed))
    wider = {'sgu_v_norm': 3.57, 'sgu_b_spatial': 3.2, 'subln_gain': 3.07, 'final_norm': 3.23}
    for name, times in wider.items():
        mean = out[name].mean()
        out[name] = (mean + times * (out[name] - mean)).astype(out[name].dtype)
    return out


DEPTH_2 = 1

D_RNN = D_MODEL // 2
RNN_BLOCKS = 8
RNN_BLOCK = D_RNN // RNN_BLOCKS
CONV_WIDTH_2 = 4
LRU_C = 8.0
N_HEADS_2 = 8
HEAD_DIM_2 = 64
N_KV = 2
REP = N_HEADS_2 // N_KV
D_ATT = N_HEADS_2 * HEAD_DIM_2
CMP_LEN = 32
CMP_STRIDE = 16
CMP_HIDDEN = 256
SLC_BLOCK = 64
SLC_TOPK = 16
WINDOW = 512
Q_BLOCK_2 = 64
D_FF_2 = 4 * D_MODEL
NEG = -1e30
FORCED = 1e4


def rms_norm(x, g):
    xf = x.astype(jnp.float32)
    y = xf * lax.rsqrt(jnp.mean(xf * xf, axis=-1, keepdims=True) + EPS)
    return (y * g.astype(jnp.float32)).astype(x.dtype)

def modulate(h, shift, scale):
    return h * (1.0 + scale[:, None, :]) + shift[:, None, :]

def alibi_slopes():
    return jnp.asarray(2.0 ** (-8.0 * np.arange(1, N_HEADS_2 + 1) / N_HEADS_2), jnp.float32)

def causal_depthwise_conv(x, w, b):
    y = lax.conv_general_dilated(x, w[:, None, :], window_strides=(1,), padding=[(CONV_WIDTH_2 - 1, 0)],
                                 dimension_numbers=('NWC', 'WIO', 'NWC'), feature_group_count=x.shape[-1])
    return y + b

def block_diag(x, w, b):
    xb = x.reshape(x.shape[:-1] + (RNN_BLOCKS, RNN_BLOCK))
    return jnp.einsum('bsni,nij->bsnj', xb, w.astype(jnp.float32)).reshape(x.shape) + b.astype(jnp.float32)

def rg_lru(x, w_a, b_a, w_x, b_x, lam):
    xf = x.astype(jnp.float32)
    r = jax.nn.sigmoid(block_diag(xf, w_a, b_a))
    i = jax.nn.sigmoid(block_diag(xf, w_x, b_x))
    log_a = -LRU_C * r * jax.nn.softplus(-lam.astype(jnp.float32))
    a = jnp.exp(log_a)
    u = jnp.sqrt(-jnp.expm1(2.0 * log_a)) * (i * xf)

    def combine(e1, e2):
        a1, b1 = e1
        a2, b2 = e2
        return a1 * a2, a2 * b1 + b2

    _, h = lax.associative_scan(combine, (a, u), axis=1)
    return h.astype(x.dtype)

def to_heads(t):
    B, S, _ = t.shape
    return t.reshape(B, S, N_KV, HEAD_DIM_2).transpose(0, 2, 1, 3)

def compress_blocks(k, pos_emb, w1, w2):
    B, G, S, D = k.shape
    n_cmp = (S - CMP_LEN) // CMP_STRIDE + 1
    idx = CMP_STRIDE * jnp.arange(n_cmp)[:, None] + jnp.arange(CMP_LEN)[None, :]
    blocks = (k[:, :, idx] + pos_emb).reshape(B, G, n_cmp, CMP_LEN * D)
    return jax.nn.gelu(blocks @ w1) @ w2

def nsa_attention(q, k_c, v_c, k_s, v_s, k_w, v_w, gate_logits,
                  cmp_pos_k, cmp_w1_k, cmp_w2_k, cmp_pos_v, cmp_w1_v, cmp_w2_v):
    B, S, _ = q.shape
    f32 = jnp.float32
    n_cmp = (S - CMP_LEN) // CMP_STRIDE + 1
    n_slc = S // SLC_BLOCK
    n_sel = min(SLC_TOPK, n_slc)
    n_qb = S // Q_BLOCK_2
    qh = q.reshape(B, S, N_KV, REP, HEAD_DIM_2).transpose(0, 2, 3, 1, 4) * (HEAD_DIM_2 ** -0.5)
    kc = compress_blocks(to_heads(k_c), cmp_pos_k, cmp_w1_k, cmp_w2_k)
    vc = compress_blocks(to_heads(v_c), cmp_pos_v, cmp_w1_v, cmp_w2_v).astype(f32)
    ks = to_heads(k_s).reshape(B, N_KV, n_slc, SLC_BLOCK, HEAD_DIM_2)
    vs = to_heads(v_s).reshape(B, N_KV, n_slc, SLC_BLOCK, HEAD_DIM_2)
    pad = ((0, 0), (0, 0), (WINDOW, 0), (0, 0))
    kw = jnp.pad(to_heads(k_w), pad)
    vw = jnp.pad(to_heads(v_w), pad)
    gates = jax.nn.sigmoid(gate_logits.astype(f32)).reshape(B, S, 3, N_KV, REP).transpose(2, 0, 3, 4, 1)
    slopes = alibi_slopes().reshape(1, N_KV, REP, 1, 1)
    c_start = CMP_STRIDE * jnp.arange(n_cmp)
    cmp_end = c_start + (CMP_LEN - 1)
    s_start = SLC_BLOCK * jnp.arange(n_slc)
    overlap = ((c_start[:, None] < s_start[None, :] + SLC_BLOCK) &
               (c_start[:, None] + CMP_LEN > s_start[None, :])).astype(f32)
    blk_ids = jnp.arange(n_slc)
    gather = jax.vmap(jax.vmap(lambda kb, ix: kb[ix]))

    def one_block(i):
        q0 = i * Q_BLOCK_2
        qb = lax.dynamic_slice_in_dim(qh, q0, Q_BLOCK_2, axis=3)
        t = q0 + jnp.arange(Q_BLOCK_2)
        d_c = (t[:, None] - cmp_end[None, :]).astype(f32)
        sc = jnp.einsum('bgrqd,bgcd->bgrqc', qb, kc).astype(f32) - slopes * d_c
        sc = jnp.where(d_c >= 0, sc, NEG)
        p_c = jax.nn.softmax(sc, axis=-1) * (t >= CMP_LEN - 1).astype(f32)[:, None]
        o_c = jnp.einsum('bgrqc,bgcd->bgrqd', p_c, vc)
        imp = jnp.einsum('bgrqc,cj->bgqj', p_c, overlap)
        cur = t // SLC_BLOCK
        forced = (blk_ids[None, :] == 0) | (blk_ids[None, :] == cur[:, None]) | (blk_ids[None, :] == cur[:, None] - 1)
        visible = s_start[None, :] <= t[:, None]
        imp = jnp.where(forced, FORCED, jnp.where(visible, imp, NEG))
        _, sel = lax.top_k(imp, n_sel)
        k_sel = gather(ks, sel)
        v_sel = gather(vs, sel).astype(f32)
        pos = sel[..., None] * SLC_BLOCK + jnp.arange(SLC_BLOCK)
        d_s = (t[:, None, None] - pos).astype(f32)[:, :, None]
        ss = jnp.einsum('bgrqd,bgqnkd->bgrqnk', qb, k_sel).astype(f32) - slopes[..., None] * d_s
        ss = jnp.where(d_s >= 0, ss, NEG)
        p_s = jax.nn.softmax(ss.reshape(ss.shape[:4] + (-1,)), axis=-1).reshape(ss.shape)
        o_s = jnp.einsum('bgrqnk,bgqnkd->bgrqd', p_s, v_sel)
        kwb = lax.dynamic_slice_in_dim(kw, q0, WINDOW + Q_BLOCK_2, axis=2)
        vwb = lax.dynamic_slice_in_dim(vw, q0, WINDOW + Q_BLOCK_2, axis=2).astype(f32)
        s_pos = q0 - WINDOW + jnp.arange(WINDOW + Q_BLOCK_2)
        d_w = (t[:, None] - s_pos[None, :]).astype(f32)
        ok = (d_w >= 0) & (d_w < WINDOW) & (s_pos[None, :] >= 0)
        sw = jnp.einsum('bgrqd,bgkd->bgrqk', qb, kwb).astype(f32) - slopes * d_w
        sw = jnp.where(ok, sw, NEG)
        o_w = jnp.einsum('bgrqk,bgkd->bgrqd', jax.nn.softmax(sw, axis=-1), vwb)
        gb = lax.dynamic_slice_in_dim(gates, q0, Q_BLOCK_2, axis=4)[..., None]
        return gb[0] * o_c + gb[1] * o_s + gb[2] * o_w

    out = lax.map(one_block, jnp.arange(n_qb))
    return out.transpose(1, 0, 4, 2, 3, 5).reshape(B, S, D_ATT).astype(q.dtype)

def hybrid_mixer(h, w_in, conv_w, conv_b, lru_wa, lru_ba, lru_wx, lru_bx, lru_lambda,
                 cmp_pos_k, cmp_w1_k, cmp_w2_k, cmp_pos_v, cmp_w1_v, cmp_w2_v,
                 norm_rnn_out, norm_att_out, w_out):
    sizes = [D_RNN, D_RNN, D_ATT] + [N_KV * HEAD_DIM_2] * 6 + [3 * N_HEADS_2]
    splits = np.cumsum(sizes)[:-1].tolist()
    z = h @ w_in
    g_rnn, x_rnn, q, k_c, v_c, k_s, v_s, k_w, v_w, gate_logits = jnp.split(z, splits, axis=-1)
    rnn = jax.nn.gelu(g_rnn) * rg_lru(causal_depthwise_conv(x_rnn, conv_w, conv_b),
                                      lru_wa, lru_ba, lru_wx, lru_bx, lru_lambda)
    att = nsa_attention(q, k_c, v_c, k_s, v_s, k_w, v_w, gate_logits,
                        cmp_pos_k, cmp_w1_k, cmp_w2_k, cmp_pos_v, cmp_w1_v, cmp_w2_v)
    y = jnp.concatenate([rms_norm(rnn, norm_rnn_out), rms_norm(att, norm_att_out)], axis=-1)
    return y @ w_out

def second_inputs(seed: int = 0) -> dict:
    key = jax.random.key(seed)
    ks = jax.random.split(key, 32)
    L = DEPTH_2
    f32 = jnp.float32

    def nrm(k, shape, scale):
        return jax.random.normal(k, shape, f32) * scale

    def gain(k, n):
        return 1.0 + 0.05 * jax.random.normal(k, (L, n), f32)

    d_in = 2 * D_RNN + D_ATT + 6 * N_KV * HEAD_DIM_2 + 3 * N_HEADS_2
    u = jax.random.uniform(ks[31], (L, D_RNN), f32, minval=0.9, maxval=0.999)
    a0 = u ** (1.0 / LRU_C)
    lam = jnp.log(a0) - jnp.log1p(-a0)
    return {
        'x': nrm(ks[0], (BATCH, SEQ, D_MODEL), 1.0),
        'c': nrm(ks[1], (BATCH, D_MODEL), 1.0),
        'ada_w': nrm(ks[2], (L, D_MODEL, 6 * D_MODEL), 0.1 * D_MODEL ** -0.5),
        'ada_b': nrm(ks[3], (L, 6 * D_MODEL), 0.01),
        'pre_norm_mix': gain(ks[4], D_MODEL),
        'w_in': nrm(ks[5], (L, D_MODEL, d_in), D_MODEL ** -0.5),
        'conv_w': nrm(ks[6], (L, CONV_WIDTH_2, D_RNN), CONV_WIDTH_2 ** -0.5),
        'conv_b': nrm(ks[7], (L, D_RNN), 0.01),
        'lru_wa': nrm(ks[8], (L, RNN_BLOCKS, RNN_BLOCK, RNN_BLOCK), RNN_BLOCK ** -0.5),
        'lru_ba': nrm(ks[9], (L, D_RNN), 0.01),
        'lru_wx': nrm(ks[10], (L, RNN_BLOCKS, RNN_BLOCK, RNN_BLOCK), RNN_BLOCK ** -0.5),
        'lru_bx': nrm(ks[11], (L, D_RNN), 0.01),
        'lru_lambda': lam,
        'cmp_pos_k': nrm(ks[12], (L, CMP_LEN, HEAD_DIM_2), 0.1),
        'cmp_w1_k': nrm(ks[13], (L, CMP_LEN * HEAD_DIM_2, CMP_HIDDEN), (CMP_LEN * HEAD_DIM_2) ** -0.5),
        'cmp_w2_k': nrm(ks[14], (L, CMP_HIDDEN, HEAD_DIM_2), CMP_HIDDEN ** -0.5),
        'cmp_pos_v': nrm(ks[15], (L, CMP_LEN, HEAD_DIM_2), 0.1),
        'cmp_w1_v': nrm(ks[16], (L, CMP_LEN * HEAD_DIM_2, CMP_HIDDEN), (CMP_LEN * HEAD_DIM_2) ** -0.5),
        'cmp_w2_v': nrm(ks[17], (L, CMP_HIDDEN, HEAD_DIM_2), CMP_HIDDEN ** -0.5),
        'norm_rnn_out': gain(ks[18], D_RNN),
        'norm_att_out': gain(ks[19], D_ATT),
        'w_out': nrm(ks[20], (L, D_RNN + D_ATT, D_MODEL), (D_RNN + D_ATT) ** -0.5),
        'post_norm_mix': gain(ks[21], D_MODEL),
        'pre_norm_mlp': gain(ks[22], D_MODEL),
        'w_ff1': nrm(ks[23], (L, D_MODEL, D_FF_2), D_MODEL ** -0.5),
        'w_ff2': nrm(ks[24], (L, D_FF_2, D_MODEL), D_FF_2 ** -0.5),
        'post_norm_mlp': gain(ks[25], D_MODEL),
    }

def second_block(x, c, ada_w, ada_b, pre_norm_mix, w_in, conv_w, conv_b, lru_wa, lru_ba, lru_wx, lru_bx,
              lru_lambda, cmp_pos_k, cmp_w1_k, cmp_w2_k, cmp_pos_v, cmp_w1_v, cmp_w2_v,
              norm_rnn_out, norm_att_out, w_out, post_norm_mix, pre_norm_mlp, w_ff1, w_ff2, post_norm_mlp):
    for l in range(DEPTH_2):
        mod = jax.nn.silu(c) @ ada_w[l] + ada_b[l]
        sh1, sc1, g1, sh2, sc2, g2 = jnp.split(mod, 6, axis=-1)
        h = modulate(rms_norm(x, pre_norm_mix[l]), sh1, sc1)
        y = hybrid_mixer(h, w_in[l], conv_w[l], conv_b[l], lru_wa[l], lru_ba[l], lru_wx[l], lru_bx[l],
                         lru_lambda[l], cmp_pos_k[l], cmp_w1_k[l], cmp_w2_k[l], cmp_pos_v[l], cmp_w1_v[l],
                         cmp_w2_v[l], norm_rnn_out[l], norm_att_out[l], w_out[l])
        x = x + (1.0 + g1[:, None, :]) * rms_norm(y, post_norm_mix[l])
        h = modulate(rms_norm(x, pre_norm_mlp[l]), sh2, sc2)
        y = jnp.square(jax.nn.relu(h @ w_ff1[l])) @ w_ff2[l]
        x = x + (1.0 + g2[:, None, :]) * rms_norm(y, post_norm_mlp[l])
    return x


def setup_inputs(seed=0):
    out = dict(first_inputs(seed))
    for name, value in second_inputs(seed + 1).items():
        if name != "x":
            out[name + "_2"] = value
    return out


def reference(
    x, positions, attn_norm, w_in, sgu_v_norm, sgu_w_spatial, sgu_b_spatial, lambda_q1,
    lambda_k1, lambda_q2, lambda_k2, subln_gain, w_out, ffn_norm, w_up, conv_w, conv_b, w_down,
    final_norm, c_2, ada_w_2, ada_b_2, pre_norm_mix_2, w_in_2, conv_w_2, conv_b_2, lru_wa_2,
    lru_ba_2, lru_wx_2, lru_bx_2, lru_lambda_2, cmp_pos_k_2, cmp_w1_k_2, cmp_w2_k_2,
    cmp_pos_v_2, cmp_w1_v_2, cmp_w2_v_2, norm_rnn_out_2, norm_att_out_2, w_out_2,
    post_norm_mix_2, pre_norm_mlp_2, w_ff1_2, w_ff2_2, post_norm_mlp_2,
):
    x = first_block(
        x, positions, attn_norm, w_in, sgu_v_norm, sgu_w_spatial, sgu_b_spatial, lambda_q1,
        lambda_k1, lambda_q2, lambda_k2, subln_gain, w_out, ffn_norm, w_up, conv_w, conv_b,
        w_down, final_norm,
    )
    return second_block(
        x, c_2, ada_w_2, ada_b_2, pre_norm_mix_2, w_in_2, conv_w_2, conv_b_2, lru_wa_2,
        lru_ba_2, lru_wx_2, lru_bx_2, lru_lambda_2, cmp_pos_k_2, cmp_w1_k_2, cmp_w2_k_2,
        cmp_pos_v_2, cmp_w1_v_2, cmp_w2_v_2, norm_rnn_out_2, norm_att_out_2, w_out_2,
        post_norm_mix_2, pre_norm_mlp_2, w_ff1_2, w_ff2_2, post_norm_mlp_2,
    )


_drawn_inputs = setup_inputs


def setup_inputs(seed=0):
    import zlib

    import numpy as np

    out = dict(_drawn_inputs(seed))
    spreads = {}
    factors = {'ada_b_2': 4.934,
     'conv_b_2': 7.848,
     'lru_ba_2': 64.0,
     'lru_bx_2': 24.291,
     'cmp_pos_k_2': 8.0,
     'cmp_pos_v_2': 3.628,
     'norm_rnn_out_2': 4.921,
     'norm_att_out_2': 4.714,
     'post_norm_mix_2': 3.405,
     'pre_norm_mlp_2': 3.27,
     'post_norm_mlp_2': 3.619}
    for name, (base, spread) in spreads.items():
        noise = np.random.default_rng([zlib.crc32(name.encode()), seed]).standard_normal(out[name].shape)
        drawn = base * np.exp(spread * noise) if base else spread * noise
        out[name] = __import__('jax').numpy.asarray(drawn.astype(out[name].dtype))
    for name, factor in factors.items():
        out[name] = (out[name] * factor).astype(out[name].dtype)
    return out
```

```python
from contextlib import ExitStack

import numpy as np
import concourse.bass as bass
from concourse import mybir

F32 = mybir.dt.float32
F32R = mybir.dt.float32r
I32 = mybir.dt.int32
ALU = mybir.AluOpType
ACT = mybir.ActivationFunctionType
AX = mybir.AxisListType

P = 128
S = 512
NT = S // P
D = 1024
DT = D // P
DEPTH = 2
HALF = D // 2
HT = HALF // P
HEADS = 4
FF = 2816
FG = FF // 256
FF2 = 4096
FG2 = FF2 // 512
EPS = 1e-6
NEG = -1e30
HEADS2 = 8
CMP_LEN, CMP_STRIDE = 32, 16
NCMP = (S - CMP_LEN) // CMP_STRIDE + 1
ROT = 16
THETA = 500000.0
LRU_C = 8.0
TAPS2 = 4
LOOK = 3
SLOPES = [2.0 ** (-8.0 * (h + 1) / HEADS2) for h in range(HEADS2)]
LAMBDA_INIT = [0.8 - 0.6 * float(np.exp(-0.3 * l)) for l in range(DEPTH)]

ROWS0 = {}
_n = 0
for _name, _k in (("attn_norm", DEPTH * DT), ("ffn_norm", DEPTH * DT), ("final_norm", DT), ("sgu_v_norm", DEPTH * HT),
                  ("subln_gain", DEPTH), ("pre_norm_mix_2", DT), ("post_norm_mix_2", DT), ("pre_norm_mlp_2", DT),
                  ("post_norm_mlp_2", DT), ("conv_b_2", HT), ("conv_w_2", TAPS2 * HT), ("lru_ba_2", HT),
                  ("lru_bx_2", HT), ("lru_lambda_2", HT), ("norm_rnn_out_2", HT), ("norm_att_out_2", HT)):
    ROWS0[_name] = (_n, _k)
    _n += _k
NROWS0 = _n
ADA_T = 6 * DT
ADA_W = ADA_T * P // 2
FT = 2 * FF // P
POS_ROW = ADA_T + DT
NROWS = [NROWS0, POS_ROW + 32] + [2 * FT] * 4
ATT_STEPS = 16 + 7
LOWEST = -3.0e38
ROUND = 12582912.0
TWO_PI = (2 * float(np.pi), 6.28125, 0.0019350051879882812, float(2 * np.pi - 6.28125 - 0.0019350051879882812))
PI_BELOW = 3.1415925


def constants():
    ident = np.eye(P, dtype=np.float32)
    half = ROT // 2
    rot = np.zeros((P, P), np.float32)
    invf = np.zeros((P, 1), np.float32)
    for base in (0, 64):
        for j in range(half):
            rot[base + j, base + half + j] = -1.0
            rot[base + half + j, base + j] = 1.0
            invf[base + j, 0] = invf[base + half + j, 0] = np.float32(THETA) ** np.float32(-2.0 * j / ROT)
    q = np.arange(P)[:, None]
    d = np.arange(S)[None, :] - (S - P) - q
    causal = np.where(d <= 0, 0.0, NEG).astype(np.float32)
    alibi = np.where(d <= 0, d, NEG).astype(np.float32)
    t = P * np.arange(NT)[None, :, None] + q[:, :, None]
    dc = (CMP_STRIDE * np.arange(NCMP) + CMP_LEN - 1)[None, None, :] - t
    alibi_c = np.where(dc <= 0, dc, NEG).astype(np.float32).reshape(P, NT * NCMP)
    seen = (q >= CMP_LEN - 1).astype(np.float32)
    return np.concatenate([ident, rot.T, causal, alibi, alibi_c, invf, seen], axis=1)


C_ID, C_ROT, C_CAUSAL, C_ALIBI = 0, P, 2 * P, 2 * P + S
C_ALIBIC = C_ALIBI + S
C_INVF = C_ALIBIC + NT * NCMP
C_SEEN = C_INVF + 1
NCONST = C_SEEN + 1


class Stripe:

    def __init__(self, kind, quarters, g0):
        self.kind, self.quarters, self.g0 = kind, quarters, g0


def plan():
    order, g = {}, 0

    def add(name, kind, quarters):
        nonlocal g
        order[name] = Stripe(kind, quarters, g)
        order[name].index = len(order) - 1
        g += quarters

    for l in range(DEPTH):
        for name, kind in (("u", "F"), ("vs", "T"), ("q", "F"), ("k", "F"), ("va", "T")):
            add((name, l), kind, 4)
        add(("out", l, 0), "F", 4)
        add(("out", l, 1), "F", 4)
        add(("up", l, 0), "U", 4)
        for j in range(1, FG):
            add(("up", l, j), "U", 4)
            add(("down", l, j - 1), "D2", 4)
        add(("down", l, FG - 1), "D2", 4)
    for name in ("g_rnn", "x_rnn", "q2"):
        add((name,), "F", 4)
    add(("kvs",), "F", 4)
    add(("kw",), "W", 3)
    add(("cmp", 0), "C", 4)
    add(("cmp", 1), "C", 4)
    add(("out2", 0), "F", 4)
    add(("out2", 1), "F", 4)
    add(("ff1", 0), "F", 4)
    for j in range(1, FG2):
        add(("ff1", j), "F", 4)
        add(("ff2", j - 1), "D4", 4)
    add(("ff2", FG2 - 1), "D4", 4)
    return order


def raw_quarter(kind, raw, q):
    if kind == "F":
        return raw[:, :].rearrange("p (k c) -> p k c", k=DT)[:, :, q * P:(q + 1) * P]
    if kind == "W":
        w = (P, P, 24)[q]
        return raw[:, 0:DT * 280].rearrange("p (k c) -> p k c", k=DT)[:, :, q * P:q * P + w]
    if kind in ("T", "C"):
        return raw[:, q * 1024:(q + 1) * 1024]
    if kind == "U":
        v = raw[:, :].rearrange("p (h k c) -> p h k c", h=2, k=DT)
        return v[:, q % 2, :, (q // 2) * P:(q // 2 + 1) * P]
    k = int(kind[1])
    return raw[:, 0:k * D].rearrange("p (k c) -> p k c", k=k)[:, :, q * 256:(q + 1) * 256]


def split_quarter(kind, part, slot, q):
    if kind in ("F", "U"):
        return part[:, slot, :].rearrange("p (k c) -> p k c", k=DT)
    if kind == "W":
        w = (P, P, 24)[q]
        return part[:, slot, 0:DT * w].rearrange("p (k c) -> p k c", k=DT)
    if kind in ("T", "C"):
        return part[:, slot, :]
    k = int(kind[1])
    return part[:, slot, 0:k * 256].rearrange("p (k c) -> p k c", k=k)


class Banks:

    def __init__(self):
        self.n, self.f, self.use = [0] * 8, [0] * 8, {}

    def take(self, key, bank, quarter=None, counted=True):
        self.use[key] = (bank, self.n[bank], self.f[bank], quarter)
        self.n[bank] += 1
        if quarter is None and counted:
            self.f[bank] += 1

    def __getitem__(self, key):
        return self.use[key]


def attention_units():
    units = []
    for hd in range(HEADS2):
        units.append((hd, "c", 0))
        for i in range(NT):
            units += [(hd, "s", i), (hd, "w", i)]
    return units


UNITS = attention_units()
NU = len(UNITS)
PV_BEFORE = [sum(1 for x in UNITS[:v] if x[1] != "c") for v in range(NU + 1)]


def bank_plan(st):
    b = Banks()
    b.ffn = {}
    for f in range(DT):
        b.take(("x", f), f)
    b.take("cols0", 0)

    def norm(e, bank=7):
        b.take(("norm", e), bank, counted=False)
        b.take(("rstd", e), bank)
        if e == ("final",):
            b.take(("rstd", ("mix2",)), 2)

    norm(("attn", 0))
    for l in range(DEPTH):
        for t in range(4):
            b.take(("u", l, t), t, st["u", l].g0 + t)
        for t in range(NT):
            b.take(("vs", l, t), 3 + t, st["vs", l].g0 + 3)
        if l == 0:
            b.take("cols1", 0)
            b.take("cols2", 1)
            for m in range(DEPTH):
                b.take(("wsT", m), 2 + m)
        for name in ("q", "k"):
            for t in range(4):
                b.take((name, l, t), t, st[name, l].g0 + t)
            for t in range(4):
                b.take(("rope", name, l, t), 4 + t % 2)
        for t in range(NT):
            b.take(("va", l, t), t, st["va", l].g0 + 3)
        for g in range(HT):
            b.take(("mix", l, g), 4 + g % 2)
        for n in range(ATT_STEPS):
            if n < 16:
                for m in range(2):
                    b.take(("S", l, n, m), 2 * (n % 2) + m)
            if 0 <= n - 2 < 16:
                b.take(("T", l, n - 2), 4 + n % 2)
            if 0 <= n - 3 < 16 and (n - 3) % 4 == 0:
                b.take(("O", l, (n - 3) // 4), 6, counted=False)
            if n >= 7 and (n - 7) % 4 == 0:
                norm(("sub", l, (n - 7) // 4))
        for m in range(DT):
            b.take(("out", l, m), m % 4, st["out", l, 0].g0 + m)
        norm(("ffn", l))
        b.ffn[l] = list(b.n)
        for t in range(4):
            b.n[t] += FG
            b.n[4 + t] += 2 * FG
        b.take(("ada", l), 0)
        norm(("attn", 1) if l == 0 else ("final",), 1)
    for name in ("g_rnn", "x_rnn", "q2"):
        for t in range(4):
            b.take((name, t), t, st[name,].g0 + t)
    for t in range(3):
        b.take(("kvs", t), t, st["kvs",].g0 + t)
    b.take(("vsel",), 3, st["kvs",].g0 + 3)
    b.take(("kw",), 0, st["kw",].g0)
    b.take(("vwin",), 1, st["kw",].g0 + 1)
    b.take(("gates",), 2, st["kw",].g0 + 2)
    for t in range(HT):
        b.take(("ra", t), 4 + t % 2)
        b.take(("rx", t), 6)
    norm(("rnn",))
    for j in range(2):
        for m in range(2):
            b.take(("chid", j, m), 2 * j + m, st["cmp", j].g0 + 3)
        b.take(("cout", j), 4 + j)
    for n in range(NU + 4):
        if n < NU:
            b.take(("S2", n), n % 3)
        if 0 <= n - 2 < NU:
            b.take(("T2", n - 2), 3 + n % 2)
        u = n - 3
        if 0 <= u < NU and u % 18 == 1:
            b.take(("O2", u // 18), 5 + (u // 18) % 2, counted=False)
    norm(("att",))
    for m in range(DT):
        b.take(("out2", m), m % 4, st["out2", 0].g0 + m)
    norm(("post_mix",))
    norm(("mlp",))
    b.ffn2 = list(b.n)
    for t in range(4):
        b.n[t] += FG2
        b.n[4 + t] += 2 * FG2
    norm(("post_mlp",), 1)
    for t in range(NT):
        for j in range(2):
            b.take(("y", t, j), 2 * (t % 2) + j)
    return b


def norm_plan():
    out, sq = {}, 0

    def add(e, k):
        nonlocal sq
        out[e] = (len(out), sq, k)
        sq += k

    for l in range(DEPTH):
        add(("attn", l), DT)
        for h in range(HEADS):
            add(("sub", l, h), 1)
        add(("ffn", l), DT)
    for e, k in ((("final",), 2 * DT), (("rnn",), HT), (("att",), HT), (("post_mix",), DT),
                 (("mlp",), DT), (("post_mlp",), DT)):
        add(e, k)
    return out


def split_plan():
    out, k = {}, 0
    for l in range(DEPTH):
        for name, n in (("attn", DT), ("sgu", HT), ("sub", HEADS), ("ffn", DT), ("act", 2 * FG)):
            out[(name, l)] = k
            k += n
    for name, n in (("mix2", DT), ("rnn", HT), ("cmp", 2), ("att", HT), ("mlp", DT), ("act2", 4 * FG2)):
        out[(name,)] = k
        k += n
    return out


def build(nc, a):
    STR = plan()
    BK = bank_plan(STR)
    NRM = norm_plan()
    SPL = split_plan()
    stripes = list(STR.values())
    by_quarter = [(st, q) for st in stripes for q in range(st.quarters)]

    with ExitStack() as ctx:
        def sb(name, shape, dt=F32, where=ctx):
            return where.enter_context(nc.sbuf_tensor(name, shape, dt))

        def sem(name):
            return ctx.enter_context(nc.semaphore(name))

        raw = [sb(f"raw{i}", [P, 4096]) for i in range(2)]
        w_hi = sb("w_hi", [P, 4, 1024], F32R)
        w_lo = sb("w_lo", [P, 4, 1024], F32R)
        h = sb("h", [P, DT, S])
        n_hi = sb("n_hi", [P, DT, S], F32R)
        n_lo = sb("n_lo", [P, DT, S], F32R)
        zb = sb("zb", [P, 4096])
        zc = sb("zc", [P, 2048])
        zd = sb("zd", [P, 3328])
        tb = sb("tb", [P, 3, S])
        sq = sb("sq", [P, 2, S])
        rt = sb("rt", [P, 2 * NT])
        rstd = sb("rstd", [P, 2 * NT + 1])
        ms = sb("ms", [P, 2 * NT])
        const = sb("const", [P, NCONST])
        ones = sb("ones", [P, P])
        cols = sb("cols", [P, 6, P])
        par = sb("par", [P, DEPTH, FG * 16])
        cpar = sb("cpar", [P, 17])
        small = sb("small", [P, 48])
        more = sb("more", [P, 144])
        blkw = sb("blkw", [P, 2, HT, P])
        cw2 = [sb(f"cw2_{i}", [P, 2, P]) for i in range(2)]
        with ExitStack() as part:
            za = sb("za", [P, 4096], F32, part)
        x_hi = sb("x_hi", [P, 4, S], F32R)
        x_lo = sb("x_lo", [P, 4, S], F32R)
        with ExitStack() as part:
            zy = sb("zy", [P, 4096], F32, part)
        cb_hi = sb("cb_hi", [P, 16, 64], F32R)
        cb_lo = sb("cb_lo", [P, 16, 64], F32R)
        sb("rest_of_zy", [P, 2048])
        ps = [ctx.enter_context(nc.psum_tensor(f"ps{i}", [P, S], F32)) for i in range(8)]

        full = [sem(f"full{i}") for i in range(8)]
        free = [sem(f"free{i}") for i in range(8)]
        landed = [sem(f"landed{i}") for i in range(2)]
        whi_ready, wlo_ready = sem("whi_ready"), sem("wlo_ready")
        quarter_done = sem("quarter_done")
        ada_in, ada_used = sem("ada_in"), sem("ada_used")
        consts_in, x_in, pos_in = sem("consts_in"), sem("x_in"), sem("pos_in")
        gains_in, rows_in = sem("gains_in"), sem("rows_in")
        lam_in, sguw_in, sgub_in, cw2_in = sem("lam_in"), sem("sguw_in"), sem("sgub_in"), sem("cw2_in")
        ones_set, sgu_masked = sem("ones_set"), sem("sgu_masked")
        blk_zero, blk_in = sem("blk_zero"), sem("blk_in")
        c_ready = sem("c_ready")
        ang_ready, rope_ready = sem("ang_ready"), sem("rope_ready")
        lam_dots, lam_exp = sem("lam_dots"), sem("lam_exp")
        h_set = sem("h_set")
        sq_ready, sq_used = sem("sq_ready"), sem("sq_used")
        means_ready = sem("means_ready")
        rstd_ready = sem("rstd_ready")
        val_ready, hi_ready, lo_ready = sem("val_ready"), sem("hi_ready"), sem("lo_ready")
        dve_seq = sem("dve_seq")
        act_seq = sem("act_seq")
        vss_ready, vroot_ready, vn_ready, qk_ready = (sem("vss_ready"), sem("vroot_ready"), sem("vn_ready"),
                                                      sem("qk_ready"))
        max_ready, exp_ready, probs_ready, pv_done = (sem("max_ready"), sem("exp_ready"), sem("probs_ready"),
                                                      sem("pv_done"))
        conv_begun, conv_tap, silu_done, par_ready = (sem("conv_begun"), sem("conv_tap"), sem("silu_done"),
                                                      sem("par_ready"))
        xr_begun, gate_set, decay_ready, ratio_ready, rootm_ready, rnn_ready = (
            sem("xr_begun"), sem("gate_set"), sem("decay_ready"), sem("ratio_ready"), sem("rootm_ready"),
            sem("rnn_ready"))
        sp_abs, sp_ready = sem("sp_abs"), sem("sp_ready")
        bias_ready, y_zero, y_sent = sem("bias_ready"), sem("y_zero"), sem("y_sent")

        def filled(e, key):
            b, _, f, quarter = BK[key]
            if quarter is None:
                e.wait_ge(full[b], f + 1)
            else:
                e.wait_ge(quarter_done, quarter + 1)
            return ps[b]

        def emptied(e, key):
            b, n = BK[key][:2]
            e.wait_ge(free[b], n + 1)

        def freed(key):
            return free[BK[key][0]]

        def tiles(buf, k=4):
            return buf.rearrange("p (t s) -> p t s", t=k)

        ident = const[:, C_ID:C_ID + P]
        rotT = const[:, C_ROT:C_ROT + P]
        causal = const[:, C_CAUSAL:C_CAUSAL + S]
        alibi = const[:, C_ALIBI:C_ALIBI + S]
        alibi_c = const[:, C_ALIBIC:C_ALIBIC + NT * NCMP]
        xin = tiles(za[:, :])
        rows = [zb[:, i * P:(i + 1) * P] for i in range(6)]
        sguw = tiles(zb[:, 1024:2048], 8)
        lamv = tiles(zb[:, 2048:2560], 8)
        lamp = tiles(zb[:, 2560:2816], 4)
        u, vg = tiles(za[:, 0:2048]), tiles(za[:, 2048:4096])
        qT, kT = tiles(zb[:, 0:2048]), tiles(zb[:, 2048:4096])
        va = tiles(zc[:, :])
        cosT, sinT = zd[:, 0:512], zd[:, 512:1024]
        wsT = tiles(zd[:, 1024:2048], 8)
        sgub = tiles(zd[:, 2048:3072], 8)
        scores = [zy[:, i * 1024:(i + 1) * 1024].rearrange("p (m s) -> p m s", m=2) for i in range(2)]
        probs = [zy[:, 2048 + i * 512:2560 + i * 512] for i in range(2)]
        pT = [zy[:, 3072 + i * 512:3584 + i * 512] for i in range(2)]
        scores2 = [zy[:, i * 512:(i + 1) * 512] for i in range(4)]
        ada_w, ada_sum = zb[:, 0:ADA_W], zy[:, 0:ADA_W]
        pTc = zd[:, 2752:3264]

        def col(name, i=0, k=1):
            c = ROWS0[name][0] + i
            return cols[:, 0, c:c + k]

        nmx, lsum, rec = small[:, 0:4], small[:, 4:8], small[:, 8:12]
        vss = small[:, 12:28]
        lamd, lame, lamneg, subg = small[:, 28:32], small[:, 32:36], small[:, 36:38], small[:, 38:40]
        eps, zero1 = small[:, 40:41], small[:, 41:42]
        mxs = small[:, 44:48]
        mod = more[:, 0:ADA_T]
        gs1, gs2, pg1, pg2 = (more[:, 48 + 8 * i:56 + 8 * i] for i in range(4))
        csilu = more[:, 80:88]
        spt = more[:, 88:116]
        cmx, csum = more[:, 116:120], more[:, 120:124]
        cbias = more[:, 124:126]
        gr, xc = tiles(za[:, 0:2048]), tiles(za[:, 2048:4096])
        oT = xc
        cval = [tiles(za[:, 2048 + i * 1024:3072 + i * 1024], 16) for i in range(2)]
        q2 = tiles(zc[:, :])
        kk = [tiles(zb[:, i * 1024:(i + 1) * 1024], 2) for i in range(2)]
        kd = [tiles(zb[:, 2048 + i * 1024:3072 + i * 1024], 2) for i in range(2)]
        v2 = [tiles(zd[:, i * 512:(i + 1) * 512]) for i in range(2)]
        gates = tiles(zd[:, 1024:1120])
        bias_h = [zd[:, 1152 + i * 512:1664 + i * 512] for i in range(2)]
        bias_c = [zd[:, 2176 + i * 124:2300 + i * 124] for i in range(2)]
        kcmp, vcmp = zd[:, 2432:2494], zd[:, 2496:2624]
        ghid = tiles(zd[:, 2624:2752], 2)
        rn = [zy[:, i * 512:(i + 1) * 512] for i in range(8)]
        rb = [zc[:, i * 512:(i + 1) * 512] for i in range(4)]
        y = tiles(zy[:, :], DT)

        def ffn_h(l, f):
            return free[4 + f % 4], BK.ffn[l][4 + f % 4] + 2 * (FG - 1) + f // 4 + 1

        def landed_value(st):
            return 32 * (st.index // 2 + 1)

        block = ctx.enter_context(nc.Block())

        @block.sync
        def _(sp):
            def room(name):
                i = STR[name].index
                if i >= 2:
                    old = stripes[i - 2]
                    sp.wait_ge(whi_ready, old.g0 + old.quarters)
                    sp.wait_ge(wlo_ready, old.g0 + old.quarters)
                return i % 2

            def two(slot, pairs):
                for dst, src in pairs:
                    sp.dma_start(dst, src).then_inc(landed[slot], 16)

            def load_f(name, w):
                slot = room(name)
                r = raw[slot][:, 0:DT * w.shape[1]].rearrange("p (k c) -> p k c", k=DT)
                v = w.rearrange("(k p) c -> p k c", p=P)
                two(slot, [(r[:, 0:4], v[:, 0:4]), (r[:, 4:8], v[:, 4:8])])

            def load_up(slot, l, j):
                r = raw[slot][:, :].rearrange("p (h k c) -> p h k c", h=2, k=DT)
                v = a["w_up"][l].rearrange("(k p) c -> p k c", p=P)
                two(slot, [(r[:, i], v[:, :, bass.ds(j * 256 + i * FF, 256)]) for i in range(2)])

            def load_down(slot, l, j):
                two(slot, [(raw[slot][:, k * D:(k + 1) * D], a["w_down"][l][bass.ds(j * 256 + k * P, P), :])
                           for k in range(2)])

            def late_loads():
                def row(tile, at, src, k):
                    sp.dma_start(rows[tile][at:at + k, :], src).then_inc(rows_in, 16)

                sp.dma_start(sguw, a["sgu_w_spatial"].rearrange("l g p q -> p (l g) q")).then_inc(sguw_in, 16)
                sp.dma_start(zd[:, 2048:3072],
                             a["sgu_b_spatial"].rearrange("l g p -> (l g p)").partition_broadcast(P))\
                    .then_inc(sgub_in, 16)
                row(1, 0, a["ada_b_2"].rearrange("l (r p) -> (l r) p", p=P), ADA_T)
                row(1, ADA_T, a["c_2"].rearrange("l (r p) -> (l r) p", p=P), DT)
                for j, name in enumerate(("cmp_pos_k_2", "cmp_pos_v_2")):
                    row(1, POS_ROW + 16 * j, a[name].rearrange("l (j e) d -> (l j) (e d)", e=2), 16)
                for l in range(DEPTH):
                    for j in range(3):
                        row(2 + 2 * l + j // 2, FT * (j % 2), a["conv_w"][l, j, :].rearrange("(r p) -> r p", p=P), FT)
                    row(3 + 2 * l, FT, a["conv_b"][l, :].rearrange("(r p) -> r p", p=P), FT)
                for j, name in enumerate(("cmp_w2_k_2", "cmp_w2_v_2")):
                    for dup in range(2):
                        sp.dma_start(cw2[j][:, :, 64 * dup:64 * dup + 64],
                                     a[name][0].rearrange("(m p) d -> p m d", p=P)).then_inc(cw2_in, 16)
                sp.wait_ge(blk_zero, 1)
                for j, name in enumerate(("lru_wa_2", "lru_wx_2")):
                    for e in range(2):
                        sp.dma_start(blkw[64 * e:64 * e + 64, j, :, 64 * e:64 * e + 64],
                                     a[name][0].rearrange("(t e) i j -> e i t j", e=2)[e]).then_inc(blk_in, 16)

            def load_ada(l, k):
                sp.dma_start(ada_w, a["ada_w_2"][0][bass.ds(k * P, P), l * ADA_W:(l + 1) * ADA_W]).then_inc(ada_in, 16)

            sp.dma_start(xin, a["x"].rearrange("b (t p) c -> p (b t) c", p=P)).then_inc(x_in, 16)
            for l in range(DEPTH):
                for j, name in enumerate(("u", "vs", "q", "k", "va")):
                    load_f((name, l), a["w_in"][l][:, j * 512:(j + 1) * 512])
                    if l == 0 and j == 1:
                        late_loads()
                for j in range(2):
                    load_f(("out", l, j), a["w_out"][l][:, j * 512:(j + 1) * 512])
                load_up(room(("up", l, 0)), l, 0)
                sp.wait_ge(lo_ready, SPL["sub", l] + HEADS)
                load_ada(l, 0)
                load_up(room(("up", l, 1)), l, 1)
                load_down(room(("down", l, 0)), l, 0)
                g0 = STR["up", l, 2].g0
                for first, end in ((2, DT + 1), (DT + 1, FG)):
                    with sp.Fori(first, end) as j:
                        sp.wait_ge(whi_ready, g0 - 4 + (j - 2) * 8)
                        sp.wait_ge(wlo_ready, g0 - 4 + (j - 2) * 8)
                        load_up(STR["up", l, 2].index % 2, l, j)
                        sp.wait_ge(whi_ready, g0 + (j - 2) * 8)
                        sp.wait_ge(wlo_ready, g0 + (j - 2) * 8)
                        load_down(STR["down", l, 1].index % 2, l, j - 1)
                        if first == 2:
                            sp.wait_ge(ada_used, DT * l + j - 1)
                            load_ada(l, j - 1)
                load_down(room(("down", l, FG - 1)), l, FG - 1)
            w2 = a["w_in_2"][0]
            for j, name in enumerate(("g_rnn", "x_rnn", "q2", "kvs")):
                load_f((name,), w2[:, j * 512:(j + 1) * 512])
            load_f(("kw",), w2[:, 2048:2328])
            for j, name in enumerate(("cmp_w1_k_2", "cmp_w1_v_2")):
                slot = room(("cmp", j))
                r = raw[slot][:, :].rearrange("p (k c) -> p k c", k=16)
                v = a[name][0].rearrange("(k p) c -> p k c", p=P)
                two(slot, [(r[:, 0:8], v[:, 0:8]), (r[:, 8:16], v[:, 8:16])])
            for j in range(2):
                load_f(("out2", j), a["w_out_2"][0][:, j * 512:(j + 1) * 512])

            def load_ff1(slot, j):
                r = raw[slot][:, :].rearrange("p (k c) -> p k c", k=DT)
                v = a["w_ff1_2"][0].rearrange("(k p) c -> p k c", p=P)
                two(slot, [(r[:, 4 * i:4 * i + 4], v[:, 4 * i:4 * i + 4, bass.ds(j * 512, 512)]) for i in range(2)])

            def load_ff2(slot, j):
                r = raw[slot][:, :].rearrange("p (k c) -> p k c", k=4)
                two(slot, [(r[:, 2 * i:2 * i + 2],
                            a["w_ff2_2"][0][bass.ds(j * 512 + i * 256, 256), :].rearrange("(k p) c -> p k c", p=P))
                           for i in range(2)])

            load_ff1(room(("ff1", 0)), 0)
            load_ff1(room(("ff1", 1)), 1)
            load_ff2(room(("ff2", 0)), 0)
            g0 = STR["ff1", 2].g0
            with sp.Fori(2, FG2) as j:
                sp.wait_ge(whi_ready, g0 - 4 + (j - 2) * 8)
                sp.wait_ge(wlo_ready, g0 - 4 + (j - 2) * 8)
                load_ff1(STR["ff1", 2].index % 2, j)
                sp.wait_ge(whi_ready, g0 + (j - 2) * 8)
                sp.wait_ge(wlo_ready, g0 + (j - 2) * 8)
                load_ff2(STR["ff2", 1].index % 2, j - 1)
            load_ff2(room(("ff2", FG2 - 1)), FG2 - 1)
            for t in range(NT):
                for j in range(2):
                    emptied(sp, ("y", t, j))
                sp.dma_start(a["out"][0, t * P:(t + 1) * P, :], zb[:, t * D:(t + 1) * D]).then_inc(y_sent, 16)
            sp.wait_ge(y_sent, 16 * NT)

        @block.gpsimd
        def _(pool):
            pool.memset(ones[:, :], 1.0).then_inc(ones_set, 1)
            pool.memset(eps, EPS).then_inc(ones_set, 1)
            pool.memset(zero1, 0.0).then_inc(ones_set, 1)
            pool.memset(blkw[:, :, :, :], 0.0).then_inc(blk_zero, 1)
            pool.wait_ge(sguw_in, 16)
            pool.affine_select(out=sguw, in_=sguw, compare_op=ALU.is_ge, fill=0.0, base=0,
                               pattern=[[0, DEPTH * 4], [-1, P]], channel_multiplier=1).then_inc(sgu_masked, 1)

            def lo(g, value, used):
                st, q = by_quarter[g]
                if used is not None:
                    pool.wait_ge(quarter_done, used)
                pool.wait_ge(whi_ready, value)
                pool.tensor_tensor(split_quarter(st.kind, w_lo, g % 4, q), raw_quarter(st.kind, raw[st.index % 2], q),
                                   split_quarter(st.kind, w_hi.bitcast(F32), g % 4, q), ALU.subtract)\
                    .then_inc(wlo_ready, 1)

            done = 0
            for first, groups in [(STR["up", l, 1].g0, FG) for l in range(DEPTH)] + [(STR["ff1", 1].g0, FG2)]:
                for g in range(done, first):
                    lo(g, g + 1, g - 3 if g >= 4 else None)
                with pool.Fori(0, groups - 1) as j:
                    for g in range(first, first + 8):
                        lo(g, g + 1 + j * 8, g - 3 + j * 8)
                done = first + 8 * (groups - 1)
            for g in range(done, len(by_quarter)):
                lo(g, g + 1, g - 3)

        @block.scalar
        def _(act):
            act.dma_start(const[:, :], a["consts"]).then_inc(consts_in, 16)
            for name, (at, k) in ROWS0.items():
                v = a[name]
                if len(v.shape) == 1:
                    v = v.rearrange("(r p) -> r p", p=P)
                elif len(v.shape) == 2:
                    v = v.rearrange("l (r p) -> (l r) p", p=P)
                else:
                    v = v.rearrange("l w (r p) -> (l w r) p", p=P)
                act.dma_start(rows[0][at:at + k, :], v).then_inc(gains_in, 16)
            act.dma_start(zc[:, 0:S].bitcast(I32), a["positions"][0, :].partition_broadcast(P)).then_inc(pos_in, 16)
            for j, name in enumerate(("lambda_q1", "lambda_k1", "lambda_q2", "lambda_k2")):
                for l in range(DEPTH):
                    act.dma_start(lamv[:, 2 * j + l, :], a[name][l, :].partition_broadcast(P)).then_inc(lam_in, 16)

            ahead = [0]

            def hi(g, landed_at, used):
                st, q = by_quarter[g]
                if q == 0:
                    act.wait_ge(landed[st.index % 2], landed_at)
                if used is not None:
                    act.wait_ge(quarter_done, used)
                act.activation(split_quarter(st.kind, w_hi, g % 4, q), raw_quarter(st.kind, raw[st.index % 2], q),
                               ACT.Copy).then_inc(whi_ready, 1)

            def ensure(upto):
                for g in range(ahead[0], min(upto, len(by_quarter))):
                    hi(g, landed_value(by_quarter[g][0]), g - 3 if g >= 4 else None)
                ahead[0] = max(ahead[0], min(upto, len(by_quarter)))

            def square(e, i, src, ready, scale=1.0):
                n = NRM[e][1] + i
                act.wait_ge(*ready)
                if n >= 2:
                    act.wait_ge(sq_used, n - 1)
                act.activation(sq[:, n % 2, :], src, ACT.Square, scale=scale).then_inc(sq_ready, 1)

            def squares(e, src, ready):
                for f in range(NRM[e][2]):
                    square(e, f, src(f), ready(f))

            def root(e, width):
                num, sq0, k = NRM[e]
                b = BK["norm", e][0]
                act.wait_ge(sq_used, sq0 + k)
                if num >= 1:
                    act.wait_ge(rstd_ready, num)
                act.activation(rt[:, 0:NT], ps[b][:, 0:NT], ACT.Sqrt, bias=eps, scale=1.0 / width)\
                    .then_inc(free[b], 1)

            def split_hi(k, src, dst):
                act.wait_ge(val_ready, k + 1)
                act.activation(dst, src, ACT.Copy).then_inc(hi_ready, 1)

            def split_tiles(name, count, at):
                for f in range(count):
                    k = SPL[name] + f
                    split_hi(k, tb[:, k % 3, :], n_hi[:, at + f, :])

            act.wait_ge(ones_set, 3)

            def tables():
                act.wait_ge(ang_ready, 1)
                act.activation(sinT, zc[:, 1024:1536], ACT.Sin).then_inc(rope_ready, 1)
                act.activation(cosT, zc[:, 1536:2048], ACT.Sin).then_inc(rope_ready, 1)
                act.wait_ge(lam_dots, 1)
                act.activation(lame, lamd, ACT.Exp).then_inc(lam_exp, 1)
                act.activation(spt[:, 0:4], col("lru_lambda_2", 0, HT), ACT.Abs).then_inc(act_seq, 1)
                act.wait_ge(act_seq, 1)
                act.activation(spt[:, 4:8], spt[:, 0:4], ACT.Exp, scale=-1.0).then_inc(sp_abs, 1)

            for l in range(DEPTH):
                g0 = STR["u", l].g0
                if l == 0:
                    squares(("attn", l), lambda f: h[:, f, :], lambda f: (free[f], BK["x", f][1] + 1))
                root(("attn", l), D)
                ensure(g0 + 4)
                split_tiles(("attn", l), DT, 0)
                for t in range(4):
                    ensure(g0 + t + 1 + LOOK)
                    act.activation(u[:, t, :], filled(act, ("u", l, t))[:, :], ACT.Gelu_apprx_tanh)\
                        .then_inc(freed(("u", l, t)), 1)
                ensure(g0 + 8 + LOOK)
                if l == 0:
                    tables()
                for t in range(NT):
                    act.activation(vg[:, t, :], filled(act, ("vs", l, t))[:, :], ACT.Gelu_apprx_tanh)\
                        .then_inc(freed(("vs", l, t)), 1)
                act.wait_ge(vss_ready, 4 * l + 4)
                act.activation(vss, vss, ACT.Sqrt, bias=eps, scale=1.0 / P).then_inc(vroot_ready, 1)
                if l == 0:
                    for key in ("cols1", "cols2", ("wsT", 0), ("wsT", 1)):
                        emptied(act, key)
                    act.activation(csilu, cols[:, 1, ADA_T:ADA_T + DT], ACT.Silu).then_inc(c_ready, 1)
                for j, name in enumerate(("q", "k")):
                    for t in range(4):
                        ensure(g0 + 8 + 4 * j + t + 1 + LOOK)
                        act.activation((qT, kT)[j][:, t, :], filled(act, (name, l, t))[:, :], ACT.Copy,
                                       scale=0.125 if j == 0 else 1.0).then_inc(freed((name, l, t)), 1)
                ensure(g0 + 20 + LOOK)
                for t in range(NT):
                    act.activation(va[:, t, :], filled(act, ("va", l, t))[:, :], ACT.Copy)\
                        .then_inc(freed(("va", l, t)), 1)
                split_tiles(("sgu", l), HT, 0)
                for n in range(ATT_STEPS):
                    if n < 16:
                        i = n % 4
                        act.wait_ge(max_ready, l * 16 + n + 1)
                        for m in range(2):
                            sc = scores[n % 2][:, m, 0:(i + 1) * P]
                            c = 2 * (n % 2) + m
                            act.activation(sc, sc, ACT.Exp, bias=nmx[:, c:c + 1], accum_out=lsum[:, c:c + 1])\
                                .then_inc(exp_ready, 1)
                    if 0 <= n - 2 < 16:
                        v = n - 2
                        i, uv = v % 4, l * 16 + v
                        t_ = filled(act, ("T", l, v))
                        if uv >= 2:
                            act.wait_ge(pv_done, uv - 1)
                        act.activation(pT[v % 2][:, 0:(i + 1) * P], t_[:, 0:(i + 1) * P], ACT.Copy)\
                            .then_inc(freed(("T", l, v)), 1)
                    if n >= 6 and (n - 6) % 4 == 0:
                        hd = (n - 6) // 4
                        if hd < HEADS:
                            squares(("sub", l, hd), lambda f: tb[:, 2, :],
                                    lambda f: (freed(("O", l, hd)), BK["O", l, hd][1] + 1))
                    if n >= 7 and (n - 7) % 4 == 0:
                        hd = (n - 7) // 4
                        root(("sub", l, hd), P)
                        k = SPL["sub", l] + hd
                        split_hi(k, tb[:, k % 2, :], n_hi[:, HT + hd, :])
                for m in range(DT):
                    ensure(STR["out", l, 0].g0 + m + LOOK + 1)
                    square(("ffn", l), m, h[:, m, :], (freed(("out", l, m)), BK["out", l, m][1] + 1))
                root(("ffn", l), D)
                ensure(STR["up", l, 0].g0 + 4)
                split_tiles(("ffn", l), DT, 0)

                n0 = BK.ffn[l]
                gq = STR["up", l, 1].g0

                def up_steps(j, first, run_ahead):
                    act.wait_ge(par_ready, 1 + l * FG + j + 1)
                    if not first:
                        act.wait_ge(lo_ready, SPL["act", l] + 2 * j)
                    for i in range(2):
                        for t in (2 * i, 2 * i + 1):
                            run_ahead(t)
                            act.wait_ge(quarter_done, STR["up", l, 0].g0 + t + 1 if first else gq + t + 1 + 8 * (j - 1))
                            act.activation(rb[t], ps[t][:, :], ACT.Identity, bias=cpar[:, 4 * t + 3:4 * t + 4],
                                           scale=cpar[:, 4 * t + 2:4 * t + 3]).then_inc(conv_begun, 1)
                        act.wait_ge(free[2 * i], n0[2 * i] + j + 1)
                        act.activation(rb[2 * i], rb[2 * i], ACT.Silu).then_inc(silu_done, 1)
                    for i in range(4, 8):
                        run_ahead(i)
                    if not first:
                        act.wait_ge(quarter_done, gq + 8 * j)
                    for i in range(2):
                        split_hi(SPL["act", l] + 2 * j + i, rb[2 * i], x_hi[:, i, :])

                g_up = STR["up", l, 0].g0
                up_steps(0, True, lambda i: ensure(g_up + min(i, 3) + 1 + LOOK))
                assert ahead[0] == gq + LOOK
                with act.Fori(1, FG) as j:
                    def run_ahead(i):
                        g = gq + i + LOOK
                        hi(g, landed_value(by_quarter[g][0]) + 32 * (j - 1), g - 3 + 8 * (j - 1))
                    up_steps(j, False, run_ahead)
                ahead[0] = gq + 8 * (FG - 1) + LOOK
                for m in range(DT):
                    ensure(gq + 8 * (FG - 1) + m // 2 + 1 + LOOK)
                    if l == 0:
                        square(("attn", 1), m, h[:, m, :], ffn_h(l, m))
                    else:
                        square(("final",), 2 * m, h[:, m, :], ffn_h(l, m))
                        square(("final",), 2 * m + 1, h[:, m, :], ffn_h(l, m), col("final_norm", m))

            act.wait_ge(means_ready, 1)
            act.wait_ge(rstd_ready, NRM["final",][0])
            act.activation(rt[:, :], ms[:, :], ACT.Sqrt, bias=zero1).then_inc(act_seq, 1)
            g0 = STR["g_rnn",].g0
            ensure(g0 + 4)
            split_tiles(("mix2",), DT, 0)
            for t in range(4):
                ensure(g0 + t + 1 + LOOK)
                act.activation(gr[:, t, :], filled(act, ("g_rnn", t))[:, :], ACT.Gelu_apprx_tanh)\
                    .then_inc(freed(("g_rnn", t)), 1)
            for t in range(4):
                ensure(g0 + 4 + t + 1 + LOOK)
                act.activation(xc[:, t, :], filled(act, ("x_rnn", t))[:, :], ACT.Identity, bias=col("conv_b_2", t),
                               scale=col("conv_w_2", 3 * HT + t)).then_inc(xr_begun, 1)
            for t in range(4):
                ensure(g0 + 8 + t + 1 + LOOK)
                act.activation(q2[:, t, :], filled(act, ("q2", t))[:, :], ACT.Copy, scale=0.125)\
                    .then_inc(freed(("q2", t)), 1)
            for j in range(2):
                ensure(g0 + 12 + j + 1 + LOOK)
                b = filled(act, ("kvs", j))
                for g in range(2):
                    act.activation(kk[j][0:64, g, :], b[64 * g:64 * g + 64, :], ACT.Copy)
                    last = act.activation(kk[j][64:128, g, 0:S - 1], b[64 * g:64 * g + 64, 1:S], ACT.Copy)
                last.then_inc(freed(("kvs", j)), 1)
            for j in range(2):
                key, vkey = ((("kvs", 2), ("vsel",)), (("kw",), ("vwin",)))[j]
                ensure(g0 + 15 + 2 * j + LOOK)
                b = filled(act, key)
                for g in range(2):
                    for half in range(2):
                        last = act.activation(kd[j][64 * half:64 * half + 64, g, :], b[64 * g:64 * g + 64, :],
                                              ACT.Copy)
                last.then_inc(freed(key), 1)
                ensure(g0 + 16 + 2 * j + LOOK)
                act.activation(zd[:, j * 512:(j + 1) * 512], filled(act, vkey)[:, :], ACT.Copy)\
                    .then_inc(freed(vkey), 1)
            ensure(g0 + 19 + LOOK)
            act.activation(zd[:, 1024:1120], filled(act, ("gates",))[:, 0:96], ACT.Sigmoid)\
                .then_inc(freed(("gates",)), 1)
            act.wait_ge(sp_ready, 1)
            for t in range(HT):
                if t >= 1:
                    act.wait_ge(rnn_ready, t)
                b = filled(act, ("ra", t))
                act.activation(rn[0], b[:, :], ACT.Sigmoid, bias=col("lru_ba_2", t)).then_inc(freed(("ra", t)), 1)
                b = filled(act, ("rx", t))
                act.activation(rn[1], b[:, :], ACT.Sigmoid, bias=col("lru_bx_2", t)).then_inc(freed(("rx", t)), 1)
                emptied(act, ("ra", t))
                act.activation(rn[2], rn[0], ACT.Exp, scale=spt[:, 20 + t:21 + t])
                act.activation(rn[3], rn[0], ACT.Tanh, scale=spt[:, 24 + t:25 + t]).then_inc(decay_ready, 1)
                act.wait_ge(ratio_ready, t + 1)
                act.activation(rn[4], rn[4], ACT.Sqrt, bias=zero1, scale=2.0).then_inc(rootm_ready, 1)
            squares(("rnn",), lambda f: gr[:, f, :], lambda f: (rnn_ready, f + 1))
            root(("rnn",), HALF)
            split_tiles(("rnn",), HT, 0)
            for j in range(2):
                act.wait_ge(val_ready, SPL["cmp",] + j + 1)
                if j == 1:
                    act.wait_ge(quarter_done, STR["cmp", 0].g0 + 4)
                act.activation(cb_hi[:, :, :], cval[j], ACT.Copy).then_inc(hi_ready, 1)
                ensure(STR["cmp", j].g0 + 4 + LOOK)
                for m in range(2):
                    b = filled(act, ("chid", j, m))
                    act.activation(cbias[:, m:m + 1], b[:, 62:63], ACT.Copy).then_inc(act_seq, 1)
                    act.wait_ge(act_seq, 3 + 2 * j + m)
                    act.activation(ghid[:, m, 0:62], b[:, 0:62], ACT.Gelu_apprx_tanh, bias=cbias[:, m:m + 1])\
                        .then_inc(freed(("chid", j, m)), 1)
                b = filled(act, ("cout", j))
                if j == 0:
                    act.activation(kcmp, b[:, 0:62], ACT.Copy).then_inc(freed(("cout", j)), 1)
                else:
                    act.activation(vcmp[0:NCMP, :], b[0:NCMP, 0:128], ACT.Copy).then_inc(freed(("cout", j)), 1)

            def bias(hd):
                act.activation(bias_h[hd % 2], alibi, ACT.Copy, scale=SLOPES[hd])
                act.activation(bias_c[hd % 2], alibi_c, ACT.Copy, scale=SLOPES[hd]).then_inc(bias_ready, 1)

            bias(0)
            for n in range(NU + 4):
                if n < NU:
                    hd, br, i = UNITS[n]
                    if br == "s" and i == 2 and hd + 1 < HEADS2:
                        bias(hd + 1)
                    sc = scores2[n % 4]
                    act.wait_ge(max_ready, 32 + n + 1)
                    if br == "c":
                        act.activation(sc[:, 0:124], sc[:, 0:124], ACT.Exp).then_inc(exp_ready, 1)
                    else:
                        sc = sc[:, 0:(i + 1) * P]
                        act.activation(sc, sc, ACT.Exp, bias=nmx[:, n % 4:n % 4 + 1],
                                       accum_out=lsum[:, n % 4:n % 4 + 1]).then_inc(exp_ready, 1)
                v = n - 2
                if 0 <= v < NU:
                    hd, br, i = UNITS[v]
                    before = PV_BEFORE[v]
                    t_ = filled(act, ("T2", v))
                    if br == "c":
                        act.wait_ge(pv_done, 32 + before)
                        act.activation(pTc[0:NCMP, :], t_[0:NCMP, :], ACT.Copy).then_inc(freed(("T2", v)), 1)
                    else:
                        act.wait_ge(pv_done, 32 + before - 1)
                        act.activation(pT[before % 2][:, 0:(i + 1) * P], t_[:, 0:(i + 1) * P], ACT.Copy)\
                            .then_inc(freed(("T2", v)), 1)
            squares(("att",), lambda f: oT[:, f, :], lambda f: (freed(("O2", f)), BK["O2", f][1] + 1))
            root(("att",), HALF)
            split_tiles(("att",), HT, HT)
            for m in range(DT):
                ensure(STR["out2", 0].g0 + m + LOOK + 1)
                square(("post_mix",), m, y[:, m, :], (freed(("out2", m)), BK["out2", m][1] + 1))
            root(("post_mix",), D)
            ensure(STR["ff1", 0].g0 + 4)
            squares(("mlp",), lambda f: h[:, f, :], lambda f: (h_set, DT + f + 1))
            root(("mlp",), D)
            split_tiles(("mlp",), DT, 0)

            n0 = BK.ffn2
            gq = STR["ff1", 1].g0

            def ff1_steps(j, first, run_ahead):
                if not first:
                    act.wait_ge(lo_ready, SPL["act2",] + 4 * j)
                for t in range(4):
                    run_ahead(t)
                    act.wait_ge(quarter_done, STR["ff1", 0].g0 + t + 1 if first else gq + t + 1 + 8 * (j - 1))
                    act.activation(rb[t], ps[t][:, :], ACT.Relu).then_inc(free[t], 1)
                for i in range(4, 8):
                    run_ahead(i)
                if not first:
                    act.wait_ge(quarter_done, gq + 8 * j)
                for t in range(4):
                    split_hi(SPL["act2",] + 4 * j + t, rb[t], x_hi[:, t, :])

            g_up = STR["ff1", 0].g0
            ff1_steps(0, True, lambda i: ensure(g_up + min(i, 3) + 1 + LOOK))
            assert ahead[0] == gq + LOOK
            with act.Fori(1, FG2) as j:
                def run_ahead(i):
                    g = gq + i + LOOK
                    hi(g, landed_value(by_quarter[min(g, len(by_quarter) - 1)][0]) + 32 * (j - 1), g - 3 + 8 * (j - 1))
                ff1_steps(j, False, run_ahead)
            ahead[0] = gq + 8 * (FG2 - 1) + LOOK
            for m in range(DT):
                ensure(gq + 8 * (FG2 - 1) + m // 2 + 1 + LOOK)
                square(("post_mlp",), m, y[:, m, :],
                       (free[4 + m % 4], BK.ffn2[4 + m % 4] + 2 * (FG2 - 1) + m // 4 + 1))
            root(("post_mlp",), D)

        @block.vector
        def _(dve):
            chain = [0]

            def link(ins):
                chain[0] += 1
                ins.then_inc(dve_seq, 1)
                dve.wait_ge(dve_seq, chain[0])

            def norm_rstd(e):
                emptied(dve, ("norm", e))
                dve.reciprocal(rstd[:, 0:NT], rt[:, 0:NT]).then_inc(rstd_ready, 1)
                return filled(dve, ("rstd", e))[:, :]

            def rstd_read(e):
                b = BK["rstd", e][0]
                dve.tensor_copy(rstd[:, 2 * NT:2 * NT + 1], ps[b][:, S - 1:S]).then_inc(free[b], 1)

            def split_lo(k, src, hi_, lo_):
                dve.wait_ge(hi_ready, k + 1)
                dve.tensor_tensor(lo_, src, hi_, ALU.subtract).then_inc(lo_ready, 1)

            def norm_split(e, name, count, src, gain, at, shift=None):
                factors = norm_rstd(e) if e != ("mix2",) else filled(dve, ("rstd", e))[:, :]

                def lo_(f):
                    k = SPL[name] + f
                    split_lo(k, tb[:, k % 3, :], n_hi.bitcast(F32)[:, at + f, :], n_lo[:, at + f, :])

                for f in range(count):
                    k = SPL[name] + f
                    t = tb[:, k % 3, :]
                    if k >= 3:
                        dve.wait_ge(lo_ready, k - 2)
                    ins = dve.scalar_tensor_tensor(t, src(f), gain(f), factors, ALU.mult, ALU.mult)
                    if shift is not None:
                        link(ins)
                        ins = dve.tensor_scalar(t, t, shift(f), None, ALU.add)
                    ins.then_inc(val_ready, 1)
                    if f >= 1:
                        lo_(f - 1)
                rstd_read(e)
                lo_(count - 1)

            for f in range(DT):
                dve.tensor_copy(h[:, f, :], filled(dve, ("x", f))[:, :]).then_inc(free[f], 1)
            dve.tensor_copy(cols[:, 0, 0:NROWS0], filled(dve, "cols0")[:, 0:NROWS0]).then_inc(freed("cols0"), 1)
            emptied(dve, "cols0")

            def angles():
                dve.wait_ge(lam_in, 16 * 8)
                for i in range(2):
                    ins = dve.tensor_tensor(lamp[:, 2 * i:2 * i + 2, :], lamv[:, 4 * i:4 * i + 2, :],
                                            lamv[:, 4 * i + 2:4 * i + 4, :], ALU.mult)
                link(ins)
                dve.tensor_reduce(lamd, lamp, AX.X, ALU.add).then_inc(lam_dots, 1)
                for l in range(DEPTH):
                    dve.tensor_scalar(subg[:, l:l + 1], col("subln_gain", l), 1.0 - LAMBDA_INIT[l], None, ALU.mult)
                dve.wait_ge(pos_in, 16)
                dve.wait_ge(consts_in, 16)
                posf, ang, turn = zc[:, 512:1024], zc[:, 0:512], tb[:, 0, :]
                link(dve.tensor_copy(posf, zc[:, 0:512].bitcast(I32)))
                link(dve.tensor_scalar(ang, posf, const[:, C_INVF:C_INVF + 1], None, ALU.mult))
                for i in range(2):
                    r = zc[:, 1024 + 512 * i:1536 + 512 * i]
                    link(dve.tensor_scalar(turn, ang, 1.0 / TWO_PI[0], 0.25 * i, ALU.mult, ALU.add))
                    link(dve.tensor_scalar(turn, turn, ROUND, None, ALU.add))
                    link(dve.tensor_scalar(turn, turn, ROUND, None, ALU.subtract))
                    for j, part in enumerate(TWO_PI[1:]):
                        link(dve.scalar_tensor_tensor(r, turn, -part, ang if j == 0 else r, ALU.mult, ALU.add))
                    link(dve.tensor_scalar(r, r, 0.5 * float(np.pi) * i, PI_BELOW, ALU.add, ALU.min))
                    ins = dve.tensor_scalar(r, r, -PI_BELOW, None, ALU.max)
                ins.then_inc(ang_ready, 1)

            def parameters():
                b = filled(dve, "cols1")
                for i in range(4):
                    last = dve.tensor_copy(cols[:, 1 + i, 0:NROWS[1 + i]], b[:, i * P:i * P + NROWS[1 + i]])
                last.then_inc(freed("cols1"), 1)
                dve.tensor_copy(cols[:, 5, 0:NROWS[5]], filled(dve, "cols2")[:, 0:NROWS[5]]).then_inc(freed("cols2"), 1)
                for l in range(DEPTH):
                    dve.tensor_copy(wsT[:, 4 * l:4 * l + 4, :].rearrange("p m q -> p (m q)"),
                                    filled(dve, ("wsT", l))[:, :]).then_inc(freed(("wsT", l)), 1)
                emptied(dve, "cols1")
                emptied(dve, "cols2")
                for l in range(DEPTH):
                    pv_ = par[:, l, :].rearrange("p (g j h c) -> p g j h c", g=FG, j=2, h=2)
                    for c in range(4):
                        src = cols[:, 2 + 2 * l + c // 2, FT * (c % 2):FT * (c % 2) + FT]\
                            .rearrange("p (h g j) -> p g j h", h=2, g=FG)
                        for half in range(2):
                            last = dve.tensor_copy(pv_[:, :, :, half, c], src[:, :, :, half])
                last.then_inc(par_ready, 1)
                dve.wait_ge(lam_exp, 1)
                link(dve.tensor_tensor(lamneg, lame[:, 2:4], lame[:, 0:2], ALU.subtract))
                for l in range(DEPTH):
                    last = dve.tensor_scalar(lamneg[:, l:l + 1], lamneg[:, l:l + 1], -LAMBDA_INIT[l], None, ALU.add)
                link(last)
                dve.wait_ge(sp_abs, 1)
                e_, s1, s2, p_, z_ = (spt[:, 4 * i:4 * i + 4] for i in (1, 2, 3, 4, 0))
                link(dve.tensor_scalar(s1, e_, 2.0, None, ALU.add))
                link(dve.reciprocal(s1, s1))
                link(dve.tensor_tensor(s1, s1, e_, ALU.mult))
                link(dve.tensor_tensor(s2, s1, s1, ALU.mult))
                link(dve.tensor_scalar(p_, s2, 1.0 / 15, None, ALU.mult))
                for k in (13, 11, 9, 7, 5, 3):
                    link(dve.scalar_tensor_tensor(p_, p_, 1.0 / k, s2, ALU.add, ALU.mult))
                link(dve.scalar_tensor_tensor(p_, p_, 1.0, s1, ALU.add, ALU.mult))
                link(dve.tensor_scalar(z_, col("lru_lambda_2", 0, HT), -1.0, 0.0, ALU.mult, ALU.max))
                link(dve.scalar_tensor_tensor(p_, p_, 2.0, z_, ALU.mult, ALU.add))
                dve.tensor_scalar(spt[:, 20:24], p_, -LRU_C, None, ALU.mult)
                dve.tensor_scalar(spt[:, 24:28], p_, LRU_C, None, ALU.mult).then_inc(sp_ready, 1)

            def modulation(l):
                c = slice(l * ADA_T // 2, (l + 1) * ADA_T // 2)
                dve.tensor_tensor(mod[:, c], filled(dve, ("ada", l))[:, 0:ADA_T // 2], cols[:, 1, c], ALU.add)\
                    .then_inc(freed(("ada", l)), 1)
                emptied(dve, ("ada", l))

            for l in range(DEPTH):
                if l == 0:
                    for f in range(DT):
                        emptied(dve, ("x", f))
                else:
                    for f in range(4, DT):
                        dve.wait_ge(*ffn_h(l - 1, f))
                norm_split(("attn", l), ("attn", l), DT, lambda f: h[:, f, :], lambda f: col("attn_norm", l * DT + f), 0)
                if l == 0:
                    angles()
                else:
                    modulation(0)
                for t in range(NT):
                    emptied(dve, ("vs", l, t))
                    link(dve.tensor_tensor(tb[:, t % 3, :], vg[:, t, :], vg[:, t, :], ALU.mult))
                    dve.tensor_reduce(vss[:, 4 * t:4 * t + 4], tiles(tb[:, t % 3, :]), AX.X, ALU.add)\
                        .then_inc(vss_ready, 1)
                    dve.wait_ge(vss_ready, 4 * l + t + 1)
                dve.wait_ge(vroot_ready, l + 1)
                link(dve.reciprocal(vss, vss))
                for t in range(NT):
                    last = dve.tensor_tensor(tiles(vg[:, t, :]), tiles(vg[:, t, :]),
                                             vss[:, 4 * t:4 * t + 4].unsqueeze(2).to_broadcast([P, 4, P]), ALU.mult)
                last.then_inc(vn_ready, 1)
                if l == 0:
                    parameters()
                dve.wait_ge(rope_ready, 2)
                for j, name in enumerate(("q", "k")):
                    for t in range(4):
                        x_ = (qT, kT)[j][:, t, :]
                        n = 8 * l + 4 * j + t
                        if n >= 3:
                            dve.wait_ge(qk_ready, n - 2)
                        dve.tensor_tensor(tb[:, n % 3, :], filled(dve, ("rope", name, l, t))[:, :], sinT, ALU.mult)\
                            .then_inc(freed(("rope", name, l, t)), 1)
                        emptied(dve, (name, l, t))
                        link(dve.tensor_tensor(x_, x_, cosT, ALU.mult))
                        emptied(dve, ("rope", name, l, t))
                        dve.tensor_tensor(x_, x_, tb[:, n % 3, :], ALU.add).then_inc(qk_ready, 1)
                dve.wait_ge(sgub_in, 16)
                dve.wait_ge(qk_ready, 8 * l + 8)

                def sgu_lo(g):
                    k = SPL["sgu", l] + g
                    split_lo(k, tb[:, k % 3, :], n_hi.bitcast(F32)[:, g, :], n_lo[:, g, :])

                for g in range(HT):
                    t = tb[:, (SPL["sgu", l] + g) % 3, :]
                    dve.scalar_tensor_tensor(tiles(t), tiles(filled(dve, ("mix", l, g))[:, :]),
                                             col("sgu_v_norm", l * HT + g),
                                             sgub[:, 4 * l + g, :].unsqueeze(1).to_broadcast([P, NT, P]),
                                             ALU.mult, ALU.add).then_inc(freed(("mix", l, g)), 1)
                    emptied(dve, ("mix", l, g))
                    emptied(dve, ("u", l, g))
                    dve.tensor_tensor(t, t, u[:, g, :], ALU.mult).then_inc(val_ready, 1)
                    if g >= 1:
                        sgu_lo(g - 1)
                sgu_lo(HT - 1)
                for n in range(ATT_STEPS):
                    if n < 16:
                        i = n % 4
                        w = (i + 1) * P
                        if l * 16 + n >= 2:
                            dve.wait_ge(max_ready, l * 16 + n - 1)
                            dve.wait_ge(probs_ready, l * 16 + n - 1)
                        for m in range(2):
                            c = 2 * (n % 2) + m
                            dve.tensor_tensor_reduce(scores[n % 2][:, m, 0:w], filled(dve, ("S", l, n, m))[:, 0:w],
                                                     causal[:, S - w:S], 1.0, LOWEST, ALU.add, ALU.max,
                                                     mxs[:, c:c + 1]).then_inc(freed(("S", l, n, m)), 1)
                        emptied(dve, ("S", l, n, 0))
                        emptied(dve, ("S", l, n, 1))
                        c = 2 * (n % 2)
                        dve.tensor_scalar(nmx[:, c:c + 2], mxs[:, c:c + 2], -1.0, None, ALU.mult)\
                            .then_inc(max_ready, 1)
                    v = n - 1
                    if 0 <= v < 16:
                        w = (v % 4 + 1) * P
                        c = 2 * (v % 2)
                        uv = l * 16 + v
                        dve.wait_ge(exp_ready, 2 * uv + 2)
                        link(dve.reciprocal(rec[:, c:c + 2], lsum[:, c:c + 2]))
                        dve.tensor_tensor(rec[:, c + 1:c + 2], rec[:, c + 1:c + 2], lamneg[:, l:l + 1], ALU.mult)
                        sc = scores[v % 2]
                        if v >= 2:
                            filled(dve, ("T", l, v - 2))
                        link(dve.tensor_scalar(probs[v % 2][:, 0:w], sc[:, 0, 0:w], rec[:, c:c + 1], None, ALU.mult))
                        dve.scalar_tensor_tensor(probs[v % 2][:, 0:w], sc[:, 1, 0:w], rec[:, c + 1:c + 2],
                                                 probs[v % 2][:, 0:w], ALU.mult, ALU.add).then_inc(probs_ready, 1)
                    if n >= 6 and (n - 6) % 4 == 0:
                        hd = (n - 6) // 4
                        if hd < HEADS:
                            dve.wait_ge(pv_done, l * 16 + 4 * hd + 4)
                            dve.tensor_copy(tb[:, 2, :], ps[6][:, :]).then_inc(freed(("O", l, hd)), 1)
                            emptied(dve, ("O", l, hd))
                    if n >= 7 and (n - 7) % 4 == 0:
                        hd = (n - 7) // 4
                        k = SPL["sub", l] + hd
                        factors = norm_rstd(("sub", l, hd))
                        dve.scalar_tensor_tensor(tb[:, k % 2, :], tb[:, 2, :], subg[:, l:l + 1], factors,
                                                 ALU.mult, ALU.mult).then_inc(val_ready, 1)
                        rstd_read(("sub", l, hd))
                        split_lo(k, tb[:, k % 2, :], n_hi.bitcast(F32)[:, HT + hd, :], n_lo[:, HT + hd, :])
                for m in range(DT):
                    dve.tensor_tensor(h[:, m, :], h[:, m, :], filled(dve, ("out", l, m))[:, :], ALU.add)\
                        .then_inc(freed(("out", l, m)), 1)
                for m in range(4, DT):
                    emptied(dve, ("out", l, m))
                norm_split(("ffn", l), ("ffn", l), DT, lambda f: h[:, f, :], lambda f: col("ffn_norm", l * DT + f), 0)

                n0 = BK.ffn[l]
                gq = STR["up", l, 1].g0

                def conv_steps(j):
                    dve.tensor_copy(cpar[:, 0:16], par[:, l, bass.ds(j * 16, 16)]).then_inc(par_ready, 1)
                    dve.wait_ge(par_ready, 1 + l * FG + j + 1)
                    for i in range(2):
                        for t in (2 * i, 2 * i + 1):
                            cv = (l * FG + j) * 4 + t + 1
                            dve.wait_ge(conv_begun, cv)
                            dve.scalar_tensor_tensor(rb[t][:, 1:S], ps[t][:, 0:S - 1], cpar[:, 4 * t + 1:4 * t + 2],
                                                     rb[t][:, 1:S], ALU.mult, ALU.add).then_inc(conv_tap, 1)
                            dve.wait_ge(conv_tap, cv)
                            dve.scalar_tensor_tensor(rb[t][:, 2:S], ps[t][:, 0:S - 2], cpar[:, 4 * t:4 * t + 1],
                                                     rb[t][:, 2:S], ALU.mult, ALU.add).then_inc(free[t], 1)
                        dve.wait_ge(free[2 * i + 1], n0[2 * i + 1] + j + 1)
                        dve.wait_ge(silu_done, (l * FG + j) * 2 + i + 1)
                        dve.tensor_tensor(rb[2 * i], rb[2 * i], rb[2 * i + 1], ALU.mult).then_inc(val_ready, 1)

                def down_steps(quarter):
                    for m in range(DT):
                        dve.wait_ge(quarter_done, quarter + m // 2 + 1)
                        dve.tensor_tensor(h[:, m, :], h[:, m, :], ps[4 + m % 4][:, :], ALU.add)\
                            .then_inc(free[4 + m % 4], 1)

                def hidden_lo(j):
                    for i in range(2):
                        split_lo(SPL["act", l] + 2 * j + i, rb[2 * i], x_hi.bitcast(F32)[:, i, :], x_lo[:, i, :])

                def ada_step(k):
                    dve.wait_ge(ada_in, 16 * (DT * l + 1) + 16 * k)
                    if isinstance(k, int):
                        dve.wait_ge(c_ready, 1)
                        ins = dve.tensor_scalar(ada_sum, ada_w, csilu[:, k:k + 1], None, ALU.mult)
                    else:
                        dve.wait_ge(ada_used, DT * l + k)
                        ins = dve.scalar_tensor_tensor(ada_sum, ada_w, cpar[:, 16:17], ada_sum, ALU.mult, ALU.add)
                    ins.then_inc(ada_used, 1)

                conv_steps(0)
                hidden_lo(0)
                ada_step(0)
                for first, end in ((1, DT), (DT, FG)):
                    with dve.Fori(first, end) as j:
                        if first == 1:
                            dve.wait_ge(ada_used, DT * l + j)
                            dve.tensor_copy(cpar[:, 16:17], csilu[:, bass.ds(j, 1)])
                        conv_steps(j)
                        down_steps(gq + 4 + 8 * (j - 1))
                        hidden_lo(j)
                        if first == 1:
                            ada_step(j)
                down_steps(gq + 8 * (FG - 1))

            for f in range(4, DT):
                dve.wait_ge(*ffn_h(DEPTH - 1, f))
            modulation(1)
            for dst, name, part in ((gs1, "pre_norm_mix_2", 1), (pg1, "post_norm_mix_2", 2),
                                    (gs2, "pre_norm_mlp_2", 4), (pg2, "post_norm_mlp_2", 5)):
                last = dve.scalar_tensor_tensor(dst, mod[:, 8 * part:8 * part + 8], 1.0, col(name, 0, DT),
                                                ALU.add, ALU.mult)
            link(last)
            link(dve.tensor_tensor(gs1, gs1, col("final_norm", 0, DT), ALU.mult))
            sums = ps[BK["norm", ("final",)][0]]
            dve.wait_ge(sq_used, NRM["final",][1] + 2 * DT)
            dve.tensor_scalar(ms[:, 0:NT], sums[:, 0:NT], 1.0 / D, EPS, ALU.mult, ALU.add)
            dve.tensor_scalar(ms[:, NT:2 * NT], sums[:, NT:2 * NT], 1.0 / D, None, ALU.mult)\
                .then_inc(freed(("norm", ("final",))), 1)
            emptied(dve, ("norm", ("final",)))
            dve.scalar_tensor_tensor(ms[:, NT:2 * NT], ms[:, 0:NT], EPS, ms[:, NT:2 * NT], ALU.mult, ALU.add)\
                .then_inc(means_ready, 1)
            dve.wait_ge(act_seq, 2)
            dve.reciprocal(rstd[:, 0:2 * NT], rt[:, :]).then_inc(rstd_ready, 1)
            norm_split(("mix2",), ("mix2",), DT, lambda f: h[:, f, :], lambda f: gs1[:, f:f + 1], 0,
                       lambda f: mod[:, f:f + 1])
            factors = filled(dve, ("rstd", ("final",)))
            for f in range(DT):
                dve.scalar_tensor_tensor(h[:, f, :], h[:, f, :], col("final_norm", f), factors[:, :],
                                         ALU.mult, ALU.mult).then_inc(h_set, 1)
            emptied(dve, ("rstd", ("mix2",)))
            rstd_read(("final",))
            for t in range(HT):
                dve.wait_ge(xr_begun, t + 1)
                b = filled(dve, ("x_rnn", t))
                for back in (1, 2, 3):
                    ins = dve.scalar_tensor_tensor(xc[:, t, back:S], b[:, 0:S - back],
                                                   col("conv_w_2", (3 - back) * HT + t), xc[:, t, back:S],
                                                   ALU.mult, ALU.add)
                    if back < 3:
                        link(ins)
                ins.then_inc(freed(("x_rnn", t)), 1)
            emptied(dve, ("gates",))
            dve.tensor_scalar(gates[:, 0, 0:HEADS2], gates[:, 0, 0:HEADS2], const[:, C_SEEN:C_SEEN + 1], None,
                              ALU.mult).then_inc(gate_set, 1)
            for t in range(HT):
                dve.wait_ge(decay_ready, t + 1)
                link(dve.tensor_scalar(rn[5], rn[3], 1.0, None, ALU.add))
                link(dve.reciprocal(rn[5], rn[5]))
                dve.tensor_tensor(rn[4], rn[3], rn[5], ALU.mult).then_inc(ratio_ready, 1)
                emptied(dve, ("rx", t))
                emptied(dve, ("x_rnn", t))
                link(dve.tensor_tensor(rn[6], rn[1], xc[:, t, :], ALU.mult))
                dve.wait_ge(rootm_ready, t + 1)
                link(dve.tensor_tensor(rn[6], rn[6], rn[4], ALU.mult))
                link(dve.tensor_tensor_scan(rn[7], rn[2], rn[6], 0.0, ALU.mult, ALU.add))
                dve.tensor_tensor(gr[:, t, :], gr[:, t, :], rn[7], ALU.mult).then_inc(rnn_ready, 1)
            dve.wait_ge(rnn_ready, HT)
            norm_split(("rnn",), ("rnn",), HT, lambda f: gr[:, f, :], lambda f: col("norm_rnn_out_2", f), 0)
            for j in range(2):
                emptied(dve, ("kvs", j))
                v = kk[j].rearrange("p g (c j r) -> p j g c r", j=8, r=2)
                for half in range(2):
                    dve.tensor_copy(cval[j][:, 8 * half:8 * half + 8, 0:62].rearrange("p j (g c) -> p j g c", g=2),
                                    v[:, :, :, half:half + NCMP, 0])
                dve.memset(cval[j][:, :, 63:64], 0.0)
                c = POS_ROW + 16 * j
                dve.tensor_copy(cval[j][:, :, 62], cols[:, 1, c:c + 16]).then_inc(val_ready, 1)
                dve.wait_ge(val_ready, SPL["cmp",] + j + 1)
                split_lo(SPL["cmp",] + j, cval[j], cb_hi.bitcast(F32)[:, :, :], cb_lo[:, :, :])
            dve.wait_ge(gate_set, 1)
            for n in range(NU + 4):
                if n < NU:
                    hd, br, i = UNITS[n]
                    b = filled(dve, ("S2", n))
                    if n >= 4:
                        filled(dve, ("T2", n - 4))
                        dve.wait_ge(max_ready, 32 + n - 3)
                        dve.wait_ge(probs_ready, 32 + n - 3)
                    sc = scores2[n % 4]
                    if br == "c":
                        dve.wait_ge(bias_ready, hd + 1)
                        dve.tensor_tensor(sc[:, 0:124], b[:, 0:124], bias_c[hd % 2], ALU.add)\
                            .then_inc(freed(("S2", n)), 1)
                        emptied(dve, ("S2", n))
                        link(dve.tensor_reduce(cmx, tiles(sc[:, 0:124]), AX.X, ALU.max))
                        dve.tensor_tensor(tiles(sc[:, 0:124]), tiles(sc[:, 0:124]),
                                          cmx.unsqueeze(2).to_broadcast([P, NT, NCMP]), ALU.subtract)\
                            .then_inc(max_ready, 1)
                    else:
                        w = (i + 1) * P
                        dve.tensor_tensor_reduce(sc[:, 0:w], b[:, 0:w], bias_h[hd % 2][:, S - w:S], 1.0, LOWEST,
                                                 ALU.add, ALU.max, mxs[:, n % 4:n % 4 + 1]).then_inc(freed(("S2", n)), 1)
                        emptied(dve, ("S2", n))
                        dve.tensor_scalar(nmx[:, n % 4:n % 4 + 1], mxs[:, n % 4:n % 4 + 1], -1.0, None, ALU.mult)\
                            .then_inc(max_ready, 1)
                v = n - 1
                if 0 <= v < NU:
                    hd, br, i = UNITS[v]
                    sc = scores2[v % 4]
                    dve.wait_ge(exp_ready, 64 + v + 1)
                    if br == "c":
                        link(dve.tensor_reduce(csum, tiles(sc[:, 0:124]), AX.X, ALU.add))
                        link(dve.reciprocal(csum, csum))
                        link(dve.tensor_tensor(csum, csum, gates[:, :, hd], ALU.mult))
                        dve.tensor_tensor(tiles(sc[:, 0:124]), tiles(sc[:, 0:124]),
                                          csum.unsqueeze(2).to_broadcast([P, NT, NCMP]), ALU.mult)\
                            .then_inc(probs_ready, 1)
                    else:
                        g = (8 if br == "s" else 16) + hd
                        w = (i + 1) * P
                        link(dve.reciprocal(rec[:, v % 4:v % 4 + 1], lsum[:, v % 4:v % 4 + 1]))
                        dve.tensor_scalar(sc[:, 0:w], sc[:, 0:w], rec[:, v % 4:v % 4 + 1], gates[:, i, g:g + 1],
                                          ALU.mult, ALU.mult).then_inc(probs_ready, 1)
                v = n - 3
                if 0 <= v < NU and v % 18 == 17:
                    hp = v // 18
                    dve.wait_ge(pv_done, 32 + PV_BEFORE[v + 1])
                    dve.tensor_copy(oT[:, hp, :], ps[5 + hp % 2][:, :]).then_inc(freed(("O2", hp)), 1)
                    emptied(dve, ("O2", hp))
            norm_split(("att",), ("att",), HT, lambda f: oT[:, f, :], lambda f: col("norm_att_out_2", f), HT)
            for m in range(DT):
                dve.tensor_copy(y[:, m, :], filled(dve, ("out2", m))[:, :]).then_inc(freed(("out2", m)), 1)
            for m in range(4, DT):
                emptied(dve, ("out2", m))

            def add_normed(e, gain):
                factors = norm_rstd(e)
                for f in range(DT):
                    link(dve.scalar_tensor_tensor(y[:, f, :], y[:, f, :], gain[:, f:f + 1], factors,
                                                  ALU.mult, ALU.mult))
                    dve.tensor_tensor(h[:, f, :], h[:, f, :], y[:, f, :], ALU.add).then_inc(h_set, 1)
                rstd_read(e)

            add_normed(("post_mix",), pg1)
            dve.wait_ge(h_set, 2 * DT)
            dve.memset(zy[:, :], 0.0).then_inc(y_zero, 1)
            norm_split(("mlp",), ("mlp",), DT, lambda f: h[:, f, :], lambda f: gs2[:, f:f + 1], 0,
                       lambda f: mod[:, 24 + f:25 + f])
            dve.wait_ge(y_zero, 1)
            n0 = BK.ffn2
            gq = STR["ff1", 1].g0

            def square_steps(j):
                for t in range(4):
                    dve.wait_ge(free[t], n0[t] + j + 1)
                    dve.tensor_tensor(rb[t], rb[t], rb[t], ALU.mult).then_inc(val_ready, 1)

            def ff2_steps(quarter):
                for m in range(DT):
                    dve.wait_ge(quarter_done, quarter + m // 2 + 1)
                    dve.tensor_tensor(y[:, m, :], y[:, m, :], ps[4 + m % 4][:, :], ALU.add)\
                        .then_inc(free[4 + m % 4], 1)

            def hidden2_lo(j):
                for t in range(4):
                    split_lo(SPL["act2",] + 4 * j + t, rb[t], x_hi.bitcast(F32)[:, t, :], x_lo[:, t, :])

            square_steps(0)
            dve.wait_ge(val_ready, SPL["act2",] + 4)
            hidden2_lo(0)
            with dve.Fori(1, FG2) as j:
                square_steps(j)
                ff2_steps(gq + 4 + 8 * (j - 1))
                hidden2_lo(j)
            ff2_steps(gq + 8 * (FG2 - 1))
            for f in range(4, DT):
                dve.wait_ge(free[4 + f % 4], n0[4 + f % 4] + 2 * FG2)
            add_normed(("post_mlp",), pg2)
            for t in range(NT):
                for j in range(2):
                    dve.tensor_copy(zb[:, t * D + j * S:t * D + (j + 1) * S], filled(dve, ("y", t, j))[:, :])\
                        .then_inc(freed(("y", t, j)), 1)

        @block.tensor
        def _(pe):
            def bank(key):
                b, n = BK[key][:2]
                if n:
                    pe.wait_ge(free[b], n)
                return ps[b]

            def quarter(g):
                pe.wait_ge(whi_ready, g + 1)
                pe.wait_ge(wlo_ready, g + 1)
                return w_hi[:, g % 4, :], w_lo[:, g % 4, :]

            def product(out, l_hi, l_lo, r_hi, r_lo, start, stop):
                pe.matmul(out, l_hi, r_hi, start=start, stop=False)
                pe.matmul(out, l_hi, r_lo, start=False, stop=False)
                return pe.matmul(out, l_lo, r_hi, start=False, stop=stop)

            def norm_tile(e, i):
                n, first, end = NRM[e][1] + i, i == 0, i == NRM[e][2] - 1
                if i == 0:
                    bank(("norm", e))
                b = ps[BK["norm", e][0]]
                c0 = NT * (i % 2) if e == ("final",) else 0
                pe.wait_ge(sq_ready, n + 1)
                for t in range(NT):
                    last = pe.matmul(b[:, c0 + t:c0 + t + 1], sq[:, n % 2, t * P:(t + 1) * P], ones[:, 0:1],
                                     start=(first and t == 0), stop=(end and t == NT - 1))
                last.then_inc(sq_used, 1)

            def spread(e, c0=0, num=None):
                pe.wait_ge(rstd_ready, (NRM[e][0] if num is None else num) + 1)
                out = bank(("rstd", e))
                for t in range(NT):
                    last = pe.matmul(out[:, t * P:(t + 1) * P], rstd[:, c0 + t:c0 + t + 1].to_broadcast([P, P]),
                                     ident, start=True, stop=True)
                last.then_inc(full[BK["rstd", e][0]], 1)

            def norm_sum(e):
                for i in range(NRM[e][2]):
                    norm_tile(e, i)
                spread(e)

            def features(keys, g0, split=None, beside=None):
                first = 0
                if split is not None:
                    first = 2
                    parts = [quarter(g0), quarter(g0 + 1)]
                    outs = [bank(keys[0]), bank(keys[1])]
                    for k in range(DT):
                        pe.wait_ge(lo_ready, split + k + 1)
                        for t in range(2):
                            wh, wl = parts[t]
                            last = product(outs[t][:, :], wh[:, k * P:(k + 1) * P], wl[:, k * P:(k + 1) * P],
                                           n_hi[:, k, :], n_lo[:, k, :], k == 0, k == DT - 1)
                            if k == DT - 1:
                                last.then_inc(quarter_done, 1)
                for t in range(first, len(keys)):
                    wh, wl = quarter(g0 + t)
                    out = bank(keys[t])
                    for k in range(DT):
                        last = product(out[:, :], wh[:, k * P:(k + 1) * P], wl[:, k * P:(k + 1) * P],
                                       n_hi[:, k, :], n_lo[:, k, :], k == 0, k == DT - 1)
                    last.then_inc(quarter_done, 1)
                    if beside is not None:
                        beside(t)

            def tokens(keys, g0):
                outs = [bank(key) for key in keys]
                for q in range(4):
                    wh, wl = quarter(g0 + q)
                    for t in range(NT):
                        for k in (2 * q, 2 * q + 1):
                            c = (k % 2) * S
                            last = product(outs[t][:, :], n_hi[:, k, t * P:(t + 1) * P], n_lo[:, k, t * P:(t + 1) * P],
                                           wh[:, c:c + S], wl[:, c:c + S], k == 0, k == DT - 1)
                    last.then_inc(quarter_done, 1)

            def tokens_narrow(key, g, width):
                wh, wl = quarter(g)
                out = bank(key)
                for t in range(NT):
                    for k in range(DT):
                        last = product(out[:, t * width:(t + 1) * width], n_hi[:, k, t * P:(t + 1) * P],
                                       n_lo[:, k, t * P:(t + 1) * P], wh[:, k * width:(k + 1) * width],
                                       wl[:, k * width:(k + 1) * width], k == 0, k == DT - 1)
                last.then_inc(quarter_done, 1)

            pe.wait_ge(consts_in, 16)
            pe.wait_ge(x_in, 16)
            for f in range(DT):
                out = bank(("x", f))
                for t in range(NT):
                    last = pe.transpose(out[:, t * P:(t + 1) * P], xin[:, t, f * P:(f + 1) * P], ident)
                last.then_inc(full[f], 1)
            pe.wait_ge(gains_in, 16 * len(ROWS0))
            pe.transpose(bank("cols0")[:, 0:NROWS0], rows[0][0:NROWS0, :], ident[0:NROWS0, 0:NROWS0])\
                .then_inc(full[BK["cols0"][0]], 1)
            pe.wait_ge(ones_set, 3)

            def turn_parameters():
                pe.wait_ge(rows_in, 16 * (4 + 4 * DEPTH))
                for i in range(1, 6):
                    key = "cols1" if i < 5 else "cols2"
                    if i in (1, 5):
                        bank(key)
                    b = BK[key][0]
                    c = (i - 1) % 4 * P
                    last = pe.transpose(ps[b][:, c:c + NROWS[i]], rows[i][0:NROWS[i], :],
                                        ident[0:NROWS[i], 0:NROWS[i]])
                    if i in (4, 5):
                        last.then_inc(full[b], 1)
                pe.wait_ge(sgu_masked, 1)
                for l in range(DEPTH):
                    out = bank(("wsT", l))
                    for g in range(4):
                        last = pe.transpose(out[:, g * P:(g + 1) * P], sguw[:, 4 * l + g, :], ident)
                    last.then_inc(full[BK["wsT", l][0]], 1)

            norm_sum(("attn", 0))
            for l in range(DEPTH):
                features([("u", l, t) for t in range(4)], STR["u", l].g0, SPL["attn", l])
                tokens([("vs", l, t) for t in range(NT)], STR["vs", l].g0)
                if l == 0:
                    turn_parameters()
                for j, name in enumerate(("q", "k")):
                    features([(name, l, t) for t in range(4)], STR[name, l].g0)
                    if j == 1:
                        tokens([("va", l, t) for t in range(NT)], STR["va", l].g0)
                    for t in range(4):
                        emptied(pe, (name, l, t))
                        out = bank(("rope", name, l, t))
                        pe.matmul(out[:, :], rotT, (qT, kT)[j][:, t, :], start=True, stop=True)\
                            .then_inc(full[BK["rope", name, l, t][0]], 1)
                pe.wait_ge(vn_ready, l + 1)
                for g in range(HT):
                    out = bank(("mix", l, g))
                    for c in range(NT):
                        last = pe.matmul(out[:, c * P:(c + 1) * P], vg[:, c, g * P:(g + 1) * P], wsT[:, 4 * l + g, :],
                                         start=True, stop=True)
                    last.then_inc(full[BK["mix", l, g][0]], 1)
                pe.wait_ge(qk_ready, l * 8 + 8)
                for t in range(NT):
                    emptied(pe, ("va", l, t))
                for n in range(ATT_STEPS):
                    if n < 16:
                        hd, i = n // 4, n % 4
                        for m in range(2):
                            out = bank(("S", l, n, m))
                            r = slice(64 * m, 64 * m + 64)
                            pe.matmul(out[:, 0:(i + 1) * P], qT[r, hd, i * P:(i + 1) * P], kT[r, hd, 0:(i + 1) * P],
                                      start=True, stop=True).then_inc(full[BK["S", l, n, m][0]], 1)
                    v = n - 2
                    if 0 <= v < 16:
                        pe.wait_ge(probs_ready, l * 16 + v + 1)
                        out = bank(("T", l, v))
                        for kt in range(v % 4 + 1):
                            last = pe.transpose(out[:, kt * P:(kt + 1) * P], probs[v % 2][:, kt * P:(kt + 1) * P], ident)
                        last.then_inc(full[BK["T", l, v][0]], 1)
                    v = n - 3
                    if 0 <= v < 16:
                        hd, i = v // 4, v % 4
                        if i == 0:
                            bank(("O", l, hd))
                        emptied(pe, ("T", l, v))
                        for kt in range(i + 1):
                            last = pe.matmul(ps[6][:, i * P:(i + 1) * P], va[:, kt, hd * P:(hd + 1) * P],
                                             pT[v % 2][:, kt * P:(kt + 1) * P], start=(kt == 0), stop=(kt == i))
                        last.then_inc(pv_done, 1)
                    if n >= 7 and (n - 7) % 4 == 0:
                        norm_sum(("sub", l, (n - 7) // 4))
                pe.wait_ge(lo_ready, SPL["sub", l] + HEADS)
                features([("out", l, m) for m in range(DT)], STR["out", l, 0].g0,
                         beside=lambda t: norm_tile(("ffn", l), t - 1) if t else None)
                norm_tile(("ffn", l), DT - 1)
                spread(("ffn", l))
                n0 = BK.ffn[l]

                def up(g, j, split=None):
                    turn = 0 if isinstance(j, int) else 8 * (j - 1)

                    def ready(t):
                        pe.wait_ge(whi_ready, g + t + 1 + turn)
                        pe.wait_ge(wlo_ready, g + t + 1 + turn)
                        pe.wait_ge(free[t], n0[t] + j)

                    def one(t, k):
                        wh, wl = w_hi[:, (g + t) % 4, :], w_lo[:, (g + t) % 4, :]
                        last = product(ps[t][:, :], wh[:, k * P:(k + 1) * P], wl[:, k * P:(k + 1) * P],
                                       n_hi[:, k, :], n_lo[:, k, :], k == 0, k == DT - 1)
                        if k == DT - 1:
                            last.then_inc(quarter_done, 1)

                    if split is not None:
                        ready(0)
                        ready(1)
                        for k in range(DT):
                            pe.wait_ge(lo_ready, split + k + 1)
                            one(0, k)
                            one(1, k)
                    for t in range(0 if split is None else 2, 4):
                        ready(t)
                        for k in range(DT):
                            one(t, k)

                def down(g, j, turn, kn, split, beside=None):
                    pe.wait_ge(lo_ready, split + kn * j + kn)
                    for q in range(4):
                        pe.wait_ge(whi_ready, g + q + 1 + turn)
                        pe.wait_ge(wlo_ready, g + q + 1 + turn)
                        wh, wl = w_hi[:, (g + q) % 4, :], w_lo[:, (g + q) % 4, :]
                        for m in (2 * q, 2 * q + 1):
                            pe.wait_ge(free[4 + m % 4], n0[4 + m % 4] + 2 * j + m // 4)
                            for k in range(kn):
                                c = k * 256 + (m % 2) * P
                                last = product(ps[4 + m % 4][:, :], wh[:, c:c + P], wl[:, c:c + P],
                                               x_hi[:, k, :], x_lo[:, k, :], k == 0, k == kn - 1)
                        last.then_inc(quarter_done, 1)
                        if beside is not None and q:
                            beside(q - 1)

                gq = STR["up", l, 1].g0
                up(STR["up", l, 0].g0, 0, SPL["ffn", l])
                with pe.Fori(1, FG) as j:
                    up(gq, j)
                    down(gq + 4, j - 1, 8 * (j - 1), 2, SPL["act", l])
                after = ("attn", 1) if l == 0 else ("final",)

                def sums(q):
                    for i in range(NRM[after][2] // 4):
                        norm_tile(after, q * NRM[after][2] // 4 + i)

                down(gq + 8 * (FG - 1), FG - 1, 0, 2, SPL["act", l], sums)
                pe.wait_ge(ada_used, DT * (l + 1))
                out = bank(("ada", l))
                for t in range(ADA_T // 2):
                    last = pe.matmul(out[:, t:t + 1], ada_sum[:, t * P:(t + 1) * P], ones[:, 0:1], start=True,
                                     stop=True)
                last.then_inc(full[BK["ada", l][0]], 1)
                sums(3)
                if l == 0:
                    spread(after)

            spread(("mix2",), NT, NRM["final",][0])
            spread(("final",))
            for name in ("g_rnn", "x_rnn", "q2"):
                features([(name, t) for t in range(4)], STR[name,].g0, SPL["mix2",] if name == "g_rnn" else None)
            features([("kvs", t) for t in range(3)], STR["kvs",].g0)
            tokens_narrow(("vsel",), STR["kvs",].g0 + 3, P)
            features([("kw",)], STR["kw",].g0)
            tokens_narrow(("vwin",), STR["kw",].g0 + 1, P)
            tokens_narrow(("gates",), STR["kw",].g0 + 2, 24)
            pe.wait_ge(blk_in, 16 * 4)
            for t in range(HT):
                emptied(pe, ("x_rnn", t))
                for j, key in enumerate((("ra", t), ("rx", t))):
                    out = bank(key)
                    pe.matmul(out[:, :], blkw[:, j, t, :], xc[:, t, :], start=True, stop=True)\
                        .then_inc(full[BK[key][0]], 1)
            norm_sum(("rnn",))
            pe.wait_ge(cw2_in, 16 * 4)
            for j in range(2):
                pe.wait_ge(lo_ready, SPL["cmp",] + j + 1)
                outs = [bank(("chid", j, m)) for m in range(2)]
                g0 = STR["cmp", j].g0
                for q in range(4):
                    wh, wl = quarter(g0 + q)
                    for i in range(4):
                        k = 4 * q + i
                        for m in range(2):
                            c = i * 256 + m * P
                            last = product(outs[m][:, 0:64], wh[:, c:c + P], wl[:, c:c + P],
                                           cb_hi[:, k, :], cb_lo[:, k, :], k == 0, k == 15)
                    last.then_inc(quarter_done, 1)
                for m in range(2):
                    emptied(pe, ("chid", j, m))
                out = bank(("cout", j))
                for g in range(1 if j == 0 else 2):
                    for m in range(2):
                        if j == 0:
                            last = pe.matmul(out[:, 0:62], cw2[0][:, m, :], ghid[:, m, 0:62],
                                             start=(m == 0), stop=(m == 1))
                        else:
                            last = pe.matmul(out[0:NCMP, 64 * g:64 * g + 64], ghid[:, m, g * NCMP:(g + 1) * NCMP],
                                             cw2[1][:, m, 0:64], start=(m == 0), stop=(m == 1))
                last.then_inc(full[BK["cout", j][0]], 1)
            for key in (("kvs", 2), ("vsel",), ("kw",), ("vwin",), ("cout", 0), ("cout", 1)) \
                    + tuple(("q2", t) for t in range(4)):
                emptied(pe, key)
            for n in range(NU + 4):
                if n < NU:
                    hd, br, i = UNITS[n]
                    r = slice(64 * (hd % 2), 64 * (hd % 2) + 64)
                    out = bank(("S2", n))
                    if br == "c":
                        for t in range(NT):
                            last = pe.matmul(out[:, t * NCMP:(t + 1) * NCMP], q2[r, hd // 2, t * P:(t + 1) * P],
                                             kcmp[r, (hd // 4) * NCMP:(hd // 4 + 1) * NCMP], start=True, stop=True)
                    else:
                        last = pe.matmul(out[:, 0:(i + 1) * P], q2[r, hd // 2, i * P:(i + 1) * P],
                                         kd[0 if br == "s" else 1][r, hd // 4, 0:(i + 1) * P], start=True, stop=True)
                    last.then_inc(full[BK["S2", n][0]], 1)
                v = n - 2
                if 0 <= v < NU:
                    hd, br, i = UNITS[v]
                    pe.wait_ge(probs_ready, 32 + v + 1)
                    out = bank(("T2", v))
                    if br == "c":
                        for t in range(NT):
                            last = pe.transpose(out[0:NCMP, t * P:(t + 1) * P],
                                                scores2[v % 4][:, t * NCMP:(t + 1) * NCMP], ident)
                    else:
                        for kt in range(i + 1):
                            last = pe.transpose(out[:, kt * P:(kt + 1) * P], scores2[v % 4][:, kt * P:(kt + 1) * P],
                                                ident)
                    last.then_inc(full[BK["T2", v][0]], 1)
                v = n - 3
                if 0 <= v < NU and UNITS[v][1] != "c":
                    hd, br, i = UNITS[v]
                    g, r0, hp = hd // 4, 64 * (hd % 2), hd // 2
                    if v % 18 == 1:
                        bank(("O2", hp))
                    out = ps[5 + hp % 2][r0:r0 + 64, i * P:(i + 1) * P]
                    if br == "s":
                        if i == 0:
                            emptied(pe, ("T2", v - 1))
                        pe.matmul(out, vcmp[0:NCMP, 64 * g:64 * g + 64], pTc[0:NCMP, i * P:(i + 1) * P],
                                  start=True, stop=False)
                    emptied(pe, ("T2", v))
                    for kt in range(i + 1):
                        last = pe.matmul(out, v2[0 if br == "s" else 1][:, kt, 64 * g:64 * g + 64],
                                         pT[PV_BEFORE[v] % 2][:, kt * P:(kt + 1) * P],
                                         start=False, stop=(br == "w" and kt == i))
                    last.then_inc(pv_done, 1)
            norm_sum(("att",))
            pe.wait_ge(lo_ready, SPL["att",] + HT)
            features([("out2", m) for m in range(DT)], STR["out2", 0].g0,
                     beside=lambda t: norm_tile(("post_mix",), t - 1) if t else None)
            norm_tile(("post_mix",), DT - 1)
            spread(("post_mix",))
            norm_sum(("mlp",))
            n0 = BK.ffn2
            gq = STR["ff1", 1].g0
            up(STR["ff1", 0].g0, 0, SPL["mlp",])
            with pe.Fori(1, FG2) as j:
                up(gq, j)
                down(gq + 4, j - 1, 8 * (j - 1), 4, SPL["act2",])
            after = ("post_mlp",)
            down(gq + 8 * (FG2 - 1), FG2 - 1, 0, 4, SPL["act2",], sums)
            sums(3)
            spread(after)
            pe.wait_ge(h_set, 3 * DT)
            for t in range(NT):
                for j in range(2):
                    out = bank(("y", t, j))
                    for f in range(4):
                        last = pe.transpose(out[:, f * P:(f + 1) * P], h[:, 4 * j + f, t * P:(t + 1) * P], ident)
                    last.then_inc(full[BK["y", t, j][0]], 1)


_INS = ["x", "positions", "attn_norm", "w_in", "sgu_v_norm", "sgu_w_spatial", "sgu_b_spatial", "lambda_q1",
        "lambda_k1", "lambda_q2", "lambda_k2", "subln_gain", "w_out", "ffn_norm", "w_up", "conv_w", "conv_b",
        "w_down", "final_norm", "c_2", "ada_w_2", "ada_b_2", "pre_norm_mix_2", "w_in_2", "conv_w_2", "conv_b_2",
        "lru_wa_2", "lru_ba_2", "lru_wx_2", "lru_bx_2", "lru_lambda_2", "cmp_pos_k_2", "cmp_w1_k_2", "cmp_w2_k_2",
        "cmp_pos_v_2", "cmp_w1_v_2", "cmp_w2_v_2", "norm_rnn_out_2", "norm_att_out_2", "w_out_2",
        "post_norm_mix_2", "pre_norm_mlp_2", "w_ff1_2", "w_ff2_2", "post_norm_mlp_2"]


def kernel(**inputs):
    import concourse.bacc as bacc
    from concourse.bass_utils import run_bass_kernel_spmd

    nc = bacc.Bacc("TRN2", target_bir_lowering=False, num_devices=1, dynamic_dma_scratch_size=1024)
    arrays, args = {"in_consts": constants()}, {}
    for name in _INS:
        arrays["in_" + name] = np.ascontiguousarray(inputs[name])
    for name, v in arrays.items():
        args[name[3:]] = nc.dram_tensor(name, v.shape, mybir.dt.from_np(v.dtype), kind="ExternalInput").ap()
    args["out"] = nc.dram_tensor("out_y", (1, S, D), F32, kind="ExternalOutput").ap()
    build(nc, args)
    r = run_bass_kernel_spmd(nc, [arrays], core_ids=[0])
    return r.results[0]["out_y"]
```

```python
from contextlib import ExitStack

import numpy as np
import concourse.bass as bass
from concourse import mybir

F32 = mybir.dt.float32
F32R = mybir.dt.float32r
I32 = mybir.dt.int32
ALU = mybir.AluOpType
ACT = mybir.ActivationFunctionType
AX = mybir.AxisListType

P = 128
S = 512
NT = S // P
D = 1024
DT = D // P
DEPTH = 2
HALF = D // 2
HT = HALF // P
HEADS = 4
FF = 2816
FG = FF // 256
FF2 = 4096
FG2 = FF2 // 512
EPS = 1e-6
NEG = -1e30
HEADS2 = 8
CMP_LEN, CMP_STRIDE = 32, 16
NCMP = (S - CMP_LEN) // CMP_STRIDE + 1
ROT = 16
THETA = 500000.0
LRU_C = 8.0
TAPS2 = 4
LOOK = 3
SLOPES = [2.0 ** (-8.0 * (h + 1) / HEADS2) for h in range(HEADS2)]
LAMBDA_INIT = [0.8 - 0.6 * float(np.exp(-0.3 * l)) for l in range(DEPTH)]

ROWS0 = {}
_n = 0
for _name, _k in (("attn_norm", DEPTH * DT), ("ffn_norm", DEPTH * DT), ("final_norm", DT), ("sgu_v_norm", DEPTH * HT),
                  ("subln_gain", DEPTH), ("pre_norm_mix_2", DT), ("post_norm_mix_2", DT), ("pre_norm_mlp_2", DT),
                  ("post_norm_mlp_2", DT), ("conv_b_2", HT), ("conv_w_2", TAPS2 * HT), ("lru_ba_2", HT),
                  ("lru_bx_2", HT), ("lru_lambda_2", HT), ("norm_rnn_out_2", HT), ("norm_att_out_2", HT)):
    ROWS0[_name] = (_n, _k)
    _n += _k
NROWS0 = _n
ADA_T = 6 * DT
ADA_W = ADA_T * P // 2
FT = 2 * FF // P
POS_ROW = ADA_T + DT
NROWS = [NROWS0, POS_ROW + 32] + [2 * FT] * 4
ATT_STEPS = 16 + 7
LOWEST = -3.0e38
ROUND = 12582912.0
TWO_PI = (2 * float(np.pi), 6.28125, 0.0019350051879882812, float(2 * np.pi - 6.28125 - 0.0019350051879882812))
PI_BELOW = 3.1415925


def constants():
    ident = np.eye(P, dtype=np.float32)
    half = ROT // 2
    rot = np.zeros((P, P), np.float32)
    invf = np.zeros((P, 1), np.float32)
    for base in (0, 64):
        for j in range(half):
            rot[base + j, base + half + j] = -1.0
            rot[base + half + j, base + j] = 1.0
            invf[base + j, 0] = invf[base + half + j, 0] = np.float32(THETA) ** np.float32(-2.0 * j / ROT)
    q = np.arange(P)[:, None]
    d = np.arange(S)[None, :] - (S - P) - q
    causal = np.where(d <= 0, 0.0, NEG).astype(np.float32)
    alibi = np.where(d <= 0, d, NEG).astype(np.float32)
    t = P * np.arange(NT)[None, :, None] + q[:, :, None]
    dc = (CMP_STRIDE * np.arange(NCMP) + CMP_LEN - 1)[None, None, :] - t
    alibi_c = np.where(dc <= 0, dc, NEG).astype(np.float32).reshape(P, NT * NCMP)
    seen = (q >= CMP_LEN - 1).astype(np.float32)
    return np.concatenate([ident, rot.T, causal, alibi, alibi_c, invf, seen], axis=1)


C_ID, C_ROT, C_CAUSAL, C_ALIBI = 0, P, 2 * P, 2 * P + S
C_ALIBIC = C_ALIBI + S
C_INVF = C_ALIBIC + NT * NCMP
C_SEEN = C_INVF + 1
NCONST = C_SEEN + 1


class Stripe:

    def __init__(self, kind, quarters, g0):
        self.kind, self.quarters, self.g0 = kind, quarters, g0


def plan():
    order, g = {}, 0

    def add(name, kind, quarters):
        nonlocal g
        order[name] = Stripe(kind, quarters, g)
        order[name].index = len(order) - 1
        g += quarters

    for l in range(DEPTH):
        for name, kind in (("u", "F"), ("vs", "T"), ("q", "F"), ("k", "F"), ("va", "T")):
            add((name, l), kind, 4)
        add(("out", l, 0), "F", 4)
        add(("out", l, 1), "F", 4)
        add(("up", l, 0), "U", 4)
        for j in range(1, FG):
            add(("up", l, j), "U", 4)
            add(("down", l, j - 1), "D2", 4)
        add(("down", l, FG - 1), "D2", 4)
    add(("x_rnn",), "F", 4)
    add(("kvs",), "F", 4)
    add(("kw",), "W", 3)
    add(("q2",), "F", 4)
    add(("g_rnn",), "F", 4)
    add(("cmp", 0), "C", 4)
    add(("cmp", 1), "C", 4)
    add(("out2", 0), "F", 4)
    add(("out2", 1), "F", 4)
    add(("ff1", 0), "F", 4)
    for j in range(1, FG2):
        add(("ff1", j), "F", 4)
        add(("ff2", j - 1), "D4", 4)
    add(("ff2", FG2 - 1), "D4", 4)
    return order


def raw_quarter(kind, raw, q):
    if kind == "F":
        return raw[:, :].rearrange("p (k c) -> p k c", k=DT)[:, :, q * P:(q + 1) * P]
    if kind == "W":
        w = (P, P, 24)[q]
        return raw[:, 0:DT * 280].rearrange("p (k c) -> p k c", k=DT)[:, :, q * P:q * P + w]
    if kind in ("T", "C"):
        return raw[:, q * 1024:(q + 1) * 1024]
    if kind == "U":
        v = raw[:, :].rearrange("p (h k c) -> p h k c", h=2, k=DT)
        return v[:, q % 2, :, (q // 2) * P:(q // 2 + 1) * P]
    k = int(kind[1])
    return raw[:, 0:k * D].rearrange("p (k c) -> p k c", k=k)[:, :, q * 256:(q + 1) * 256]


def split_quarter(kind, part, slot, q):
    if kind in ("F", "U"):
        return part[:, slot, :].rearrange("p (k c) -> p k c", k=DT)
    if kind == "W":
        w = (P, P, 24)[q]
        return part[:, slot, 0:DT * w].rearrange("p (k c) -> p k c", k=DT)
    if kind in ("T", "C"):
        return part[:, slot, :]
    k = int(kind[1])
    return part[:, slot, 0:k * 256].rearrange("p (k c) -> p k c", k=k)


class Banks:

    def __init__(self):
        self.n, self.f, self.use = [0] * 8, [0] * 8, {}

    def take(self, key, bank, quarter=None, counted=True):
        self.use[key] = (bank, self.n[bank], self.f[bank], quarter)
        self.n[bank] += 1
        if quarter is None and counted:
            self.f[bank] += 1

    def __getitem__(self, key):
        return self.use[key]


def attention_units():
    units = []
    for hd in range(HEADS2):
        units.append((hd, "c", 0))
        for i in range(NT):
            units += [(hd, "s", i), (hd, "w", i)]
    return units


UNITS = attention_units()
NU = len(UNITS)
PV_BEFORE = [sum(1 for x in UNITS[:v] if x[1] != "c") for v in range(NU + 1)]


def bank_plan(st):
    b = Banks()
    b.ffn = {}
    for f in range(DT):
        b.take(("x", f), f)
    b.take("cols0", 0)

    def norm(e, bank=7):
        b.take(("norm", e), bank, counted=False)
        b.take(("rstd", e), bank)
        if e == ("final",):
            b.take(("rstd", ("mix2",)), 2)

    norm(("attn", 0))
    for l in range(DEPTH):
        for t in range(4):
            b.take(("u", l, t), t, st["u", l].g0 + t)
        for t in range(NT):
            b.take(("vs", l, t), 3 + t, st["vs", l].g0 + 3)
        if l == 0:
            b.take("cols1", 0)
            b.take("cols2", 1)
            for m in range(DEPTH):
                b.take(("wsT", m), 2 + m)
        for name in ("q", "k"):
            for t in range(4):
                b.take((name, l, t), t, st[name, l].g0 + t)
            for t in range(4):
                b.take(("rope", name, l, t), 4 + t % 2)
        for t in range(NT):
            b.take(("va", l, t), t, st["va", l].g0 + 3)
        for g in range(HT):
            b.take(("mix", l, g), 4 + g % 2)
        if l == 1:
            b.take(("ada", 0), 6)
        b.take(("norm", ("sub", l)), 7, counted=False)
        for n in range(ATT_STEPS):
            if n < 16:
                for m in range(2):
                    b.take(("S", l, n, m), 2 * (n % 2) + m)
            if 0 <= n - 2 < 16:
                b.take(("T", l, n - 2), 4 + n % 2)
            if 0 <= n - 3 < 16 and (n - 3) % 4 == 0:
                b.take(("O", l, (n - 3) // 4), 6, counted=False)
        for hd in range(HEADS):
            b.take(("rstd", ("sub", l, hd)), 4 + hd)
        for m in range(DT):
            b.take(("out", l, m), m % 4, st["out", l, 0].g0 + m)
        norm(("ffn", l))
        b.ffn[l] = list(b.n)
        for t in range(4):
            b.n[t] += FG
            b.n[4 + t] += 2 * FG
        norm(("attn", 1) if l == 0 else ("final",), 1)
    for t in range(4):
        b.take(("x_rnn", t), t, st["x_rnn",].g0 + t)
    b.take(("ada", 1), 7)
    for t in range(3):
        b.take(("kvs", t), t, st["kvs",].g0 + t)
    b.take(("vsel",), 3, st["kvs",].g0 + 3)
    b.take(("kw",), 0, st["kw",].g0)
    b.take(("vwin",), 1, st["kw",].g0 + 1)
    b.take(("gates",), 2, st["kw",].g0 + 2)
    for name in ("q2", "g_rnn"):
        for t in range(4):
            b.take((name, t), t, st[name,].g0 + t)
    for t in range(HT):
        b.take(("ra", t), 4 + t % 2)
        b.take(("rx", t), 6)
    norm(("rnn",))
    for j in range(2):
        b.take(("chid", j), 2 * j, st["cmp", j].g0 + 3)
        b.take(("cturn", j), 6)
        b.take(("cout", j), 4 + j)
    for n in range(NU + 4):
        if n < NU:
            b.take(("S2", n), n % 3)
        if 0 <= n - 2 < NU:
            b.take(("T2", n - 2), 3 + n % 2)
        u = n - 3
        if 0 <= u < NU and u % 18 == 1:
            b.take(("O2", u // 18), 5 + (u // 18) % 2, counted=False)
    norm(("att",))
    for m in range(DT):
        b.take(("out2", m), m % 4, st["out2", 0].g0 + m)
    norm(("post_mix",))
    norm(("mlp",))
    b.ffn2 = list(b.n)
    for t in range(4):
        b.n[t] += FG2
        b.n[4 + t] += 2 * FG2
    norm(("post_mlp",), 1)
    for t in range(NT):
        for j in range(2):
            b.take(("y", t, j), 2 * (t % 2) + j)
    return b


def norm_plan():
    out, sq, adds, sums = {}, 0, 0, 0

    def add(e, k):
        nonlocal sq, adds, sums
        out[e] = (len(out), sq, k, adds, sums)
        sums += HEADS if e[0] == "sub" else 1
        sq += k
        adds += k - sums_of(e)

    for l in range(DEPTH):
        add(("attn", l), DT)
        add(("sub", l), HEADS)
        add(("ffn", l), DT)
    for e, k in ((("final",), 2 * DT), (("rnn",), HT), (("att",), HT), (("post_mix",), DT),
                 (("mlp",), DT), (("post_mlp",), DT)):
        add(e, k)
    return out


def sums_of(e):
    return HEADS if e[0] == "sub" else 2 if e == ("final",) else 1


def split_plan():
    out, k = {}, 0
    for l in range(DEPTH):
        for name, n in (("attn", DT), ("sgu", HT), ("sub", HEADS), ("ffn", DT), ("act", 2 * FG)):
            out[(name, l)] = k
            k += n
    for name, n in (("mix2", DT), ("cmp", 2), ("rnn", HT), ("att", HT), ("mlp", DT), ("act2", 4 * FG2)):
        out[(name,)] = k
        k += n
    return out


def build(nc, a):
    STR = plan()
    BK = bank_plan(STR)
    NRM = norm_plan()
    SPL = split_plan()
    stripes = list(STR.values())
    by_quarter = [(st, q) for st in stripes for q in range(st.quarters)]

    with ExitStack() as ctx:
        def sb(name, shape, dt=F32, where=ctx):
            return where.enter_context(nc.sbuf_tensor(name, shape, dt))

        def sem(name):
            return ctx.enter_context(nc.semaphore(name))

        raw = [sb(f"raw{i}", [P, 4096]) for i in range(2)]
        w_hi = sb("w_hi", [P, 4, 1024], F32R)
        w_lo = sb("w_lo", [P, 4, 1024], F32R)
        h = sb("h", [P, DT, S])
        n_hi = sb("n_hi", [P, DT, S], F32R)
        n_lo = sb("n_lo", [P, DT, S], F32R)
        zb = sb("zb", [P, 4096])
        zc = sb("zc", [P, 2048])
        zd = sb("zd", [P, 3328])
        tb = sb("tb", [P, 3, S])
        sq = sb("sq", [P, 2, S])
        rt = sb("rt", [P, HEADS * NT])
        rstd = sb("rstd", [P, HEADS * NT + 1])
        ms = sb("ms", [P, 2 * NT])
        ss = sb("ss", [P, 2, S])
        const = sb("const", [P, NCONST])
        ones = sb("ones", [P, P])
        cols = sb("cols", [P, 6, P])
        par = sb("par", [P, DEPTH, FG * 16])
        cpar = sb("cpar", [P, 17])
        small = sb("small", [P, 48])
        more = sb("more", [P, 144])
        blkw = sb("blkw", [P, 2, HT, P])
        cw2 = [sb(f"cw2_{i}", [P, 2, P]) for i in range(2)]
        with ExitStack() as part:
            za = sb("za", [P, 4096], F32, part)
        x_hi = sb("x_hi", [P, 4, S], F32R)
        x_lo = sb("x_lo", [P, 4, S], F32R)
        with ExitStack() as part:
            zy = sb("zy", [P, 4096], F32, part)
        cb_hi = sb("cb_hi", [P, 16, 64], F32R)
        cb_lo = sb("cb_lo", [P, 16, 64], F32R)
        sb("rest_of_zy", [P, 2048])
        ps = [ctx.enter_context(nc.psum_tensor(f"ps{i}", [P, S], F32)) for i in range(8)]

        full = [sem(f"full{i}") for i in range(8)]
        free = [sem(f"free{i}") for i in range(8)]
        landed = [sem(f"landed{i}") for i in range(2)]
        whi_ready, wlo_ready = sem("whi_ready"), sem("wlo_ready")
        quarter_done = sem("quarter_done")
        ada_in, ada_used = sem("ada_in"), sem("ada_used")
        consts_in, x_in, pos_in = sem("consts_in"), sem("x_in"), sem("pos_in")
        gains_in, rows_in = sem("gains_in"), sem("rows_in")
        lam_in, sguw_in, sgub_in, cw2_in = sem("lam_in"), sem("sguw_in"), sem("sgub_in"), sem("cw2_in")
        ones_set, sgu_masked = sem("ones_set"), sem("sgu_masked")
        blk_zero, blk_in = sem("blk_zero"), sem("blk_in")
        c_ready = sem("c_ready")
        ang_ready, rope_ready = sem("ang_ready"), sem("rope_ready")
        lam_dots, lam_exp = sem("lam_dots"), sem("lam_exp")
        h_set = sem("h_set")
        sq_ready, sq_used = sem("sq_ready"), sem("sq_used")
        sums_ready, means_ready = sem("sums_ready"), sem("means_ready")
        rstd_ready = sem("rstd_ready")
        val_ready, hi_ready, lo_ready = sem("val_ready"), sem("hi_ready"), sem("lo_ready")
        dve_seq = sem("dve_seq")
        act_seq = sem("act_seq")
        vss_ready, vroot_ready, vn_ready, qk_ready = (sem("vss_ready"), sem("vroot_ready"), sem("vn_ready"),
                                                      sem("qk_ready"))
        max_ready, exp_ready, probs_ready, pv_done = (sem("max_ready"), sem("exp_ready"), sem("probs_ready"),
                                                      sem("pv_done"))
        conv_begun, conv_tap, silu_done, par_ready = (sem("conv_begun"), sem("conv_tap"), sem("silu_done"),
                                                      sem("par_ready"))
        xr_begun, gate_set, decay_ready, ratio_ready, rootm_ready, rnn_ready, gr_ready = (
            sem("xr_begun"), sem("gate_set"), sem("decay_ready"), sem("ratio_ready"), sem("rootm_ready"),
            sem("rnn_ready"), sem("gr_ready"))
        sp_abs, sp_ready = sem("sp_abs"), sem("sp_ready")
        bias_ready, y_zero, y_sent = sem("bias_ready"), sem("y_zero"), sem("y_sent")

        def filled(e, key):
            b, _, f, quarter = BK[key]
            if quarter is None:
                e.wait_ge(full[b], f + 1)
            else:
                e.wait_ge(quarter_done, quarter + 1)
            return ps[b]

        def emptied(e, key):
            b, n = BK[key][:2]
            e.wait_ge(free[b], n + 1)

        def freed(key):
            return free[BK[key][0]]

        def tiles(buf, k=4):
            return buf.rearrange("p (t s) -> p t s", t=k)

        ident = const[:, C_ID:C_ID + P]
        rotT = const[:, C_ROT:C_ROT + P]
        causal = const[:, C_CAUSAL:C_CAUSAL + S]
        alibi = const[:, C_ALIBI:C_ALIBI + S]
        alibi_c = const[:, C_ALIBIC:C_ALIBIC + NT * NCMP]
        xin = tiles(za[:, :])
        rows = [zb[:, i * P:(i + 1) * P] for i in range(6)]
        sguw = tiles(zb[:, 1024:2048], 8)
        lamv = tiles(zb[:, 2048:2560], 8)
        lamp = tiles(zb[:, 2560:2816], 4)
        u, vg = tiles(za[:, 0:2048]), tiles(za[:, 2048:4096])
        qT, kT = tiles(zb[:, 0:2048]), tiles(zb[:, 2048:4096])
        va = tiles(zc[:, :])
        cosT, sinT = zd[:, 0:512], zd[:, 512:1024]
        wsT = tiles(zd[:, 1024:2048], 8)
        sgub = tiles(zd[:, 2048:3072], 8)
        scores = [zy[:, i * 1024:(i + 1) * 1024].rearrange("p (m s) -> p m s", m=2) for i in range(2)]
        probs = [zy[:, 2048 + i * 512:2560 + i * 512] for i in range(2)]
        pT = [zy[:, 3072 + i * 512:3584 + i * 512] for i in range(2)]
        scores2 = [zy[:, i * 512:(i + 1) * 512] for i in range(4)]
        ada_w, ada_sum = zb[:, 0:ADA_W], zy[:, 0:ADA_W]
        pTc = zd[:, 2752:3264]

        def col(name, i=0, k=1):
            c = ROWS0[name][0] + i
            return cols[:, 0, c:c + k]

        nmx, lsum, rec = small[:, 0:4], small[:, 4:8], small[:, 8:12]
        vss = small[:, 12:28]
        lamd, lame, lamneg, subg = small[:, 28:32], small[:, 32:36], small[:, 36:38], small[:, 38:40]
        eps, zero1 = small[:, 40:41], small[:, 41:42]
        mxs = small[:, 44:48]
        mod = more[:, 0:ADA_T]
        gs1, gs2, pg1, pg2 = (more[:, 48 + 8 * i:56 + 8 * i] for i in range(4))
        csilu = more[:, 80:88]
        spt = more[:, 88:116]
        cmx, csum = more[:, 116:120], more[:, 120:124]
        gr, xc = tiles(za[:, 0:2048]), tiles(za[:, 2048:4096])
        oT = xc
        cval = [tiles(za[:, 2048 + i * 1024:3072 + i * 1024], 16) for i in range(2)]
        q2 = tiles(zc[:, :])
        kk = [tiles(zb[:, i * 1024:(i + 1) * 1024], 2) for i in range(2)]
        kd = [tiles(zb[:, 2048 + i * 1024:3072 + i * 1024], 2) for i in range(2)]
        v2 = [tiles(zd[:, i * 512:(i + 1) * 512]) for i in range(2)]
        gates = tiles(zd[:, 1024:1120])
        bias_h = [zd[:, 1152 + i * 512:1664 + i * 512] for i in range(2)]
        bias_c = [zd[:, 2176 + i * 124:2300 + i * 124] for i in range(2)]
        kcmp, vcmp = zd[:, 2432:2494], zd[:, 2496:2624]
        ghid = tiles(zd[:, 2624:2752], 2)
        hidden = zd[:, 1152:1408]
        rn = [zy[:, i * 512:(i + 1) * 512] for i in range(8)]
        rb = [zc[:, i * 512:(i + 1) * 512] for i in range(4)]
        y = tiles(zy[:, :], DT)

        def ffn_h(l, f):
            return free[4 + f % 4], BK.ffn[l][4 + f % 4] + 2 * (FG - 1) + f // 4 + 1

        def landed_value(st):
            return 32 * (st.index // 2 + 1)

        block = ctx.enter_context(nc.Block())

        @block.sync
        def _(sp):
            def room(name):
                i = STR[name].index
                if i >= 2:
                    old = stripes[i - 2]
                    sp.wait_ge(whi_ready, old.g0 + old.quarters)
                    sp.wait_ge(wlo_ready, old.g0 + old.quarters)
                return i % 2

            def two(slot, pairs):
                for dst, src in pairs:
                    sp.dma_start(dst, src).then_inc(landed[slot], 16)

            def load_f(name, w):
                slot = room(name)
                r = raw[slot][:, 0:DT * w.shape[1]].rearrange("p (k c) -> p k c", k=DT)
                v = w.rearrange("(k p) c -> p k c", p=P)
                two(slot, [(r[:, 0:4], v[:, 0:4]), (r[:, 4:8], v[:, 4:8])])

            def load_up(slot, l, j):
                r = raw[slot][:, :].rearrange("p (h k c) -> p h k c", h=2, k=DT)
                v = a["w_up"][l].rearrange("(k p) c -> p k c", p=P)
                two(slot, [(r[:, i], v[:, :, bass.ds(j * 256 + i * FF, 256)]) for i in range(2)])

            def load_down(slot, l, j):
                two(slot, [(raw[slot][:, k * D:(k + 1) * D], a["w_down"][l][bass.ds(j * 256 + k * P, P), :])
                           for k in range(2)])

            def late_loads():
                def row(tile, at, src, k):
                    sp.dma_start(rows[tile][at:at + k, :], src).then_inc(rows_in, 16)

                sp.dma_start(zc[:, 0:S].bitcast(I32), a["positions"][0, :].partition_broadcast(P)).then_inc(pos_in, 16)
                for j, name in enumerate(("lambda_q1", "lambda_k1", "lambda_q2", "lambda_k2")):
                    for l in range(DEPTH):
                        sp.dma_start(lamv[:, 2 * j + l, :], a[name][l, :].partition_broadcast(P)).then_inc(lam_in, 16)
                sp.dma_start(sguw, a["sgu_w_spatial"].rearrange("l g p q -> p (l g) q")).then_inc(sguw_in, 16)
                sp.dma_start(zd[:, 2048:3072],
                             a["sgu_b_spatial"].rearrange("l g p -> (l g p)").partition_broadcast(P))\
                    .then_inc(sgub_in, 16)
                row(1, 0, a["ada_b_2"].rearrange("l (r p) -> (l r) p", p=P), ADA_T)
                row(1, ADA_T, a["c_2"].rearrange("l (r p) -> (l r) p", p=P), DT)
                for j, name in enumerate(("cmp_pos_k_2", "cmp_pos_v_2")):
                    row(1, POS_ROW + 16 * j, a[name].rearrange("l (j e) d -> (l j) (e d)", e=2), 16)
                for l in range(DEPTH):
                    for j in range(3):
                        row(2 + 2 * l + j // 2, FT * (j % 2), a["conv_w"][l, j, :].rearrange("(r p) -> r p", p=P), FT)
                    row(3 + 2 * l, FT, a["conv_b"][l, :].rearrange("(r p) -> r p", p=P), FT)
                for j, name in enumerate(("cmp_w2_k_2", "cmp_w2_v_2")):
                    for dup in range(2):
                        sp.dma_start(cw2[j][:, :, 64 * dup:64 * dup + 64],
                                     a[name][0].rearrange("(m p) d -> p m d", p=P)).then_inc(cw2_in, 16)
                sp.wait_ge(blk_zero, 1)
                for j, name in enumerate(("lru_wa_2", "lru_wx_2")):
                    for e in range(2):
                        sp.dma_start(blkw[64 * e:64 * e + 64, j, :, 64 * e:64 * e + 64],
                                     a[name][0].rearrange("(t e) i j -> e i t j", e=2)[e]).then_inc(blk_in, 16)

            def load_ada(l, k):
                sp.dma_start(ada_w, a["ada_w_2"][0][bass.ds(k * P, P), l * ADA_W:(l + 1) * ADA_W]).then_inc(ada_in, 16)

            sp.dma_start(xin, a["x"].rearrange("b (t p) c -> p (b t) c", p=P)).then_inc(x_in, 16)
            for l in range(DEPTH):
                for j, name in enumerate(("u", "vs", "q", "k", "va")):
                    load_f((name, l), a["w_in"][l][:, j * 512:(j + 1) * 512])
                    if l == 0 and j == 1:
                        late_loads()
                for j in range(2):
                    load_f(("out", l, j), a["w_out"][l][:, j * 512:(j + 1) * 512])
                load_up(room(("up", l, 0)), l, 0)
                sp.wait_ge(lo_ready, SPL["sub", l] + HEADS)
                load_ada(l, 0)
                load_up(room(("up", l, 1)), l, 1)
                load_down(room(("down", l, 0)), l, 0)
                g0 = STR["up", l, 2].g0
                for first, end in ((2, DT + 1), (DT + 1, FG)):
                    with sp.Fori(first, end) as j:
                        sp.wait_ge(whi_ready, g0 - 4 + (j - 2) * 8)
                        sp.wait_ge(wlo_ready, g0 - 4 + (j - 2) * 8)
                        load_up(STR["up", l, 2].index % 2, l, j)
                        sp.wait_ge(whi_ready, g0 + (j - 2) * 8)
                        sp.wait_ge(wlo_ready, g0 + (j - 2) * 8)
                        load_down(STR["down", l, 1].index % 2, l, j - 1)
                        if first == 2:
                            sp.wait_ge(ada_used, DT * l + j - 1)
                            load_ada(l, j - 1)
                load_down(room(("down", l, FG - 1)), l, FG - 1)
            w2 = a["w_in_2"][0]
            for name, c, w in (("x_rnn", 512, 512), ("kvs", 1536, 512), ("kw", 2048, 280), ("q2", 1024, 512),
                               ("g_rnn", 0, 512)):
                load_f((name,), w2[:, c:c + w])
            for j, name in enumerate(("cmp_w1_k_2", "cmp_w1_v_2")):
                slot = room(("cmp", j))
                r = raw[slot][:, :].rearrange("p (k c) -> p k c", k=16)
                v = a[name][0].rearrange("(k p) c -> p k c", p=P)
                two(slot, [(r[:, 0:8], v[:, 0:8]), (r[:, 8:16], v[:, 8:16])])
            for j in range(2):
                load_f(("out2", j), a["w_out_2"][0][:, j * 512:(j + 1) * 512])

            def load_ff1(slot, j):
                r = raw[slot][:, :].rearrange("p (k c) -> p k c", k=DT)
                v = a["w_ff1_2"][0].rearrange("(k p) c -> p k c", p=P)
                two(slot, [(r[:, 4 * i:4 * i + 4], v[:, 4 * i:4 * i + 4, bass.ds(j * 512, 512)]) for i in range(2)])

            def load_ff2(slot, j):
                r = raw[slot][:, :].rearrange("p (k c) -> p k c", k=4)
                two(slot, [(r[:, 2 * i:2 * i + 2],
                            a["w_ff2_2"][0][bass.ds(j * 512 + i * 256, 256), :].rearrange("(k p) c -> p k c", p=P))
                           for i in range(2)])

            load_ff1(room(("ff1", 0)), 0)
            load_ff1(room(("ff1", 1)), 1)
            load_ff2(room(("ff2", 0)), 0)
            g0 = STR["ff1", 2].g0
            with sp.Fori(2, FG2) as j:
                sp.wait_ge(whi_ready, g0 - 4 + (j - 2) * 8)
                sp.wait_ge(wlo_ready, g0 - 4 + (j - 2) * 8)
                load_ff1(STR["ff1", 2].index % 2, j)
                sp.wait_ge(whi_ready, g0 + (j - 2) * 8)
                sp.wait_ge(wlo_ready, g0 + (j - 2) * 8)
                load_ff2(STR["ff2", 1].index % 2, j - 1)
            load_ff2(room(("ff2", FG2 - 1)), FG2 - 1)
            for t in range(NT):
                for j in range(2):
                    emptied(sp, ("y", t, j))
                sp.dma_start(a["out"][0, t * P:(t + 1) * P, :], zb[:, t * D:(t + 1) * D]).then_inc(y_sent, 16)
            sp.wait_ge(y_sent, 16 * NT)

        @block.gpsimd
        def _(pool):
            pool.memset(ones[:, :], 1.0).then_inc(ones_set, 1)
            pool.memset(eps, EPS).then_inc(ones_set, 1)
            pool.memset(zero1, 0.0).then_inc(ones_set, 1)
            pool.memset(blkw[:, :, :, :], 0.0).then_inc(blk_zero, 1)
            pool.wait_ge(sguw_in, 16)
            pool.affine_select(out=sguw, in_=sguw, compare_op=ALU.is_ge, fill=0.0, base=0,
                               pattern=[[0, DEPTH * 4], [-1, P]], channel_multiplier=1).then_inc(sgu_masked, 1)

            def lo(g, value, used):
                st, q = by_quarter[g]
                if used is not None:
                    pool.wait_ge(quarter_done, used)
                pool.wait_ge(whi_ready, value)
                pool.tensor_tensor(split_quarter(st.kind, w_lo, g % 4, q), raw_quarter(st.kind, raw[st.index % 2], q),
                                   split_quarter(st.kind, w_hi.bitcast(F32), g % 4, q), ALU.subtract)\
                    .then_inc(wlo_ready, 1)

            done = 0
            for first, groups in [(STR["up", l, 1].g0, FG) for l in range(DEPTH)] + [(STR["ff1", 1].g0, FG2)]:
                for g in range(done, first):
                    lo(g, g + 1, g - 3 if g >= 4 else None)
                with pool.Fori(0, groups - 1) as j:
                    for g in range(first, first + 8):
                        lo(g, g + 1 + j * 8, g - 3 + j * 8)
                done = first + 8 * (groups - 1)
            for g in range(done, len(by_quarter)):
                lo(g, g + 1, g - 3)

        @block.scalar
        def _(act):
            act.dma_start(const[:, :], a["consts"]).then_inc(consts_in, 16)
            for name, (at, k) in ROWS0.items():
                v = a[name]
                if len(v.shape) == 1:
                    v = v.rearrange("(r p) -> r p", p=P)
                elif len(v.shape) == 2:
                    v = v.rearrange("l (r p) -> (l r) p", p=P)
                else:
                    v = v.rearrange("l w (r p) -> (l w r) p", p=P)
                act.dma_start(rows[0][at:at + k, :], v).then_inc(gains_in, 16)

            ahead = [0]

            def hi(g, landed_at, used):
                st, q = by_quarter[g]
                if q == 0:
                    act.wait_ge(landed[st.index % 2], landed_at)
                if used is not None:
                    act.wait_ge(quarter_done, used)
                act.activation(split_quarter(st.kind, w_hi, g % 4, q), raw_quarter(st.kind, raw[st.index % 2], q),
                               ACT.Copy).then_inc(whi_ready, 1)

            def ensure(upto):
                for g in range(ahead[0], min(upto, len(by_quarter))):
                    hi(g, landed_value(by_quarter[g][0]), g - 3 if g >= 4 else None)
                ahead[0] = max(ahead[0], min(upto, len(by_quarter)))

            def square(e, i, src, ready, scale=1.0):
                _, _, _, adds, sums = NRM[e]
                act.wait_ge(*ready)
                if i < sums_of(e):
                    used = sums + max(i - 1, 0)
                    if used >= 1:
                        act.wait_ge(sums_ready, used)
                    dst = ss[:, i % 2, :]
                else:
                    n = adds + i - sums_of(e)
                    if n >= 2:
                        act.wait_ge(sq_used, n - 1)
                    dst = sq[:, n % 2, :]
                act.activation(dst, src, ACT.Square, scale=scale).then_inc(sq_ready, 1)

            def squares(e, src, ready):
                for f in range(NRM[e][2]):
                    square(e, f, src(f), ready(f))

            def root(e, width):
                num, sums = NRM[e][0], NRM[e][4]
                n = NT * HEADS if e[0] == "sub" else NT
                b = BK["norm", e][0]
                act.wait_ge(sums_ready, sums + n // NT)
                if num >= 1:
                    act.wait_ge(rstd_ready, num)
                act.activation(rt[:, 0:n], ps[b][:, 0:n], ACT.Sqrt, bias=eps, scale=1.0 / width)\
                    .then_inc(free[b], 1)

            def split_hi(k, src, dst):
                act.wait_ge(val_ready, k + 1)
                act.activation(dst, src, ACT.Copy).then_inc(hi_ready, 1)

            def split_tiles(name, count, at):
                for f in range(count):
                    k = SPL[name] + f
                    split_hi(k, tb[:, k % 3, :], n_hi[:, at + f, :])

            act.wait_ge(ones_set, 3)

            def tables():
                act.wait_ge(ang_ready, 1)
                act.activation(sinT, zc[:, 1024:1536], ACT.Sin).then_inc(rope_ready, 1)
                act.activation(cosT, zc[:, 1536:2048], ACT.Sin).then_inc(rope_ready, 1)
                act.wait_ge(lam_dots, 1)
                act.activation(lame, lamd, ACT.Exp).then_inc(lam_exp, 1)
                act.activation(spt[:, 0:4], col("lru_lambda_2", 0, HT), ACT.Abs).then_inc(act_seq, 1)
                act.wait_ge(act_seq, 1)
                act.activation(spt[:, 4:8], spt[:, 0:4], ACT.Exp, scale=-1.0).then_inc(sp_abs, 1)

            for l in range(DEPTH):
                g0 = STR["u", l].g0
                if l == 0:
                    squares(("attn", l), lambda f: h[:, f, :], lambda f: (free[f], BK["x", f][1] + 1))
                root(("attn", l), D)
                ensure(g0 + 4)
                split_tiles(("attn", l), DT, 0)
                for t in range(4):
                    ensure(g0 + t + 1 + LOOK)
                    act.activation(u[:, t, :], filled(act, ("u", l, t))[:, :], ACT.Gelu_apprx_tanh)\
                        .then_inc(freed(("u", l, t)), 1)
                ensure(g0 + 8 + LOOK)
                if l == 0:
                    tables()
                for t in range(NT):
                    act.activation(vg[:, t, :], filled(act, ("vs", l, t))[:, :], ACT.Gelu_apprx_tanh)\
                        .then_inc(freed(("vs", l, t)), 1)
                act.wait_ge(vss_ready, 4 * l + 4)
                act.activation(vss, vss, ACT.Sqrt, bias=eps, scale=1.0 / P).then_inc(vroot_ready, 1)
                if l == 0:
                    for key in ("cols1", "cols2", ("wsT", 0), ("wsT", 1)):
                        emptied(act, key)
                    act.activation(csilu, cols[:, 1, ADA_T:ADA_T + DT], ACT.Silu).then_inc(c_ready, 1)
                for j, name in enumerate(("q", "k")):
                    for t in range(4):
                        ensure(g0 + 8 + 4 * j + t + 1 + LOOK)
                        act.activation((qT, kT)[j][:, t, :], filled(act, (name, l, t))[:, :], ACT.Copy,
                                       scale=0.125 if j == 0 else 1.0).then_inc(freed((name, l, t)), 1)
                ensure(g0 + 20 + LOOK)
                for t in range(NT):
                    act.activation(va[:, t, :], filled(act, ("va", l, t))[:, :], ACT.Copy)\
                        .then_inc(freed(("va", l, t)), 1)
                split_tiles(("sgu", l), HT, 0)
                for n in range(ATT_STEPS):
                    if n < 16:
                        i = n % 4
                        act.wait_ge(max_ready, l * 16 + n + 1)
                        for m in range(2):
                            sc = scores[n % 2][:, m, 0:(i + 1) * P]
                            c = 2 * (n % 2) + m
                            act.activation(sc, sc, ACT.Exp, bias=nmx[:, c:c + 1], accum_out=lsum[:, c:c + 1])\
                                .then_inc(exp_ready, 1)
                    if 0 <= n - 2 < 16:
                        v = n - 2
                        i, uv = v % 4, l * 16 + v
                        t_ = filled(act, ("T", l, v))
                        if uv >= 2:
                            act.wait_ge(pv_done, uv - 1)
                        act.activation(pT[v % 2][:, 0:(i + 1) * P], t_[:, 0:(i + 1) * P], ACT.Copy)\
                            .then_inc(freed(("T", l, v)), 1)
                    if n >= 6 and (n - 6) % 4 == 0:
                        hd = (n - 6) // 4
                        if hd < HEADS:
                            square(("sub", l), hd, oT[:, hd, :], (freed(("O", l, hd)), BK["O", l, hd][1] + 1))
                root(("sub", l), P)
                split_tiles(("sub", l), HEADS, HT)
                for m in range(DT):
                    ensure(STR["out", l, 0].g0 + m + LOOK + 1)
                    square(("ffn", l), m, h[:, m, :], (freed(("out", l, m)), BK["out", l, m][1] + 1))
                root(("ffn", l), D)
                ensure(STR["up", l, 0].g0 + 4)
                split_tiles(("ffn", l), DT, 0)

                n0 = BK.ffn[l]
                gq = STR["up", l, 1].g0

                def up_steps(j, first, run_ahead):
                    act.wait_ge(par_ready, 1 + l * FG + j + 1)
                    if not first:
                        act.wait_ge(lo_ready, SPL["act", l] + 2 * j)
                    for i in range(2):
                        for t in (2 * i, 2 * i + 1):
                            run_ahead(t)
                            act.wait_ge(quarter_done, STR["up", l, 0].g0 + t + 1 if first else gq + t + 1 + 8 * (j - 1))
                            act.activation(rb[t], ps[t][:, :], ACT.Identity, bias=cpar[:, 4 * t + 3:4 * t + 4],
                                           scale=cpar[:, 4 * t + 2:4 * t + 3]).then_inc(conv_begun, 1)
                        act.wait_ge(free[2 * i], n0[2 * i] + j + 1)
                        act.activation(rb[2 * i], rb[2 * i], ACT.Silu).then_inc(silu_done, 1)
                    for i in range(4, 8):
                        run_ahead(i)
                    if not first:
                        act.wait_ge(quarter_done, gq + 8 * j)
                    for i in range(2):
                        split_hi(SPL["act", l] + 2 * j + i, rb[2 * i], x_hi[:, i, :])

                g_up = STR["up", l, 0].g0
                up_steps(0, True, lambda i: ensure(g_up + min(i, 3) + 1 + LOOK))
                assert ahead[0] == gq + LOOK
                with act.Fori(1, FG) as j:
                    def run_ahead(i):
                        g = gq + i + LOOK
                        hi(g, landed_value(by_quarter[g][0]) + 32 * (j - 1), g - 3 + 8 * (j - 1))
                    up_steps(j, False, run_ahead)
                ahead[0] = gq + 8 * (FG - 1) + LOOK
                for m in range(DT):
                    ensure(gq + 8 * (FG - 1) + m // 2 + 1 + LOOK)
                    if l == 0:
                        square(("attn", 1), m, h[:, m, :], ffn_h(l, m))
                    else:
                        square(("final",), 2 * m, h[:, m, :], ffn_h(l, m))
                        square(("final",), 2 * m + 1, h[:, m, :], ffn_h(l, m), col("final_norm", m))

            act.wait_ge(means_ready, 1)
            act.wait_ge(rstd_ready, NRM["final",][0])
            act.activation(rt[:, 0:2 * NT], ms[:, :], ACT.Sqrt, bias=zero1).then_inc(act_seq, 1)
            g0 = STR["x_rnn",].g0
            ensure(g0 + 4)
            split_tiles(("mix2",), DT, 0)
            for t in range(4):
                ensure(g0 + t + 1 + LOOK)
                act.activation(xc[:, t, :], filled(act, ("x_rnn", t))[:, :], ACT.Identity, bias=col("conv_b_2", t),
                               scale=col("conv_w_2", 3 * HT + t)).then_inc(xr_begun, 1)

            def decay(t):
                if t == 0:
                    act.wait_ge(sp_ready, 1)
                else:
                    act.wait_ge(rnn_ready, t)
                b = filled(act, ("ra", t))
                act.activation(rn[0], b[:, :], ACT.Sigmoid, bias=col("lru_ba_2", t)).then_inc(freed(("ra", t)), 1)
                b = filled(act, ("rx", t))
                act.activation(rn[1], b[:, :], ACT.Sigmoid, bias=col("lru_bx_2", t)).then_inc(freed(("rx", t)), 1)
                emptied(act, ("ra", t))
                act.activation(rn[2], rn[0], ACT.Exp, scale=spt[:, 20 + t:21 + t])
                act.activation(rn[3], rn[0], ACT.Tanh, scale=spt[:, 24 + t:25 + t]).then_inc(decay_ready, 1)

            def decay_root(t):
                act.wait_ge(ratio_ready, t + 1)
                act.activation(rn[4], rn[4], ACT.Sqrt, bias=zero1, scale=2.0).then_inc(rootm_ready, 1)

            def keys(j):
                key, vkey = ((("kvs", 2), ("vsel",)), (("kw",), ("vwin",)))[j]
                ensure(STR["kvs",].g0 + (3, 5)[j] + LOOK)
                b = filled(act, key)
                for g in range(2):
                    for half in range(2):
                        last = act.activation(kd[j][64 * half:64 * half + 64, g, :], b[64 * g:64 * g + 64, :],
                                              ACT.Copy)
                last.then_inc(freed(key), 1)
                ensure(STR["kvs",].g0 + (4, 6)[j] + LOOK)
                act.activation(zd[:, j * 512:(j + 1) * 512], filled(act, vkey)[:, :], ACT.Copy)\
                    .then_inc(freed(vkey), 1)

            def queries(t):
                ensure(STR["q2",].g0 + t + 1 + LOOK)
                act.activation(q2[:, t, :], filled(act, ("q2", t))[:, :], ACT.Copy, scale=0.125)\
                    .then_inc(freed(("q2", t)), 1)

            for j in range(2):
                ensure(STR["kvs",].g0 + j + 1 + LOOK)
                b = filled(act, ("kvs", j))
                for g in range(2):
                    act.activation(kk[j][0:64, g, :], b[64 * g:64 * g + 64, :], ACT.Copy)
                    last = act.activation(kk[j][64:128, g, 0:S - 1], b[64 * g:64 * g + 64, 1:S], ACT.Copy)
                last.then_inc(freed(("kvs", j)), 1)
            decay(0)
            keys(0)
            decay_root(0)
            decay(1)
            keys(1)
            ensure(STR["kw",].g0 + 3 + LOOK)
            act.activation(zd[:, 1024:1120], filled(act, ("gates",))[:, 0:96], ACT.Sigmoid)\
                .then_inc(freed(("gates",)), 1)
            decay_root(1)
            decay(2)
            queries(0)
            queries(1)
            decay_root(2)
            decay(3)
            queries(2)
            queries(3)
            decay_root(3)
            act.wait_ge(rnn_ready, HT)
            for t in range(4):
                ensure(STR["g_rnn",].g0 + t + 1 + LOOK)
                act.activation(rn[4 + t], filled(act, ("g_rnn", t))[:, :], ACT.Gelu_apprx_tanh)\
                    .then_inc(freed(("g_rnn", t)), 1)
            for j in range(2):
                act.wait_ge(val_ready, SPL["cmp",] + j + 1)
                if j == 1:
                    act.wait_ge(quarter_done, STR["cmp", 0].g0 + 4)
                act.activation(cb_hi[:, :, 0:2 * NCMP], cval[j][:, :, 0:2 * NCMP], ACT.Copy).then_inc(hi_ready, 1)
                ensure(STR["cmp", j].g0 + 4 + LOOK)
                act.activation(hidden[0:2 * NCMP, :], filled(act, ("chid", j))[0:2 * NCMP, 0:256],
                               ACT.Gelu_apprx_tanh).then_inc(freed(("chid", j)), 1)
                b = filled(act, ("cturn", j))
                act.activation(ghid[:, :, 0:2 * NCMP],
                               b[:, 0:4 * NCMP].rearrange("p (m c) -> p m c", m=2), ACT.Copy)\
                    .then_inc(freed(("cturn", j)), 1)
                b = filled(act, ("cout", j))
                if j == 0:
                    act.activation(kcmp, b[:, 0:62], ACT.Copy).then_inc(freed(("cout", j)), 1)
                else:
                    act.activation(vcmp[0:NCMP, :], b[0:NCMP, 0:128], ACT.Copy).then_inc(freed(("cout", j)), 1)

            def bias(hd):
                act.activation(bias_h[hd % 2], alibi, ACT.Copy, scale=SLOPES[hd])
                act.activation(bias_c[hd % 2], alibi_c, ACT.Copy, scale=SLOPES[hd]).then_inc(bias_ready, 1)

            bias(0)
            for n in range(NU + 4):
                if n == 0:
                    squares(("rnn",), lambda f: gr[:, f, :], lambda f: (gr_ready, f + 1))
                if n == 2:
                    root(("rnn",), HALF)
                if 4 <= n < 4 + HT:
                    k = SPL["rnn",] + n - 4
                    split_hi(k, tb[:, k % 3, :], n_hi[:, n - 4, :])
                if n < NU:
                    hd, br, i = UNITS[n]
                    if br == "s" and i == 2 and hd + 1 < HEADS2:
                        bias(hd + 1)
                    sc = scores2[n % 4]
                    act.wait_ge(max_ready, 32 + n + 1)
                    if br == "c":
                        act.activation(sc[:, 0:124], sc[:, 0:124], ACT.Exp).then_inc(exp_ready, 1)
                    else:
                        sc = sc[:, 0:(i + 1) * P]
                        act.activation(sc, sc, ACT.Exp, bias=nmx[:, n % 4:n % 4 + 1],
                                       accum_out=lsum[:, n % 4:n % 4 + 1]).then_inc(exp_ready, 1)
                v = n - 2
                if 0 <= v < NU:
                    hd, br, i = UNITS[v]
                    before = PV_BEFORE[v]
                    t_ = filled(act, ("T2", v))
                    if br == "c":
                        act.wait_ge(pv_done, 32 + before)
                        act.activation(pTc[0:NCMP, :], t_[0:NCMP, :], ACT.Copy).then_inc(freed(("T2", v)), 1)
                    else:
                        act.wait_ge(pv_done, 32 + before - 1)
                        act.activation(pT[before % 2][:, 0:(i + 1) * P], t_[:, 0:(i + 1) * P], ACT.Copy)\
                            .then_inc(freed(("T2", v)), 1)
            squares(("att",), lambda f: oT[:, f, :], lambda f: (freed(("O2", f)), BK["O2", f][1] + 1))
            root(("att",), HALF)
            split_tiles(("att",), HT, HT)
            for m in range(DT):
                ensure(STR["out2", 0].g0 + m + LOOK + 1)
                square(("post_mix",), m, y[:, m, :], (freed(("out2", m)), BK["out2", m][1] + 1))
            root(("post_mix",), D)
            ensure(STR["ff1", 0].g0 + 4)
            squares(("mlp",), lambda f: h[:, f, :], lambda f: (h_set, DT + f + 1))
            root(("mlp",), D)
            split_tiles(("mlp",), DT, 0)

            n0 = BK.ffn2
            gq = STR["ff1", 1].g0

            def ff1_steps(j, first, run_ahead):
                if not first:
                    act.wait_ge(lo_ready, SPL["act2",] + 4 * j)
                for t in range(4):
                    run_ahead(t)
                    act.wait_ge(quarter_done, STR["ff1", 0].g0 + t + 1 if first else gq + t + 1 + 8 * (j - 1))
                    act.activation(rb[t], ps[t][:, :], ACT.Relu).then_inc(free[t], 1)
                for i in range(4, 8):
                    run_ahead(i)
                if not first:
                    act.wait_ge(quarter_done, gq + 8 * j)
                for t in range(4):
                    split_hi(SPL["act2",] + 4 * j + t, rb[t], x_hi[:, t, :])

            g_up = STR["ff1", 0].g0
            ff1_steps(0, True, lambda i: ensure(g_up + min(i, 3) + 1 + LOOK))
            assert ahead[0] == gq + LOOK
            with act.Fori(1, FG2) as j:
                def run_ahead(i):
                    g = gq + i + LOOK
                    hi(g, landed_value(by_quarter[min(g, len(by_quarter) - 1)][0]) + 32 * (j - 1), g - 3 + 8 * (j - 1))
                ff1_steps(j, False, run_ahead)
            ahead[0] = gq + 8 * (FG2 - 1) + LOOK
            for m in range(DT):
                ensure(gq + 8 * (FG2 - 1) + m // 2 + 1 + LOOK)
                square(("post_mlp",), m, y[:, m, :],
                       (free[4 + m % 4], BK.ffn2[4 + m % 4] + 2 * (FG2 - 1) + m // 4 + 1))
            root(("post_mlp",), D)

        @block.vector
        def _(dve):
            chain = [0]

            def link(ins):
                chain[0] += 1
                ins.then_inc(dve_seq, 1)
                dve.wait_ge(dve_seq, chain[0])

            def add_square(e, i):
                _, sq0, _, adds, _ = NRM[e]
                k = sums_of(e)
                if i < k:
                    return
                n = adds + i - k
                dve.wait_ge(sq_ready, sq0 + i + 1)
                if i >= 2 * k:
                    dve.wait_ge(sq_used, n + 1 - k)
                c = i % k
                dve.tensor_tensor(ss[:, c, :], ss[:, c, :], sq[:, n % 2, :], ALU.add).then_inc(sq_used, 1)

            def norm_rstd(e):
                emptied(dve, ("norm", e))
                dve.reciprocal(rstd[:, 0:NT], rt[:, 0:NT]).then_inc(rstd_ready, 1)
                return filled(dve, ("rstd", e))[:, :]

            def rstd_read(e):
                b = BK["rstd", e][0]
                dve.tensor_copy(rstd[:, HEADS * NT:HEADS * NT + 1], ps[b][:, S - 1:S]).then_inc(free[b], 1)

            def split_lo(k, src, hi_, lo_):
                dve.wait_ge(hi_ready, k + 1)
                dve.tensor_tensor(lo_, src, hi_, ALU.subtract).then_inc(lo_ready, 1)

            def norm_split(e, name, count, src, gain, at, shift=None):
                factors = norm_rstd(e) if e != ("mix2",) else filled(dve, ("rstd", e))[:, :]

                def lo_(f):
                    k = SPL[name] + f
                    split_lo(k, tb[:, k % 3, :], n_hi.bitcast(F32)[:, at + f, :], n_lo[:, at + f, :])

                for f in range(count):
                    k = SPL[name] + f
                    t = tb[:, k % 3, :]
                    if k >= 3:
                        dve.wait_ge(lo_ready, k - 2)
                    ins = dve.scalar_tensor_tensor(t, src(f), gain(f), factors, ALU.mult, ALU.mult)
                    if shift is not None:
                        link(ins)
                        ins = dve.tensor_scalar(t, t, shift(f), None, ALU.add)
                    ins.then_inc(val_ready, 1)
                    if f >= 1:
                        lo_(f - 1)
                rstd_read(e)
                lo_(count - 1)

            for f in range(DT):
                dve.tensor_copy(h[:, f, :], filled(dve, ("x", f))[:, :]).then_inc(free[f], 1)
            dve.tensor_copy(cols[:, 0, 0:NROWS0], filled(dve, "cols0")[:, 0:NROWS0]).then_inc(freed("cols0"), 1)
            emptied(dve, "cols0")

            def angles():
                dve.wait_ge(lam_in, 16 * 8)
                for i in range(2):
                    ins = dve.tensor_tensor(lamp[:, 2 * i:2 * i + 2, :], lamv[:, 4 * i:4 * i + 2, :],
                                            lamv[:, 4 * i + 2:4 * i + 4, :], ALU.mult)
                link(ins)
                dve.tensor_reduce(lamd, lamp, AX.X, ALU.add).then_inc(lam_dots, 1)
                for l in range(DEPTH):
                    dve.tensor_scalar(subg[:, l:l + 1], col("subln_gain", l), 1.0 - LAMBDA_INIT[l], None, ALU.mult)
                dve.wait_ge(pos_in, 16)
                dve.wait_ge(consts_in, 16)
                posf, ang, turn = zc[:, 512:1024], zc[:, 0:512], tb[:, 0, :]
                link(dve.tensor_copy(posf, zc[:, 0:512].bitcast(I32)))
                link(dve.tensor_scalar(ang, posf, const[:, C_INVF:C_INVF + 1], None, ALU.mult))
                for i in range(2):
                    r = zc[:, 1024 + 512 * i:1536 + 512 * i]
                    link(dve.tensor_scalar(turn, ang, 1.0 / TWO_PI[0], 0.25 * i, ALU.mult, ALU.add))
                    link(dve.tensor_scalar(turn, turn, ROUND, None, ALU.add))
                    link(dve.tensor_scalar(turn, turn, ROUND, None, ALU.subtract))
                    for j, part in enumerate(TWO_PI[1:]):
                        link(dve.scalar_tensor_tensor(r, turn, -part, ang if j == 0 else r, ALU.mult, ALU.add))
                    link(dve.tensor_scalar(r, r, 0.5 * float(np.pi) * i, PI_BELOW, ALU.add, ALU.min))
                    ins = dve.tensor_scalar(r, r, -PI_BELOW, None, ALU.max)
                ins.then_inc(ang_ready, 1)

            def parameters():
                b = filled(dve, "cols1")
                for i in range(4):
                    last = dve.tensor_copy(cols[:, 1 + i, 0:NROWS[1 + i]], b[:, i * P:i * P + NROWS[1 + i]])
                last.then_inc(freed("cols1"), 1)
                dve.tensor_copy(cols[:, 5, 0:NROWS[5]], filled(dve, "cols2")[:, 0:NROWS[5]]).then_inc(freed("cols2"), 1)
                for l in range(DEPTH):
                    dve.tensor_copy(wsT[:, 4 * l:4 * l + 4, :].rearrange("p m q -> p (m q)"),
                                    filled(dve, ("wsT", l))[:, :]).then_inc(freed(("wsT", l)), 1)
                emptied(dve, "cols1")
                emptied(dve, "cols2")

            def conv_parameters():
                for l in range(DEPTH):
                    pv_ = par[:, l, :].rearrange("p (g j h c) -> p g j h c", g=FG, j=2, h=2)
                    for c in range(4):
                        src = cols[:, 2 + 2 * l + c // 2, FT * (c % 2):FT * (c % 2) + FT]\
                            .rearrange("p (h g j) -> p g j h", h=2, g=FG)
                        for half in range(2):
                            last = dve.tensor_copy(pv_[:, :, :, half, c], src[:, :, :, half])
                last.then_inc(par_ready, 1)

            def scalars():
                dve.wait_ge(lam_exp, 1)
                link(dve.tensor_tensor(lamneg, lame[:, 2:4], lame[:, 0:2], ALU.subtract))
                for l in range(DEPTH):
                    last = dve.tensor_scalar(lamneg[:, l:l + 1], lamneg[:, l:l + 1], -LAMBDA_INIT[l], None, ALU.add)
                link(last)
                dve.wait_ge(sp_abs, 1)
                e_, s1, s2, p_, z_ = (spt[:, 4 * i:4 * i + 4] for i in (1, 2, 3, 4, 0))
                link(dve.tensor_scalar(s1, e_, 2.0, None, ALU.add))
                link(dve.reciprocal(s1, s1))
                link(dve.tensor_tensor(s1, s1, e_, ALU.mult))
                link(dve.tensor_tensor(s2, s1, s1, ALU.mult))
                link(dve.tensor_scalar(p_, s2, 1.0 / 15, None, ALU.mult))
                for k in (13, 11, 9, 7, 5, 3):
                    link(dve.scalar_tensor_tensor(p_, p_, 1.0 / k, s2, ALU.add, ALU.mult))
                link(dve.scalar_tensor_tensor(p_, p_, 1.0, s1, ALU.add, ALU.mult))
                link(dve.tensor_scalar(z_, col("lru_lambda_2", 0, HT), -1.0, 0.0, ALU.mult, ALU.max))
                link(dve.scalar_tensor_tensor(p_, p_, 2.0, z_, ALU.mult, ALU.add))
                dve.tensor_scalar(spt[:, 20:24], p_, -LRU_C, None, ALU.mult)
                dve.tensor_scalar(spt[:, 24:28], p_, LRU_C, None, ALU.mult).then_inc(sp_ready, 1)

            def modulation(l, gains):
                c = slice(l * ADA_T // 2, (l + 1) * ADA_T // 2)
                dve.tensor_tensor(mod[:, c], filled(dve, ("ada", l))[:, 0:ADA_T // 2], cols[:, 1, c], ALU.add)\
                    .then_inc(freed(("ada", l)), 1)
                emptied(dve, ("ada", l))
                for dst, name, part in gains:
                    last = dve.scalar_tensor_tensor(dst, mod[:, 8 * part:8 * part + 8], 1.0, col(name, 0, DT),
                                                    ALU.add, ALU.mult)
                link(last)

            for f in range(DT):
                add_square(("attn", 0), f)
            for l in range(DEPTH):
                if l == 0:
                    for f in range(DT):
                        emptied(dve, ("x", f))
                else:
                    for f in range(4, DT):
                        dve.wait_ge(*ffn_h(l - 1, f))
                norm_split(("attn", l), ("attn", l), DT, lambda f: h[:, f, :], lambda f: col("attn_norm", l * DT + f), 0)
                if l == 0:
                    angles()
                    scalars()
                    parameters()
                for t in range(NT):
                    emptied(dve, ("vs", l, t))
                    link(dve.tensor_tensor(tb[:, t % 3, :], vg[:, t, :], vg[:, t, :], ALU.mult))
                    dve.tensor_reduce(vss[:, 4 * t:4 * t + 4], tiles(tb[:, t % 3, :]), AX.X, ALU.add)\
                        .then_inc(vss_ready, 1)
                    dve.wait_ge(vss_ready, 4 * l + t + 1)
                dve.wait_ge(vroot_ready, l + 1)
                link(dve.reciprocal(vss, vss))
                for t in range(NT):
                    last = dve.tensor_tensor(tiles(vg[:, t, :]), tiles(vg[:, t, :]),
                                             vss[:, 4 * t:4 * t + 4].unsqueeze(2).to_broadcast([P, 4, P]), ALU.mult)
                last.then_inc(vn_ready, 1)
                dve.wait_ge(rope_ready, 2)
                for j, name in enumerate(("q", "k")):
                    for t in range(4):
                        x_ = (qT, kT)[j][:, t, :]
                        n = 8 * l + 4 * j + t
                        if n >= 3:
                            dve.wait_ge(qk_ready, n - 2)
                        dve.tensor_tensor(tb[:, n % 3, :], filled(dve, ("rope", name, l, t))[:, :], sinT, ALU.mult)\
                            .then_inc(freed(("rope", name, l, t)), 1)
                        emptied(dve, (name, l, t))
                        link(dve.tensor_tensor(x_, x_, cosT, ALU.mult))
                        emptied(dve, ("rope", name, l, t))
                        dve.tensor_tensor(x_, x_, tb[:, n % 3, :], ALU.add).then_inc(qk_ready, 1)
                if l == 0:
                    conv_parameters()
                dve.wait_ge(sgub_in, 16)
                dve.wait_ge(qk_ready, 8 * l + 8)

                def sgu_lo(g):
                    k = SPL["sgu", l] + g
                    split_lo(k, tb[:, k % 3, :], n_hi.bitcast(F32)[:, g, :], n_lo[:, g, :])

                for g in range(HT):
                    t = tb[:, (SPL["sgu", l] + g) % 3, :]
                    dve.scalar_tensor_tensor(tiles(t), tiles(filled(dve, ("mix", l, g))[:, :]),
                                             col("sgu_v_norm", l * HT + g),
                                             sgub[:, 4 * l + g, :].unsqueeze(1).to_broadcast([P, NT, P]),
                                             ALU.mult, ALU.add).then_inc(freed(("mix", l, g)), 1)
                    emptied(dve, ("mix", l, g))
                    emptied(dve, ("u", l, g))
                    dve.tensor_tensor(t, t, u[:, g, :], ALU.mult).then_inc(val_ready, 1)
                    if g >= 1:
                        sgu_lo(g - 1)
                sgu_lo(HT - 1)
                if l == 1:
                    modulation(0, ((gs1, "pre_norm_mix_2", 1), (pg1, "post_norm_mix_2", 2)))
                    link(dve.tensor_tensor(gs1, gs1, col("final_norm", 0, DT), ALU.mult))
                for n in range(ATT_STEPS):
                    if n < 16:
                        i = n % 4
                        w = (i + 1) * P
                        if l * 16 + n >= 2:
                            dve.wait_ge(max_ready, l * 16 + n - 1)
                            dve.wait_ge(probs_ready, l * 16 + n - 1)
                        for m in range(2):
                            c = 2 * (n % 2) + m
                            dve.tensor_tensor_reduce(scores[n % 2][:, m, 0:w], filled(dve, ("S", l, n, m))[:, 0:w],
                                                     causal[:, S - w:S], 1.0, LOWEST, ALU.add, ALU.max,
                                                     mxs[:, c:c + 1]).then_inc(freed(("S", l, n, m)), 1)
                        emptied(dve, ("S", l, n, 0))
                        emptied(dve, ("S", l, n, 1))
                        c = 2 * (n % 2)
                        dve.tensor_scalar(nmx[:, c:c + 2], mxs[:, c:c + 2], -1.0, None, ALU.mult)\
                            .then_inc(max_ready, 1)
                    v = n - 1
                    if 0 <= v < 16:
                        w = (v % 4 + 1) * P
                        c = 2 * (v % 2)
                        uv = l * 16 + v
                        dve.wait_ge(exp_ready, 2 * uv + 2)
                        link(dve.reciprocal(rec[:, c:c + 2], lsum[:, c:c + 2]))
                        dve.tensor_tensor(rec[:, c + 1:c + 2], rec[:, c + 1:c + 2], lamneg[:, l:l + 1], ALU.mult)
                        sc = scores[v % 2]
                        if v >= 2:
                            filled(dve, ("T", l, v - 2))
                        link(dve.tensor_scalar(probs[v % 2][:, 0:w], sc[:, 0, 0:w], rec[:, c:c + 1], None, ALU.mult))
                        dve.scalar_tensor_tensor(probs[v % 2][:, 0:w], sc[:, 1, 0:w], rec[:, c + 1:c + 2],
                                                 probs[v % 2][:, 0:w], ALU.mult, ALU.add).then_inc(probs_ready, 1)
                    if n >= 6 and (n - 6) % 4 == 0:
                        hd = (n - 6) // 4
                        if hd < HEADS:
                            dve.wait_ge(pv_done, l * 16 + 4 * hd + 4)
                            dve.tensor_copy(oT[:, hd, :], ps[6][:, :]).then_inc(freed(("O", l, hd)), 1)
                            emptied(dve, ("O", l, hd))
                emptied(dve, ("norm", ("sub", l)))
                dve.reciprocal(rstd[:, 0:HEADS * NT], rt[:, :]).then_inc(rstd_ready, 1)

                def sub_lo(hd):
                    k = SPL["sub", l] + hd
                    split_lo(k, tb[:, k % 3, :], n_hi.bitcast(F32)[:, HT + hd, :], n_lo[:, HT + hd, :])

                for hd in range(HEADS):
                    k = SPL["sub", l] + hd
                    dve.wait_ge(lo_ready, k - 2)
                    dve.scalar_tensor_tensor(tb[:, k % 3, :], oT[:, hd, :], subg[:, l:l + 1],
                                             filled(dve, ("rstd", ("sub", l, hd)))[:, :],
                                             ALU.mult, ALU.mult).then_inc(val_ready, 1)
                    if hd >= 1:
                        emptied(dve, ("rstd", ("sub", l, hd - 1)))
                        sub_lo(hd - 1)
                    rstd_read(("sub", l, hd))
                sub_lo(HEADS - 1)
                for m in range(DT):
                    dve.tensor_tensor(h[:, m, :], h[:, m, :], filled(dve, ("out", l, m))[:, :], ALU.add)\
                        .then_inc(freed(("out", l, m)), 1)
                    if m:
                        add_square(("ffn", l), m - 1)
                add_square(("ffn", l), DT - 1)
                for m in range(4, DT):
                    emptied(dve, ("out", l, m))
                norm_split(("ffn", l), ("ffn", l), DT, lambda f: h[:, f, :], lambda f: col("ffn_norm", l * DT + f), 0)

                n0 = BK.ffn[l]
                gq = STR["up", l, 1].g0

                def conv_steps(j):
                    dve.tensor_copy(cpar[:, 0:16], par[:, l, bass.ds(j * 16, 16)]).then_inc(par_ready, 1)
                    dve.wait_ge(par_ready, 1 + l * FG + j + 1)
                    for i in range(2):
                        for t in (2 * i, 2 * i + 1):
                            cv = (l * FG + j) * 4 + t + 1
                            dve.wait_ge(conv_begun, cv)
                            dve.scalar_tensor_tensor(rb[t][:, 1:S], ps[t][:, 0:S - 1], cpar[:, 4 * t + 1:4 * t + 2],
                                                     rb[t][:, 1:S], ALU.mult, ALU.add).then_inc(conv_tap, 1)
                            dve.wait_ge(conv_tap, cv)
                            dve.scalar_tensor_tensor(rb[t][:, 2:S], ps[t][:, 0:S - 2], cpar[:, 4 * t:4 * t + 1],
                                                     rb[t][:, 2:S], ALU.mult, ALU.add).then_inc(free[t], 1)
                        dve.wait_ge(free[2 * i + 1], n0[2 * i + 1] + j + 1)
                        dve.wait_ge(silu_done, (l * FG + j) * 2 + i + 1)
                        dve.tensor_tensor(rb[2 * i], rb[2 * i], rb[2 * i + 1], ALU.mult).then_inc(val_ready, 1)

                def down_steps(quarter, after=None):
                    for m in range(DT):
                        dve.wait_ge(quarter_done, quarter + m // 2 + 1)
                        dve.tensor_tensor(h[:, m, :], h[:, m, :], ps[4 + m % 4][:, :], ALU.add)\
                            .then_inc(free[4 + m % 4], 1)
                        if after is not None and m >= 3 and m % 2:
                            for i in range((m - 3) * sums_of(after), (m - 1) * sums_of(after)):
                                add_square(after, i)
                    if after is not None:
                        for i in range((DT - 2) * sums_of(after), DT * sums_of(after)):
                            add_square(after, i)

                def hidden_lo(j):
                    for i in range(2):
                        split_lo(SPL["act", l] + 2 * j + i, rb[2 * i], x_hi.bitcast(F32)[:, i, :], x_lo[:, i, :])

                def ada_step(k):
                    dve.wait_ge(ada_in, 16 * (DT * l + 1) + 16 * k)
                    if isinstance(k, int):
                        dve.wait_ge(c_ready, 1)
                        ins = dve.tensor_scalar(ada_sum, ada_w, csilu[:, k:k + 1], None, ALU.mult)
                    else:
                        dve.wait_ge(ada_used, DT * l + k)
                        ins = dve.scalar_tensor_tensor(ada_sum, ada_w, cpar[:, 16:17], ada_sum, ALU.mult, ALU.add)
                    ins.then_inc(ada_used, 1)

                conv_steps(0)
                hidden_lo(0)
                ada_step(0)
                for first, end in ((1, DT), (DT, FG)):
                    with dve.Fori(first, end) as j:
                        if first == 1:
                            dve.wait_ge(ada_used, DT * l + j)
                            dve.tensor_copy(cpar[:, 16:17], csilu[:, bass.ds(j, 1)])
                        conv_steps(j)
                        down_steps(gq + 4 + 8 * (j - 1))
                        hidden_lo(j)
                        if first == 1:
                            ada_step(j)
                down_steps(gq + 8 * (FG - 1), ("attn", 1) if l == 0 else ("final",))

            for f in range(4, DT):
                dve.wait_ge(*ffn_h(DEPTH - 1, f))
            sums = ps[BK["norm", ("final",)][0]]
            dve.wait_ge(sums_ready, NRM["final",][4] + 1)
            dve.tensor_scalar(ms[:, 0:NT], sums[:, 0:NT], 1.0 / D, EPS, ALU.mult, ALU.add)
            dve.tensor_scalar(ms[:, NT:2 * NT], sums[:, NT:2 * NT], 1.0 / D, None, ALU.mult)\
                .then_inc(freed(("norm", ("final",))), 1)
            emptied(dve, ("norm", ("final",)))
            dve.scalar_tensor_tensor(ms[:, NT:2 * NT], ms[:, 0:NT], EPS, ms[:, NT:2 * NT], ALU.mult, ALU.add)\
                .then_inc(means_ready, 1)
            dve.wait_ge(act_seq, 2)
            dve.reciprocal(rstd[:, 0:2 * NT], rt[:, 0:2 * NT]).then_inc(rstd_ready, 1)
            norm_split(("mix2",), ("mix2",), DT, lambda f: h[:, f, :], lambda f: gs1[:, f:f + 1], 0,
                       lambda f: mod[:, f:f + 1])
            factors = filled(dve, ("rstd", ("final",)))
            for f in range(DT):
                dve.scalar_tensor_tensor(h[:, f, :], h[:, f, :], col("final_norm", f), factors[:, :],
                                         ALU.mult, ALU.mult).then_inc(h_set, 1)
            emptied(dve, ("rstd", ("mix2",)))
            rstd_read(("final",))
            modulation(1, ((gs2, "pre_norm_mlp_2", 4), (pg2, "post_norm_mlp_2", 5)))
            for t in range(HT):
                dve.wait_ge(xr_begun, t + 1)
                b = filled(dve, ("x_rnn", t))
                for back in (1, 2, 3):
                    ins = dve.scalar_tensor_tensor(xc[:, t, back:S], b[:, 0:S - back],
                                                   col("conv_w_2", (3 - back) * HT + t), xc[:, t, back:S],
                                                   ALU.mult, ALU.add)
                    if back < 3:
                        link(ins)
                ins.then_inc(freed(("x_rnn", t)), 1)
            for t in range(HT):
                dve.wait_ge(decay_ready, t + 1)
                link(dve.tensor_scalar(rn[5], rn[3], 1.0, None, ALU.add))
                link(dve.reciprocal(rn[5], rn[5]))
                dve.tensor_tensor(rn[4], rn[3], rn[5], ALU.mult).then_inc(ratio_ready, 1)
                emptied(dve, ("rx", t))
                emptied(dve, ("x_rnn", t))
                link(dve.tensor_tensor(rn[6], rn[1], xc[:, t, :], ALU.mult))
                dve.wait_ge(rootm_ready, t + 1)
                link(dve.tensor_tensor(rn[6], rn[6], rn[4], ALU.mult))
                dve.tensor_tensor_scan(gr[:, t, :], rn[2], rn[6], 0.0, ALU.mult, ALU.add).then_inc(rnn_ready, 1)
            dve.wait_ge(rnn_ready, HT)
            emptied(dve, ("gates",))
            dve.tensor_scalar(gates[:, 0, 0:HEADS2], gates[:, 0, 0:HEADS2], const[:, C_SEEN:C_SEEN + 1], None,
                              ALU.mult).then_inc(gate_set, 1)
            for j in range(2):
                emptied(dve, ("kvs", j))
                v = kk[j].rearrange("p g (c j r) -> p j g c r", j=8, r=2)
                for half in range(2):
                    c = POS_ROW + 16 * j + 8 * half
                    for g in range(2):
                        last = dve.tensor_tensor(
                            cval[j][:, 8 * half:8 * half + 8, g * NCMP:(g + 1) * NCMP],
                            v[:, :, g, half:half + NCMP, 0],
                            cols[:, 1, c:c + 8].unsqueeze(2).to_broadcast([P, 8, NCMP]), ALU.add)
                last.then_inc(val_ready, 1)
                dve.wait_ge(val_ready, SPL["cmp",] + j + 1)
                k = slice(0, 2 * NCMP)
                split_lo(SPL["cmp",] + j, cval[j][:, :, k], cb_hi.bitcast(F32)[:, :, k], cb_lo[:, :, k])
            for t in range(HT):
                emptied(dve, ("g_rnn", t))
                dve.tensor_tensor(gr[:, t, :], gr[:, t, :], rn[4 + t], ALU.mult).then_inc(gr_ready, 1)
            dve.wait_ge(gate_set, 1)
            for n in range(NU + 4):
                if n == 1:
                    for f in range(HT):
                        add_square(("rnn",), f)
                if n == 3:
                    factors = norm_rstd(("rnn",))
                f = n - 4
                k = SPL["rnn",] + f
                if 1 <= f < HT + 1:
                    split_lo(k - 1, tb[:, (k - 1) % 3, :], n_hi.bitcast(F32)[:, f - 1, :], n_lo[:, f - 1, :])
                if 0 <= f < HT:
                    if f == 3:
                        dve.wait_ge(lo_ready, k - 2)
                    dve.scalar_tensor_tensor(tb[:, k % 3, :], gr[:, f, :], col("norm_rnn_out_2", f), factors,
                                             ALU.mult, ALU.mult).then_inc(val_ready, 1)
                if f == HT:
                    rstd_read(("rnn",))
                if n < NU:
                    hd, br, i = UNITS[n]
                    b = filled(dve, ("S2", n))
                    if n >= 4:
                        filled(dve, ("T2", n - 4))
                        dve.wait_ge(max_ready, 32 + n - 3)
                        dve.wait_ge(probs_ready, 32 + n - 3)
                    sc = scores2[n % 4]
                    if br == "c":
                        dve.wait_ge(bias_ready, hd + 1)
                        dve.tensor_tensor(sc[:, 0:124], b[:, 0:124], bias_c[hd % 2], ALU.add)\
                            .then_inc(freed(("S2", n)), 1)
                        emptied(dve, ("S2", n))
                        link(dve.tensor_reduce(cmx, tiles(sc[:, 0:124]), AX.X, ALU.max))
                        dve.tensor_tensor(tiles(sc[:, 0:124]), tiles(sc[:, 0:124]),
                                          cmx.unsqueeze(2).to_broadcast([P, NT, NCMP]), ALU.subtract)\
                            .then_inc(max_ready, 1)
                    else:
                        w = (i + 1) * P
                        dve.tensor_tensor_reduce(sc[:, 0:w], b[:, 0:w], bias_h[hd % 2][:, S - w:S], 1.0, LOWEST,
                                                 ALU.add, ALU.max, mxs[:, n % 4:n % 4 + 1]).then_inc(freed(("S2", n)), 1)
                        emptied(dve, ("S2", n))
                        dve.tensor_scalar(nmx[:, n % 4:n % 4 + 1], mxs[:, n % 4:n % 4 + 1], -1.0, None, ALU.mult)\
                            .then_inc(max_ready, 1)
                v = n - 1
                if 0 <= v < NU:
                    hd, br, i = UNITS[v]
                    sc = scores2[v % 4]
                    dve.wait_ge(exp_ready, 64 + v + 1)
                    if br == "c":
                        link(dve.tensor_reduce(csum, tiles(sc[:, 0:124]), AX.X, ALU.add))
                        link(dve.reciprocal(csum, csum))
                        link(dve.tensor_tensor(csum, csum, gates[:, :, hd], ALU.mult))
                        dve.tensor_tensor(tiles(sc[:, 0:124]), tiles(sc[:, 0:124]),
                                          csum.unsqueeze(2).to_broadcast([P, NT, NCMP]), ALU.mult)\
                            .then_inc(probs_ready, 1)
                    else:
                        g = (8 if br == "s" else 16) + hd
                        w = (i + 1) * P
                        link(dve.reciprocal(rec[:, v % 4:v % 4 + 1], lsum[:, v % 4:v % 4 + 1]))
                        dve.tensor_scalar(sc[:, 0:w], sc[:, 0:w], rec[:, v % 4:v % 4 + 1], gates[:, i, g:g + 1],
                                          ALU.mult, ALU.mult).then_inc(probs_ready, 1)
                v = n - 3
                if 0 <= v < NU and v % 18 == 17:
                    hp = v // 18
                    dve.wait_ge(pv_done, 32 + PV_BEFORE[v + 1])
                    dve.tensor_copy(oT[:, hp, :], ps[5 + hp % 2][:, :]).then_inc(freed(("O2", hp)), 1)
                    emptied(dve, ("O2", hp))
            for f in range(HT):
                add_square(("att",), f)
            norm_split(("att",), ("att",), HT, lambda f: oT[:, f, :], lambda f: col("norm_att_out_2", f), HT)
            for m in range(DT):
                dve.tensor_copy(y[:, m, :], filled(dve, ("out2", m))[:, :]).then_inc(freed(("out2", m)), 1)
                if m:
                    add_square(("post_mix",), m - 1)
            add_square(("post_mix",), DT - 1)
            for m in range(4, DT):
                emptied(dve, ("out2", m))

            def add_normed(e, gain, after=None):
                factors = norm_rstd(e)
                for f in range(DT):
                    if after is not None and f:
                        add_square(after, f - 1)
                    link(dve.scalar_tensor_tensor(y[:, f, :], y[:, f, :], gain[:, f:f + 1], factors,
                                                  ALU.mult, ALU.mult))
                    dve.tensor_tensor(h[:, f, :], h[:, f, :], y[:, f, :], ALU.add).then_inc(h_set, 1)
                rstd_read(e)
                if after is not None:
                    add_square(after, DT - 1)

            add_normed(("post_mix",), pg1, ("mlp",))
            dve.wait_ge(h_set, 2 * DT)
            dve.memset(zy[:, :], 0.0).then_inc(y_zero, 1)
            norm_split(("mlp",), ("mlp",), DT, lambda f: h[:, f, :], lambda f: gs2[:, f:f + 1], 0,
                       lambda f: mod[:, 24 + f:25 + f])
            dve.wait_ge(y_zero, 1)
            n0 = BK.ffn2
            gq = STR["ff1", 1].g0

            def square_steps(j):
                for t in range(4):
                    dve.wait_ge(free[t], n0[t] + j + 1)
                    dve.tensor_tensor(rb[t], rb[t], rb[t], ALU.mult).then_inc(val_ready, 1)

            def ff2_steps(quarter, after=None):
                for m in range(DT):
                    dve.wait_ge(quarter_done, quarter + m // 2 + 1)
                    dve.tensor_tensor(y[:, m, :], y[:, m, :], ps[4 + m % 4][:, :], ALU.add)\
                        .then_inc(free[4 + m % 4], 1)
                    if after is not None and m:
                        add_square(after, m - 1)
                if after is not None:
                    add_square(after, DT - 1)

            def hidden2_lo(j):
                for t in range(4):
                    split_lo(SPL["act2",] + 4 * j + t, rb[t], x_hi.bitcast(F32)[:, t, :], x_lo[:, t, :])

            square_steps(0)
            dve.wait_ge(val_ready, SPL["act2",] + 4)
            hidden2_lo(0)
            with dve.Fori(1, FG2) as j:
                square_steps(j)
                ff2_steps(gq + 4 + 8 * (j - 1))
                hidden2_lo(j)
            ff2_steps(gq + 8 * (FG2 - 1), ("post_mlp",))
            for f in range(4, DT):
                dve.wait_ge(free[4 + f % 4], n0[4 + f % 4] + 2 * FG2)
            add_normed(("post_mlp",), pg2)
            for t in range(NT):
                for j in range(2):
                    dve.tensor_copy(zb[:, t * D + j * S:t * D + (j + 1) * S], filled(dve, ("y", t, j))[:, :])\
                        .then_inc(freed(("y", t, j)), 1)

        @block.tensor
        def _(pe):
            def bank(key):
                b, n = BK[key][:2]
                if n:
                    pe.wait_ge(free[b], n)
                return ps[b]

            def quarter(g):
                pe.wait_ge(whi_ready, g + 1)
                pe.wait_ge(wlo_ready, g + 1)
                return w_hi[:, g % 4, :], w_lo[:, g % 4, :]

            def product(out, l_hi, l_lo, r_hi, r_lo, start, stop):
                pe.matmul(out, l_hi, r_hi, start=start, stop=False)
                pe.matmul(out, l_hi, r_lo, start=False, stop=False)
                return pe.matmul(out, l_lo, r_hi, start=False, stop=stop)

            def norm_sums(e):
                _, sq0, k, adds, _ = NRM[e]
                out = bank(("norm", e))
                pe.wait_ge(sq_ready, sq0 + k)
                if k > sums_of(e):
                    pe.wait_ge(sq_used, adds + k - sums_of(e))
                for c in range(sums_of(e)):
                    for t in range(NT):
                        last = pe.matmul(out[:, c * NT + t:c * NT + t + 1], ss[:, c, t * P:(t + 1) * P], ones[:, 0:1],
                                         start=True, stop=True)
                last.then_inc(sums_ready, 1)

            def spread(e, c0=0, norm=None):
                pe.wait_ge(rstd_ready, NRM[norm or e][0] + 1)
                out = bank(("rstd", e))
                for t in range(NT):
                    last = pe.matmul(out[:, t * P:(t + 1) * P], rstd[:, c0 + t:c0 + t + 1].to_broadcast([P, P]),
                                     ident, start=True, stop=True)
                last.then_inc(full[BK["rstd", e][0]], 1)

            def norm_sum(e):
                norm_sums(e)
                spread(e)

            def modulation_sums(l, tiles_):
                if tiles_[0] == 0:
                    pe.wait_ge(ada_used, DT * (l + 1))
                    bank(("ada", l))
                b = BK["ada", l][0]
                for t in tiles_:
                    last = pe.matmul(ps[b][:, t:t + 1], ada_sum[:, t * P:(t + 1) * P], ones[:, 0:1], start=True,
                                     stop=True)
                if tiles_[-1] == ADA_T // 2 - 1:
                    last.then_inc(full[b], 1)

            def features(keys, g0, split=None, beside=None):
                first = 0
                if split is not None:
                    first = 2
                    parts = [quarter(g0), quarter(g0 + 1)]
                    outs = [bank(keys[0]), bank(keys[1])]
                    for k in range(DT):
                        pe.wait_ge(lo_ready, split + k + 1)
                        for t in range(2):
                            wh, wl = parts[t]
                            last = product(outs[t][:, :], wh[:, k * P:(k + 1) * P], wl[:, k * P:(k + 1) * P],
                                           n_hi[:, k, :], n_lo[:, k, :], k == 0, k == DT - 1)
                            if k == DT - 1:
                                last.then_inc(quarter_done, 1)
                        if beside is not None:
                            beside(k)
                for t in range(first, len(keys)):
                    wh, wl = quarter(g0 + t)
                    out = bank(keys[t])
                    for k in range(DT):
                        last = product(out[:, :], wh[:, k * P:(k + 1) * P], wl[:, k * P:(k + 1) * P],
                                       n_hi[:, k, :], n_lo[:, k, :], k == 0, k == DT - 1)
                    last.then_inc(quarter_done, 1)

            def tokens(keys, g0):
                outs = [bank(key) for key in keys]
                for q in range(4):
                    wh, wl = quarter(g0 + q)
                    for t in range(NT):
                        for k in (2 * q, 2 * q + 1):
                            c = (k % 2) * S
                            last = product(outs[t][:, :], n_hi[:, k, t * P:(t + 1) * P], n_lo[:, k, t * P:(t + 1) * P],
                                           wh[:, c:c + S], wl[:, c:c + S], k == 0, k == DT - 1)
                    last.then_inc(quarter_done, 1)

            def tokens_narrow(key, g, width):
                wh, wl = quarter(g)
                out = bank(key)
                for t in range(NT):
                    for k in range(DT):
                        last = product(out[:, t * width:(t + 1) * width], n_hi[:, k, t * P:(t + 1) * P],
                                       n_lo[:, k, t * P:(t + 1) * P], wh[:, k * width:(k + 1) * width],
                                       wl[:, k * width:(k + 1) * width], k == 0, k == DT - 1)
                last.then_inc(quarter_done, 1)

            pe.wait_ge(consts_in, 16)
            pe.wait_ge(x_in, 16)
            for f in range(DT):
                out = bank(("x", f))
                for t in range(NT):
                    last = pe.transpose(out[:, t * P:(t + 1) * P], xin[:, t, f * P:(f + 1) * P], ident)
                last.then_inc(full[f], 1)
            pe.wait_ge(gains_in, 16 * len(ROWS0))
            pe.transpose(bank("cols0")[:, 0:NROWS0], rows[0][0:NROWS0, :], ident[0:NROWS0, 0:NROWS0])\
                .then_inc(full[BK["cols0"][0]], 1)
            pe.wait_ge(ones_set, 3)

            def turn_parameters():
                pe.wait_ge(rows_in, 16 * (4 + 4 * DEPTH))
                for i in range(1, 6):
                    key = "cols1" if i < 5 else "cols2"
                    if i in (1, 5):
                        bank(key)
                    b = BK[key][0]
                    c = (i - 1) % 4 * P
                    last = pe.transpose(ps[b][:, c:c + NROWS[i]], rows[i][0:NROWS[i], :],
                                        ident[0:NROWS[i], 0:NROWS[i]])
                    if i in (4, 5):
                        last.then_inc(full[b], 1)
                pe.wait_ge(sgu_masked, 1)
                for l in range(DEPTH):
                    out = bank(("wsT", l))
                    for g in range(4):
                        last = pe.transpose(out[:, g * P:(g + 1) * P], sguw[:, 4 * l + g, :], ident)
                    last.then_inc(full[BK["wsT", l][0]], 1)

            norm_sum(("attn", 0))
            for l in range(DEPTH):
                features([("u", l, t) for t in range(4)], STR["u", l].g0, SPL["attn", l])
                tokens([("vs", l, t) for t in range(NT)], STR["vs", l].g0)
                if l == 0:
                    turn_parameters()
                for j, name in enumerate(("q", "k")):
                    features([(name, l, t) for t in range(4)], STR[name, l].g0)
                    if j == 1:
                        tokens([("va", l, t) for t in range(NT)], STR["va", l].g0)
                    for t in range(4):
                        emptied(pe, (name, l, t))
                        out = bank(("rope", name, l, t))
                        pe.matmul(out[:, :], rotT, (qT, kT)[j][:, t, :], start=True, stop=True)\
                            .then_inc(full[BK["rope", name, l, t][0]], 1)
                pe.wait_ge(vn_ready, l + 1)
                for g in range(HT):
                    out = bank(("mix", l, g))
                    for c in range(NT):
                        last = pe.matmul(out[:, c * P:(c + 1) * P], vg[:, c, g * P:(g + 1) * P], wsT[:, 4 * l + g, :],
                                         start=True, stop=True)
                    last.then_inc(full[BK["mix", l, g][0]], 1)
                if l == 1:
                    modulation_sums(0, range(ADA_T // 2))
                pe.wait_ge(qk_ready, l * 8 + 8)
                for t in range(NT):
                    emptied(pe, ("va", l, t))
                for n in range(ATT_STEPS):
                    if n < 16:
                        hd, i = n // 4, n % 4
                        for m in range(2):
                            out = bank(("S", l, n, m))
                            r = slice(64 * m, 64 * m + 64)
                            pe.matmul(out[:, 0:(i + 1) * P], qT[r, hd, i * P:(i + 1) * P], kT[r, hd, 0:(i + 1) * P],
                                      start=True, stop=True).then_inc(full[BK["S", l, n, m][0]], 1)
                    v = n - 2
                    if 0 <= v < 16:
                        pe.wait_ge(probs_ready, l * 16 + v + 1)
                        out = bank(("T", l, v))
                        for kt in range(v % 4 + 1):
                            last = pe.transpose(out[:, kt * P:(kt + 1) * P], probs[v % 2][:, kt * P:(kt + 1) * P], ident)
                        last.then_inc(full[BK["T", l, v][0]], 1)
                    v = n - 3
                    if 0 <= v < 16:
                        hd, i = v // 4, v % 4
                        if i == 0:
                            bank(("O", l, hd))
                        emptied(pe, ("T", l, v))
                        for kt in range(i + 1):
                            last = pe.matmul(ps[6][:, i * P:(i + 1) * P], va[:, kt, hd * P:(hd + 1) * P],
                                             pT[v % 2][:, kt * P:(kt + 1) * P], start=(kt == 0), stop=(kt == i))
                        last.then_inc(pv_done, 1)
                    if n >= 7 and (n - 7) % 4 == 0:
                        hd = (n - 7) // 4
                        out = bank(("norm", ("sub", l))) if hd == 0 else ps[7]
                        pe.wait_ge(sq_ready, NRM["sub", l][1] + hd + 1)
                        for t in range(NT):
                            last = pe.matmul(out[:, hd * NT + t:hd * NT + t + 1], ss[:, hd % 2, t * P:(t + 1) * P],
                                             ones[:, 0:1], start=True, stop=True)
                        last.then_inc(sums_ready, 1)

                def spread_heads(k):
                    if k == HT - 1:
                        for hd in range(HEADS):
                            spread(("sub", l, hd), hd * NT, ("sub", l))

                features([("out", l, m) for m in range(DT)], STR["out", l, 0].g0, SPL["sgu", l], spread_heads)
                norm_sum(("ffn", l))
                n0 = BK.ffn[l]

                def up(g, j, split=None):
                    turn = 0 if isinstance(j, int) else 8 * (j - 1)

                    def ready(t):
                        pe.wait_ge(whi_ready, g + t + 1 + turn)
                        pe.wait_ge(wlo_ready, g + t + 1 + turn)
                        pe.wait_ge(free[t], n0[t] + j)

                    def one(t, k):
                        wh, wl = w_hi[:, (g + t) % 4, :], w_lo[:, (g + t) % 4, :]
                        last = product(ps[t][:, :], wh[:, k * P:(k + 1) * P], wl[:, k * P:(k + 1) * P],
                                       n_hi[:, k, :], n_lo[:, k, :], k == 0, k == DT - 1)
                        if k == DT - 1:
                            last.then_inc(quarter_done, 1)

                    if split is not None:
                        ready(0)
                        ready(1)
                        for k in range(DT):
                            pe.wait_ge(lo_ready, split + k + 1)
                            one(0, k)
                            one(1, k)
                    for t in range(0 if split is None else 2, 4):
                        ready(t)
                        for k in range(DT):
                            one(t, k)

                def down(g, j, turn, kn, split):
                    pe.wait_ge(lo_ready, split + kn * j + kn)
                    for q in range(4):
                        pe.wait_ge(whi_ready, g + q + 1 + turn)
                        pe.wait_ge(wlo_ready, g + q + 1 + turn)
                        wh, wl = w_hi[:, (g + q) % 4, :], w_lo[:, (g + q) % 4, :]
                        for m in (2 * q, 2 * q + 1):
                            pe.wait_ge(free[4 + m % 4], n0[4 + m % 4] + 2 * j + m // 4)
                            for k in range(kn):
                                c = k * 256 + (m % 2) * P
                                last = product(ps[4 + m % 4][:, :], wh[:, c:c + P], wl[:, c:c + P],
                                               x_hi[:, k, :], x_lo[:, k, :], k == 0, k == kn - 1)
                        last.then_inc(quarter_done, 1)

                gq = STR["up", l, 1].g0
                up(STR["up", l, 0].g0, 0, SPL["ffn", l])
                with pe.Fori(1, FG) as j:
                    up(gq, j)
                    down(gq + 4, j - 1, 8 * (j - 1), 2, SPL["act", l])
                down(gq + 8 * (FG - 1), FG - 1, 0, 2, SPL["act", l])
                if l == 0:
                    norm_sum(("attn", 1))

            norm_sums(("final",))
            spread(("mix2",), NT, ("final",))
            spread(("final",))
            def recurrence_gates(t):
                if t == 0:
                    pe.wait_ge(blk_in, 16 * 4)
                emptied(pe, ("x_rnn", t))
                for j, key in enumerate((("ra", t), ("rx", t))):
                    out = bank(key)
                    pe.matmul(out[:, :], blkw[:, j, t, :], xc[:, t, :], start=True, stop=True)\
                        .then_inc(full[BK[key][0]], 1)

            features([("x_rnn", t) for t in range(4)], STR["x_rnn",].g0, SPL["mix2",],
                     lambda k: modulation_sums(1, range(3 * k, 3 * k + 3)))
            features([("kvs", t) for t in range(2)], STR["kvs",].g0)
            recurrence_gates(0)
            features([("kvs", 2)], STR["kvs",].g0 + 2)
            tokens_narrow(("vsel",), STR["kvs",].g0 + 3, P)
            recurrence_gates(1)
            features([("kw",)], STR["kw",].g0)
            tokens_narrow(("vwin",), STR["kw",].g0 + 1, P)
            tokens_narrow(("gates",), STR["kw",].g0 + 2, 24)
            recurrence_gates(2)
            features([("q2", t) for t in range(2)], STR["q2",].g0)
            recurrence_gates(3)
            features([("q2", t) for t in range(2, 4)], STR["q2",].g0 + 2)
            features([("g_rnn", t) for t in range(4)], STR["g_rnn",].g0)
            pe.wait_ge(cw2_in, 16 * 4)
            for j in range(2):
                pe.wait_ge(lo_ready, SPL["cmp",] + j + 1)
                out = bank(("chid", j))
                g0 = STR["cmp", j].g0
                for q in range(4):
                    wh, wl = quarter(g0 + q)
                    for i in range(4):
                        k = 4 * q + i
                        c = slice(i * 256, (i + 1) * 256)
                        last = product(out[0:2 * NCMP, 0:256], cb_hi[:, k, 0:2 * NCMP], cb_lo[:, k, 0:2 * NCMP],
                                       wh[:, c], wl[:, c], k == 0, k == 15)
                    last.then_inc(quarter_done, 1)
                emptied(pe, ("chid", j))
                out = bank(("cturn", j))
                for m in range(2):
                    last = pe.transpose(out[:, m * 2 * NCMP:(m + 1) * 2 * NCMP],
                                        hidden[0:2 * NCMP, m * P:(m + 1) * P], ident[0:2 * NCMP, 0:2 * NCMP])
                last.then_inc(full[BK["cturn", j][0]], 1)
                emptied(pe, ("cturn", j))
                out = bank(("cout", j))
                for g in range(1 if j == 0 else 2):
                    for m in range(2):
                        if j == 0:
                            last = pe.matmul(out[:, 0:62], cw2[0][:, m, :], ghid[:, m, 0:62],
                                             start=(m == 0), stop=(m == 1))
                        else:
                            last = pe.matmul(out[0:NCMP, 64 * g:64 * g + 64], ghid[:, m, g * NCMP:(g + 1) * NCMP],
                                             cw2[1][:, m, 0:64], start=(m == 0), stop=(m == 1))
                last.then_inc(full[BK["cout", j][0]], 1)
            for key in (("kvs", 2), ("vsel",), ("kw",), ("vwin",), ("cout", 0), ("cout", 1)) \
                    + tuple(("q2", t) for t in range(4)):
                emptied(pe, key)
            for n in range(NU + 4):
                if n < NU:
                    hd, br, i = UNITS[n]
                    r = slice(64 * (hd % 2), 64 * (hd % 2) + 64)
                    out = bank(("S2", n))
                    if br == "c":
                        for t in range(NT):
                            last = pe.matmul(out[:, t * NCMP:(t + 1) * NCMP], q2[r, hd // 2, t * P:(t + 1) * P],
                                             kcmp[r, (hd // 4) * NCMP:(hd // 4 + 1) * NCMP], start=True, stop=True)
                    else:
                        last = pe.matmul(out[:, 0:(i + 1) * P], q2[r, hd // 2, i * P:(i + 1) * P],
                                         kd[0 if br == "s" else 1][r, hd // 4, 0:(i + 1) * P], start=True, stop=True)
                    last.then_inc(full[BK["S2", n][0]], 1)
                if n == 1:
                    norm_sums(("rnn",))
                if n == 3:
                    spread(("rnn",))
                v = n - 2
                if 0 <= v < NU:
                    hd, br, i = UNITS[v]
                    pe.wait_ge(probs_ready, 32 + v + 1)
                    out = bank(("T2", v))
                    if br == "c":
                        for t in range(NT):
                            last = pe.transpose(out[0:NCMP, t * P:(t + 1) * P],
                                                scores2[v % 4][:, t * NCMP:(t + 1) * NCMP], ident)
                    else:
                        for kt in range(i + 1):
                            last = pe.transpose(out[:, kt * P:(kt + 1) * P], scores2[v % 4][:, kt * P:(kt + 1) * P],
                                                ident)
                    last.then_inc(full[BK["T2", v][0]], 1)
                v = n - 3
                if 0 <= v < NU and UNITS[v][1] != "c":
                    hd, br, i = UNITS[v]
                    g, r0, hp = hd // 4, 64 * (hd % 2), hd // 2
                    if v % 18 == 1:
                        bank(("O2", hp))
                    out = ps[5 + hp % 2][r0:r0 + 64, i * P:(i + 1) * P]
                    if br == "s":
                        if i == 0:
                            emptied(pe, ("T2", v - 1))
                        pe.matmul(out, vcmp[0:NCMP, 64 * g:64 * g + 64], pTc[0:NCMP, i * P:(i + 1) * P],
                                  start=True, stop=False)
                    emptied(pe, ("T2", v))
                    for kt in range(i + 1):
                        last = pe.matmul(out, v2[0 if br == "s" else 1][:, kt, 64 * g:64 * g + 64],
                                         pT[PV_BEFORE[v] % 2][:, kt * P:(kt + 1) * P],
                                         start=False, stop=(br == "w" and kt == i))
                    last.then_inc(pv_done, 1)
            norm_sum(("att",))
            pe.wait_ge(lo_ready, SPL["att",] + HT)
            features([("out2", m) for m in range(DT)], STR["out2", 0].g0)
            norm_sum(("post_mix",))
            norm_sum(("mlp",))
            n0 = BK.ffn2
            gq = STR["ff1", 1].g0
            up(STR["ff1", 0].g0, 0, SPL["mlp",])
            with pe.Fori(1, FG2) as j:
                up(gq, j)
                down(gq + 4, j - 1, 8 * (j - 1), 4, SPL["act2",])
            down(gq + 8 * (FG2 - 1), FG2 - 1, 0, 4, SPL["act2",])
            norm_sum(("post_mlp",))
            pe.wait_ge(h_set, 3 * DT)
            for t in range(NT):
                for j in range(2):
                    out = bank(("y", t, j))
                    for f in range(4):
                        last = pe.transpose(out[:, f * P:(f + 1) * P], h[:, 4 * j + f, t * P:(t + 1) * P], ident)
                    last.then_inc(full[BK["y", t, j][0]], 1)


_INS = ["x", "positions", "attn_norm", "w_in", "sgu_v_norm", "sgu_w_spatial", "sgu_b_spatial", "lambda_q1",
        "lambda_k1", "lambda_q2", "lambda_k2", "subln_gain", "w_out", "ffn_norm", "w_up", "conv_w", "conv_b",
        "w_down", "final_norm", "c_2", "ada_w_2", "ada_b_2", "pre_norm_mix_2", "w_in_2", "conv_w_2", "conv_b_2",
        "lru_wa_2", "lru_ba_2", "lru_wx_2", "lru_bx_2", "lru_lambda_2", "cmp_pos_k_2", "cmp_w1_k_2", "cmp_w2_k_2",
        "cmp_pos_v_2", "cmp_w1_v_2", "cmp_w2_v_2", "norm_rnn_out_2", "norm_att_out_2", "w_out_2",
        "post_norm_mix_2", "pre_norm_mlp_2", "w_ff1_2", "w_ff2_2", "post_norm_mlp_2"]


def kernel(**inputs):
    import concourse.bacc as bacc
    from concourse.bass_utils import run_bass_kernel_spmd

    nc = bacc.Bacc("TRN2", target_bir_lowering=False, num_devices=1, dynamic_dma_scratch_size=1024)
    arrays, args = {"in_consts": constants()}, {}
    for name in _INS:
        arrays["in_" + name] = np.ascontiguousarray(inputs[name])
    for name, v in arrays.items():
        args[name[3:]] = nc.dram_tensor(name, v.shape, mybir.dt.from_np(v.dtype), kind="ExternalInput").ap()
    args["out"] = nc.dram_tensor("out_y", (1, S, D), F32, kind="ExternalOutput").ap()
    build(nc, args)
    r = run_bass_kernel_spmd(nc, [arrays], core_ids=[0])
    return r.results[0]["out_y"]
```
